# Optimizing a Trainium2 kernel written in Bass

```python
import math
import jax, jax.numpy as jnp
from jax import lax
import numpy as np
import jax
import jax.numpy as jnp

D_MODEL = 1024
BATCH = 1
SEQ = 256
DEPTH = 2

LRU_WIDTH = D_MODEL // 2
LRU_HEADS = 8
LRU_HEAD_DIM = LRU_WIDTH // LRU_HEADS
CONV_WIDTH = 4
LRU_C = 8.0
RWKV_WIDTH = D_MODEL // 2
RWKV_HEAD_DIM = 64
RWKV_HEADS = RWKV_WIDTH // RWKV_HEAD_DIM
DECAY_LORA = 64
AAA_LORA = 64
GATE_LORA = 128
RWKV_IN = 3 * RWKV_WIDTH + DECAY_LORA + AAA_LORA + GATE_LORA
EVEN_IN = 2 * LRU_WIDTH + RWKV_IN
GN_EPS = 64e-5
DIFF_HEAD_DIM = 64
DIFF_HEADS = D_MODEL // (2 * DIFF_HEAD_DIM)
DIFF_V_DIM = 2 * DIFF_HEAD_DIM
QKV_DIM = 2 * DIFF_HEADS * 2 * DIFF_HEAD_DIM + DIFF_HEADS * DIFF_V_DIM
ROPE_DIM = DIFF_HEAD_DIM // 4
ROPE_THETA = 500000.0
Q_BLOCK = 128
FFN_DIM = 2816
N_EXPERTS = 8
TOP_K = 2
EXPERT_DIM = 3584
RMS_EPS = 1e-6


F32 = jnp.float32

def rms_norm(x, g, eps=RMS_EPS):
    xf = x.astype(F32)
    y = xf * lax.rsqrt(jnp.mean(jnp.square(xf), axis=-1, keepdims=True) + eps)
    return (y * g.astype(F32)).astype(x.dtype)

def token_shift(x):
    return jnp.pad(x, ((0, 0), (1, 0), (0, 0)))[:, :-1]

def swiglu(x, wg, wu, wd):
    return (jax.nn.silu(x @ wg) * (x @ wu)) @ wd

def causal_dwconv(x, w, b):
    y = lax.conv_general_dilated(x, w[:, None, :].astype(x.dtype), window_strides=(1,),
                                 padding=[(CONV_WIDTH - 1, 0)],
                                 dimension_numbers=('NWC', 'WIO', 'NWC'),
                                 feature_group_count=x.shape[-1])
    return y + b

def rg_lru(x, wa, ba, wx, bx, lam):
    B, T, _ = x.shape
    xf = x.astype(F32)
    xh = xf.reshape(B, T, LRU_HEADS, LRU_HEAD_DIM)
    gate_a = jnp.einsum('bthi,hij->bthj', xh, wa.astype(F32)).reshape(B, T, LRU_WIDTH) + ba
    gate_x = jnp.einsum('bthi,hij->bthj', xh, wx.astype(F32)).reshape(B, T, LRU_WIDTH) + bx
    log_a = -LRU_C * jax.nn.sigmoid(gate_a) * jax.nn.softplus(-lam.astype(F32))
    a = jnp.exp(log_a)
    u = jnp.sqrt(-jnp.expm1(2.0 * log_a)) * jax.nn.sigmoid(gate_x) * xf

    def combine(l, r):
        return (l[0] * r[0], r[0] * l[1] + r[1])

    _, h = lax.associative_scan(combine, (a, u), axis=1)
    return h.astype(x.dtype)

def rwkv7_scan(r, w, k, v, kk, a):
    B, T, H, N = r.shape

    def step(S, inp):
        r_t, w_t, k_t, v_t, kk_t, a_t = inp
        sa = jnp.einsum('bhvk,bhk->bhv', S, -kk_t)
        S = S * w_t[:, :, None, :] + sa[..., None] * (kk_t * a_t)[:, :, None, :] \
            + v_t[..., None] * k_t[:, :, None, :]
        o = jnp.einsum('bhvk,bhk->bhv', S, r_t)
        return S, o

    xs = tuple(jnp.moveaxis(t, 1, 0) for t in (r, w, k, v, kk, a))
    S0 = jnp.zeros((B, H, N, N), F32)
    _, o = lax.scan(step, S0, xs)
    return jnp.moveaxis(o, 0, 1)

def rwkv7_mixer(p, mu, w0, w2, a0, a2, g2, k_k, k_a, r_k, gn_w, gn_b):
    B, T, _ = p.shape
    pf = p.astype(F32)
    ps = pf + (token_shift(pf) - pf) * mu
    idx = np.cumsum([RWKV_WIDTH, RWKV_WIDTH, RWKV_WIDTH, DECAY_LORA, AAA_LORA]).tolist()
    r, k, v, xw, xa, xg = jnp.split(ps, idx, axis=-1)
    wlog = -jax.nn.softplus(-(w0 + jnp.tanh(xw) @ w2)) - 0.5
    decay = jnp.exp(-jnp.exp(wlog))
    a = jax.nn.sigmoid(a0 + xa @ a2)
    g = jax.nn.sigmoid(xg) @ g2

    def hs(t):
        return t.reshape(B, T, RWKV_HEADS, RWKV_HEAD_DIM)

    kk = hs(k * k_k)
    kk = kk / jnp.maximum(jnp.linalg.norm(kk, axis=-1, keepdims=True), 1e-12)
    k = k * (1.0 + (a - 1.0) * k_a)
    rh, kh, vh = hs(r), hs(k), hs(v)
    o = rwkv7_scan(rh, hs(decay), kh, vh, kk, hs(a))
    mean = jnp.mean(o, axis=-1, keepdims=True)
    var = jnp.mean(jnp.square(o - mean), axis=-1, keepdims=True)
    on = ((o - mean) * lax.rsqrt(var + GN_EPS)).reshape(B, T, RWKV_WIDTH) * gn_w + gn_b
    bonus = (jnp.sum(rh * kh * r_k, axis=-1, keepdims=True) * vh).reshape(B, T, RWKV_WIDTH)
    return (on + bonus) * g

def even_mixer(xn, w_in, conv_w, conv_b, gate_a_w, gate_a_b, gate_x_w, gate_x_b, lru_lambda,
               shift_mu, w0, w2, a0, a2, g2, k_k, k_a, r_k, gn_w, gn_b, w_out):
    proj = xn @ w_in
    lru_x, lru_g, rw = jnp.split(proj, [LRU_WIDTH, 2 * LRU_WIDTH], axis=-1)
    h = rg_lru(causal_dwconv(lru_x, conv_w, conv_b), gate_a_w, gate_a_b, gate_x_w, gate_x_b, lru_lambda)
    y_lru = jax.nn.gelu(lru_g) * h
    y_rwkv = rwkv7_mixer(rw, shift_mu, w0, w2, a0, a2, g2, k_k, k_a, r_k, gn_w, gn_b)
    y = jnp.concatenate([y_lru, y_rwkv.astype(y_lru.dtype)], axis=-1)
    return y @ w_out

def partial_rope(x, positions):
    half = ROPE_DIM // 2
    inv_freq = ROPE_THETA ** (-jnp.arange(0, ROPE_DIM, 2, dtype=F32) / ROPE_DIM)
    ang = positions.astype(F32)[:, :, None] * inv_freq
    cos = jnp.cos(ang)[:, :, None, None, :]
    sin = jnp.sin(ang)[:, :, None, None, :]
    xf = x.astype(F32)
    x1 = xf[..., :half]
    x2 = xf[..., half:ROPE_DIM]
    out = jnp.concatenate([x1 * cos - x2 * sin, x2 * cos + x1 * sin, xf[..., ROPE_DIM:]], axis=-1)
    return out.astype(x.dtype)

def diff_attention(xn, positions, w_qkv, q_norm, k_norm, lq1, lk1, lq2, lk2, subln, w_o, lambda_init):
    B, T, _ = xn.shape
    qkv = xn @ w_qkv
    qd = DIFF_HEADS * 2 * DIFF_HEAD_DIM
    q, k, v = jnp.split(qkv, [qd, 2 * qd], axis=-1)
    q = q.reshape(B, T, DIFF_HEADS, 2, DIFF_HEAD_DIM)
    k = k.reshape(B, T, DIFF_HEADS, 2, DIFF_HEAD_DIM)
    v = v.reshape(B, T, DIFF_HEADS, DIFF_V_DIM).astype(F32)
    q = partial_rope(rms_norm(q, q_norm), positions)
    k = partial_rope(rms_norm(k, k_norm), positions)
    lam = jnp.exp(jnp.sum(lq1.astype(F32) * lk1.astype(F32))) \
        - jnp.exp(jnp.sum(lq2.astype(F32) * lk2.astype(F32))) + lambda_init
    n_blk = T // Q_BLOCK
    qb = jnp.moveaxis(q.reshape(B, n_blk, Q_BLOCK, DIFF_HEADS, 2, DIFF_HEAD_DIM), 1, 0)
    kpos = jnp.arange(T)
    scale = DIFF_HEAD_DIM ** -0.5

    def block(args):
        q_blk, bi = args
        s = jnp.einsum('bqhcd,bkhcd->bhcqk', q_blk, k, preferred_element_type=F32) * scale
        qpos = bi * Q_BLOCK + jnp.arange(Q_BLOCK)
        s = jnp.where(kpos[None, :] <= qpos[:, None], s, -jnp.inf)
        p = jax.nn.softmax(s, axis=-1)
        attn = p[:, :, 0] - lam * p[:, :, 1]
        return jnp.einsum('bhqk,bkhe->bqhe', attn, v)

    o = lax.map(block, (qb, jnp.arange(n_blk)))
    o = jnp.moveaxis(o, 0, 1).reshape(B, T, DIFF_HEADS, DIFF_V_DIM)
    o = rms_norm(o, subln) * (1.0 - lambda_init)
    return o.reshape(B, T, DIFF_HEADS * DIFF_V_DIM).astype(xn.dtype) @ w_o

def moe_swiglu(xn, router, wg, wu, wd):
    B, T, D = xn.shape
    xt = xn.reshape(B * T, D)
    logits = (xt @ router).astype(F32)
    topv, topi = lax.top_k(logits, TOP_K)
    gates = jax.nn.softmax(topv, axis=-1)
    combine = jnp.sum(jax.nn.one_hot(topi, N_EXPERTS, dtype=F32) * gates[..., None], axis=1)
    y = jnp.zeros((B * T, D), F32)
    for e in range(N_EXPERTS):
        y = y + combine[:, e:e + 1] * swiglu(xt, wg[e], wu[e], wd[e]).astype(F32)
    return y.reshape(B, T, D).astype(xn.dtype)

def first_inputs(seed: int = 0) -> dict:
    key = jax.random.key(seed)
    keys = jax.random.split(key, 64)
    counter = [0]

    def nk():
        kk = keys[counter[0]]
        counter[0] += 1
        return kk

    def nrm(shape, scale):
        return jax.random.normal(nk(), shape, F32) * scale

    def gain(shape):
        return 1.0 + nrm(shape, 0.02)

    ne = (DEPTH + 1) // 2
    no = DEPTH // 2
    D = D_MODEL
    x = jax.random.normal(nk(), (BATCH, SEQ, D), F32)
    positions = jnp.broadcast_to(jnp.arange(SEQ, dtype=jnp.int32), (BATCH, SEQ))
    u = jax.random.uniform(nk(), (ne, LRU_WIDTH), F32, 0.9, 0.999)
    s = u ** (1.0 / LRU_C)
    return {
        'x': x,
        'positions': positions,
        'e_ln_mix': gain((ne, D)),
        'e_w_in': nrm((ne, D, EVEN_IN), D ** -0.5),
        'e_conv_w': nrm((ne, CONV_WIDTH, LRU_WIDTH), CONV_WIDTH ** -0.5),
        'e_conv_b': nrm((ne, LRU_WIDTH), 0.01),
        'e_gate_a_w': nrm((ne, LRU_HEADS, LRU_HEAD_DIM, LRU_HEAD_DIM), LRU_HEAD_DIM ** -0.5),
        'e_gate_a_b': nrm((ne, LRU_WIDTH), 0.01),
        'e_gate_x_w': nrm((ne, LRU_HEADS, LRU_HEAD_DIM, LRU_HEAD_DIM), LRU_HEAD_DIM ** -0.5),
        'e_gate_x_b': nrm((ne, LRU_WIDTH), 0.01),
        'e_lru_lambda': jnp.log(s) - jnp.log1p(-s),
        'e_shift_mu': jax.random.uniform(nk(), (ne, RWKV_IN), F32),
        'e_w0': jax.random.uniform(nk(), (ne, RWKV_WIDTH), F32, -6.0, 1.0),
        'e_w2': nrm((ne, DECAY_LORA, RWKV_WIDTH), 0.1),
        'e_a0': nrm((ne, RWKV_WIDTH), 0.1),
        'e_a2': nrm((ne, AAA_LORA, RWKV_WIDTH), 0.1),
        'e_g2': nrm((ne, GATE_LORA, RWKV_WIDTH), GATE_LORA ** -0.5),
        'e_k_k': 0.85 + nrm((ne, RWKV_WIDTH), 0.02),
        'e_k_a': gain((ne, RWKV_WIDTH)),
        'e_r_k': nrm((ne, RWKV_HEADS, RWKV_HEAD_DIM), 0.1),
        'e_gn_w': gain((ne, RWKV_WIDTH)),
        'e_gn_b': nrm((ne, RWKV_WIDTH), 0.01),
        'e_w_out': nrm((ne, D, D), D ** -0.5),
        'e_ln_ffn': gain((ne, D)),
        'e_ffn_gate': nrm((ne, D, FFN_DIM), D ** -0.5),
        'e_ffn_up': nrm((ne, D, FFN_DIM), D ** -0.5),
        'e_ffn_down': nrm((ne, FFN_DIM, D), FFN_DIM ** -0.5),
        'o_ln_mix': gain((no, D)),
        'o_w_qkv': nrm((no, D, QKV_DIM), D ** -0.5),
        'o_q_norm': gain((no, DIFF_HEAD_DIM)),
        'o_k_norm': gain((no, DIFF_HEAD_DIM)),
        'o_lambda_q1': nrm((no, DIFF_HEAD_DIM), 0.1),
        'o_lambda_k1': nrm((no, DIFF_HEAD_DIM), 0.1),
        'o_lambda_q2': nrm((no, DIFF_HEAD_DIM), 0.1),
        'o_lambda_k2': nrm((no, DIFF_HEAD_DIM), 0.1),
        'o_subln': gain((no, DIFF_V_DIM)),
        'o_w_o': nrm((no, DIFF_HEADS * DIFF_V_DIM, D), D ** -0.5),
        'o_ln_ffn': gain((no, D)),
        'o_router': nrm((no, D, N_EXPERTS), D ** -0.5),
        'o_moe_gate': nrm((no, N_EXPERTS, D, EXPERT_DIM), D ** -0.5),
        'o_moe_up': nrm((no, N_EXPERTS, D, EXPERT_DIM), D ** -0.5),
        'o_moe_down': nrm((no, N_EXPERTS, EXPERT_DIM, D), EXPERT_DIM ** -0.5),
    }

def first_block(x, positions, e_ln_mix, e_w_in, e_conv_w, e_conv_b, e_gate_a_w, e_gate_a_b,
              e_gate_x_w, e_gate_x_b, e_lru_lambda, e_shift_mu, e_w0, e_w2, e_a0, e_a2, e_g2,
              e_k_k, e_k_a, e_r_k, e_gn_w, e_gn_b, e_w_out, e_ln_ffn, e_ffn_gate, e_ffn_up,
              e_ffn_down, o_ln_mix, o_w_qkv, o_q_norm, o_k_norm, o_lambda_q1, o_lambda_k1,
              o_lambda_q2, o_lambda_k2, o_subln, o_w_o, o_ln_ffn, o_router, o_moe_gate,
              o_moe_up, o_moe_down):
    for i in range(DEPTH):
        j = i // 2
        if i % 2 == 0:
            h = rms_norm(x, e_ln_mix[j])
            x = x + even_mixer(h, e_w_in[j], e_conv_w[j], e_conv_b[j], e_gate_a_w[j], e_gate_a_b[j],
                               e_gate_x_w[j], e_gate_x_b[j], e_lru_lambda[j], e_shift_mu[j], e_w0[j],
                               e_w2[j], e_a0[j], e_a2[j], e_g2[j], e_k_k[j], e_k_a[j], e_r_k[j],
                               e_gn_w[j], e_gn_b[j], e_w_out[j])
            h = rms_norm(x, e_ln_ffn[j])
            x = x + swiglu(h, e_ffn_gate[j], e_ffn_up[j], e_ffn_down[j])
        else:
            lambda_init = 0.8 - 0.6 * math.exp(-0.3 * i)
            h = rms_norm(x, o_ln_mix[j])
            x = x + diff_attention(h, positions, o_w_qkv[j], o_q_norm[j], o_k_norm[j],
                                   o_lambda_q1[j], o_lambda_k1[j], o_lambda_q2[j], o_lambda_k2[j],
                                   o_subln[j], o_w_o[j], lambda_init)
            h = rms_norm(x, o_ln_ffn[j])
            x = x + moe_swiglu(h, o_router[j], o_moe_gate[j], o_moe_up[j], o_moe_down[j])
    return x


GRID_W = 64
CTX_LEN = 256
QBLK = 128
ROPE_THETA_2 = 10000.0
EPS = 1e-6

POOL_GROUPS = 4
POOL_CH = 64
POOL_DIM = POOL_GROUPS * POOL_CH
POOL_WINDOWS = (2, 4, 8, 16)

HEAD_DIM = 64
GQA_HEADS = 12
GQA_KV_HEADS = 4
GQA_GROUP = GQA_HEADS // GQA_KV_HEADS
GQA_Q_DIM = GQA_HEADS * HEAD_DIM
GQA_KV_DIM = GQA_KV_HEADS * HEAD_DIM
L0_IN = POOL_DIM + GQA_Q_DIM + 2 * GQA_KV_DIM
L0_MIX = POOL_DIM + GQA_Q_DIM

MLA_HEADS = 8
MLA_NOPE = 64
MLA_ROPE = 32
MLA_QK = MLA_NOPE + MLA_ROPE
MLA_V = 64
MLA_Q_LORA = 384
MLA_KV_LORA = 256

NA_HEADS = 8
NA_HEAD_DIM = 64
NA_DIM = NA_HEADS * NA_HEAD_DIM
NA_ROWS = 8
NA_COLS = 16

L1_IN = MLA_Q_LORA + MLA_KV_LORA + MLA_ROPE + 3 * NA_DIM
L1_MIX = MLA_HEADS * MLA_V + NA_DIM

FFN_DIM_2 = -(-8 * D_MODEL // (3 * 256)) * 256


def rmsnorm(x, g):
    xf = x.astype(jnp.float32)
    y = xf * lax.rsqrt(jnp.mean(xf * xf, axis=-1, keepdims=True) + EPS)
    return y.astype(x.dtype) * g

def rope_1d(x, pos):
    d = x.shape[-1]
    half = d // 2
    inv = (ROPE_THETA_2 ** (-np.arange(half, dtype=np.float32) * 2.0 / d)).astype(np.float32)
    ang = pos.astype(jnp.float32)[:, None] * inv[None, :]
    shape = (1, x.shape[1]) + (1,) * (x.ndim - 3) + (half,)
    cos = jnp.cos(ang).reshape(shape)
    sin = jnp.sin(ang).reshape(shape)
    xf = x.astype(jnp.float32)
    x1, x2 = xf[..., :half], xf[..., half:]
    return jnp.concatenate([x1 * cos - x2 * sin, x1 * sin + x2 * cos], axis=-1).astype(x.dtype)

def axial_rope(x, row, col):
    half = x.shape[-1] // 2
    return jnp.concatenate([rope_1d(x[..., :half], row), rope_1d(x[..., half:], col)], axis=-1)

def split_cols(p, sizes):
    return jnp.split(p, [int(o) for o in np.cumsum(sizes)[:-1]], axis=-1)

def block_attention(q, k, v, scale):
    B, T = q.shape[:2]
    qb = jnp.moveaxis(q.reshape((B, T // QBLK, QBLK) + q.shape[2:]), 1, 0)

    def one_block(q_blk):
        s = jnp.einsum("bqhgd,bkhd->bhgqk", q_blk, k).astype(jnp.float32) * scale
        p = jax.nn.softmax(s, axis=-1).astype(v.dtype)
        return jnp.einsum("bhgqk,bkhd->bqhgd", p, v)

    o = lax.map(one_block, qb)
    return jnp.moveaxis(o, 0, 1).reshape((B, T) + o.shape[3:])

def multiscale_pool(u, w_grp, ch_scale):
    B, T, _ = u.shape
    ug = u.reshape(B, T, POOL_GROUPS, POOL_CH).astype(jnp.float32)
    csum = jnp.concatenate([jnp.zeros((B, 1, POOL_GROUPS, POOL_CH), jnp.float32),
                            jnp.cumsum(ug, axis=1)], axis=1)
    t = np.arange(T)
    lo = np.stack([np.clip(t - w // 2, 0, T) for w in POOL_WINDOWS], axis=-1).astype(np.int32)
    hi = np.stack([np.clip(t - w // 2 + w, 0, T) for w in POOL_WINDOWS], axis=-1).astype(np.int32)
    grp = np.arange(POOL_GROUPS, dtype=np.int32)[None, :]
    win_sum = csum[:, hi, grp] - csum[:, lo, grp]
    count = jnp.asarray((hi - lo).astype(np.float32))[None, :, :, None]
    d = (win_sum / count - ug).astype(u.dtype)
    y = jnp.einsum("btgc,gcd->btgd", d, w_grp).reshape(B, T, POOL_DIM)
    return y * ch_scale

def neighbourhood_attention(q, k, v, k_ctx, v_ctx, rpb, scale):
    B, S, H, dh = q.shape
    rows = S // GRID_W
    kr = min(NA_ROWS, rows)
    kc = NA_COLS
    cols = np.arange(GRID_W)
    key_col = (np.clip(cols - kc // 2, 0, GRID_W - kc)[:, None] + np.arange(kc)[None, :]).astype(np.int32)
    dc_idx = (key_col - cols[:, None] + (NA_COLS - 1)).astype(np.int32)
    n_win = kr * kc
    q_rows = jnp.moveaxis(q.reshape(B, rows, GRID_W, H, dh), 1, 0)

    def one_row(args):
        r, q_r = args
        r0 = jnp.clip(r - kr // 2, 0, rows - kr)
        key_row = r0 + jnp.arange(kr, dtype=jnp.int32)
        idx = (key_row[None, :, None] * GRID_W + key_col[:, None, :]).reshape(GRID_W, n_win)
        k_w = jnp.take(k, idx, axis=1)
        v_w = jnp.take(v, idx, axis=1)
        bias = rpb[:, key_row - r + (NA_ROWS - 1)][:, :, dc_idx]
        bias = jnp.transpose(bias, (0, 2, 1, 3)).reshape(H, GRID_W, n_win)
        s_win = jnp.einsum("bqhd,bqkhd->bhqk", q_r, k_w).astype(jnp.float32) * scale + bias.astype(jnp.float32)
        s_ctx = jnp.einsum("bqhd,bchd->bhqc", q_r, k_ctx).astype(jnp.float32) * scale
        p = jax.nn.softmax(jnp.concatenate([s_win, s_ctx], axis=-1), axis=-1).astype(v.dtype)
        return (jnp.einsum("bhqk,bqkhd->bqhd", p[..., :n_win], v_w)
                + jnp.einsum("bhqc,bchd->bqhd", p[..., n_win:], v_ctx))

    o = lax.map(one_row, (jnp.arange(rows, dtype=jnp.int32), q_rows))
    return jnp.moveaxis(o, 0, 1).reshape(B, S, H, dh)

def adaln(cond, w, b):
    d = w.shape[0]
    m = jax.nn.silu(cond) @ w + b
    return [m[:, None, i * d:(i + 1) * d] for i in range(6)]

def modulate(x, g, shift, scale):
    return rmsnorm(x, g) * (1.0 + scale) + shift

def swiglu_2(h, wg, wu, wd):
    return (jax.nn.silu(h @ wg) * (h @ wu)) @ wd

def mixer_pool_gqa(h, hc, row, col, need_ctx, w_in, pool_w, pool_scale, q_gain, k_gain, w_out):
    B, S, _ = h.shape
    Tc = hc.shape[1]
    sizes = (POOL_DIM, GQA_Q_DIM, GQA_KV_DIM, GQA_KV_DIM)
    a, q, k, v = split_cols(h @ w_in, sizes)
    ac, qc, kc, vc = split_cols(hc @ w_in, sizes)
    q = axial_rope(rmsnorm(q.reshape(B, S, GQA_KV_HEADS, GQA_GROUP, HEAD_DIM), q_gain), row, col)
    k = axial_rope(rmsnorm(k.reshape(B, S, GQA_KV_HEADS, HEAD_DIM), k_gain), row, col)
    v = v.reshape(B, S, GQA_KV_HEADS, HEAD_DIM)
    kc = rmsnorm(kc.reshape(B, Tc, GQA_KV_HEADS, HEAD_DIM), k_gain)
    vc = vc.reshape(B, Tc, GQA_KV_HEADS, HEAD_DIM)
    scale = HEAD_DIM ** -0.5
    attn = block_attention(q, jnp.concatenate([kc, k], axis=1), jnp.concatenate([vc, v], axis=1),
                           scale).reshape(B, S, GQA_Q_DIM)
    out = jnp.concatenate([multiscale_pool(a, pool_w, pool_scale), attn], axis=-1) @ w_out
    if not need_ctx:
        return out, None
    qc = rmsnorm(qc.reshape(B, Tc, GQA_KV_HEADS, GQA_GROUP, HEAD_DIM), q_gain)
    attn_c = block_attention(qc, kc, vc, scale).reshape(B, Tc, GQA_Q_DIM)
    out_c = jnp.concatenate([multiscale_pool(ac, pool_w, pool_scale), attn_c], axis=-1) @ w_out
    return out, out_c

def mixer_mla_na(h, hc, row, col, need_ctx, w_in, q_a_gain, kv_a_gain, w_uq, w_ukv,
                 mla_q_gain, mla_k_gain, na_q_gain, na_k_gain, na_rpb, w_out):
    B, S, _ = h.shape
    Tc = hc.shape[1]
    sizes = (MLA_Q_LORA, MLA_KV_LORA, MLA_ROPE, NA_DIM, NA_DIM, NA_DIM)
    cq, ckv, kr, nq, nk, nv = split_cols(h @ w_in, sizes)
    cqc, ckvc, krc, nqc, nkc, nvc = split_cols(hc @ w_in, sizes)

    def mla_q(cq_, T):
        q_ = (rmsnorm(cq_, q_a_gain) @ w_uq).reshape(B, T, MLA_HEADS, MLA_QK)
        return rmsnorm(q_, mla_q_gain)

    def mla_kv(ckv_, kr_, T):
        kv = (rmsnorm(ckv_, kv_a_gain) @ w_ukv).reshape(B, T, MLA_HEADS, MLA_NOPE + MLA_V)
        k_rope = jnp.broadcast_to(kr_[:, :, None, :], (B, T, MLA_HEADS, MLA_ROPE))
        k_ = jnp.concatenate([kv[..., :MLA_NOPE], k_rope], axis=-1)
        return rmsnorm(k_, mla_k_gain), kv[..., MLA_NOPE:]

    def rope_tail(t):
        return jnp.concatenate([t[..., :MLA_NOPE], axial_rope(t[..., MLA_NOPE:], row, col)], axis=-1)

    mq = rope_tail(mla_q(cq, S))
    mk, mv = mla_kv(ckv, kr, S)
    mk = rope_tail(mk)
    mkc, mvc = mla_kv(ckvc, krc, Tc)
    mla_scale = MLA_QK ** -0.5
    o_mla = block_attention(mq[:, :, :, None], jnp.concatenate([mkc, mk], axis=1),
                            jnp.concatenate([mvc, mv], axis=1), mla_scale).reshape(B, S, MLA_HEADS * MLA_V)

    q_na = rmsnorm(nq.reshape(B, S, NA_HEADS, NA_HEAD_DIM), na_q_gain)
    k_na = rmsnorm(nk.reshape(B, S, NA_HEADS, NA_HEAD_DIM), na_k_gain)
    v_na = nv.reshape(B, S, NA_HEADS, NA_HEAD_DIM)
    k_nac = rmsnorm(nkc.reshape(B, Tc, NA_HEADS, NA_HEAD_DIM), na_k_gain)
    v_nac = nvc.reshape(B, Tc, NA_HEADS, NA_HEAD_DIM)
    na_scale = NA_HEAD_DIM ** -0.5
    o_na = neighbourhood_attention(q_na, k_na, v_na, k_nac, v_nac, na_rpb, na_scale).reshape(B, S, NA_DIM)

    out = jnp.concatenate([o_mla, o_na], axis=-1) @ w_out
    if not need_ctx:
        return out, None
    mqc = mla_q(cqc, Tc)
    o_mla_c = block_attention(mqc[:, :, :, None], mkc, mvc, mla_scale).reshape(B, Tc, MLA_HEADS * MLA_V)
    q_nac = rmsnorm(nqc.reshape(B, Tc, NA_HEADS, NA_HEAD_DIM), na_q_gain)
    o_na_c = block_attention(q_nac[:, :, :, None], k_nac, v_nac, na_scale).reshape(B, Tc, NA_DIM)
    out_c = jnp.concatenate([o_mla_c, o_na_c], axis=-1) @ w_out
    return out, out_c

def second_inputs(seed: int = 0) -> dict:
    key = jax.random.key(seed)
    ks = iter(jax.random.split(key, 48))

    def nrm(shape, s):
        return jax.random.normal(next(ks), shape, jnp.float32) * s

    def gain(n):
        return 1.0 + nrm((n,), 0.1)

    D = D_MODEL
    inp = {}
    inp["x"] = nrm((BATCH, SEQ, D), 1.0)
    inp["c"] = nrm((BATCH, D), 1.0)
    inp["ctx"] = nrm((BATCH, CTX_LEN, D), 1.0)
    inp["c_ctx"] = nrm((D,), 1.0)
    inp["l0_ada_w"] = nrm((D, 6 * D), 0.5 * D ** -0.5)
    inp["l0_ada_b"] = nrm((6 * D,), 0.02)
    inp["l0_norm_mix"] = gain(D)
    inp["l0_norm_ffn"] = gain(D)
    inp["l0_w_in"] = nrm((D, L0_IN), D ** -0.5)
    inp["l0_pool_w"] = nrm((POOL_GROUPS, POOL_CH, POOL_CH), POOL_CH ** -0.5)
    inp["l0_pool_scale"] = gain(POOL_DIM)
    inp["l0_q_gain"] = gain(HEAD_DIM)
    inp["l0_k_gain"] = gain(HEAD_DIM)
    inp["l0_w_out"] = nrm((L0_MIX, D), L0_MIX ** -0.5)
    inp["l0_ffn_w_gate"] = nrm((D, FFN_DIM_2), D ** -0.5)
    inp["l0_ffn_w_up"] = nrm((D, FFN_DIM_2), D ** -0.5)
    inp["l0_ffn_w_down"] = nrm((FFN_DIM_2, D), FFN_DIM_2 ** -0.5)
    inp["l1_ada_w"] = nrm((D, 6 * D), 0.5 * D ** -0.5)
    inp["l1_ada_b"] = nrm((6 * D,), 0.02)
    inp["l1_norm_mix"] = gain(D)
    inp["l1_norm_ffn"] = gain(D)
    inp["l1_w_in"] = nrm((D, L1_IN), D ** -0.5)
    inp["l1_mla_q_a_gain"] = gain(MLA_Q_LORA)
    inp["l1_mla_kv_a_gain"] = gain(MLA_KV_LORA)
    inp["l1_mla_w_uq"] = nrm((MLA_Q_LORA, MLA_HEADS * MLA_QK), MLA_Q_LORA ** -0.5)
    inp["l1_mla_w_ukv"] = nrm((MLA_KV_LORA, MLA_HEADS * (MLA_NOPE + MLA_V)), MLA_KV_LORA ** -0.5)
    inp["l1_mla_q_gain"] = gain(MLA_QK)
    inp["l1_mla_k_gain"] = gain(MLA_QK)
    inp["l1_na_q_gain"] = gain(NA_HEAD_DIM)
    inp["l1_na_k_gain"] = gain(NA_HEAD_DIM)
    inp["l1_na_rpb"] = nrm((NA_HEADS, 2 * NA_ROWS - 1, 2 * NA_COLS - 1), 0.1)
    inp["l1_w_out"] = nrm((L1_MIX, D), L1_MIX ** -0.5)
    inp["l1_ffn_w_gate"] = nrm((D, FFN_DIM_2), D ** -0.5)
    inp["l1_ffn_w_up"] = nrm((D, FFN_DIM_2), D ** -0.5)
    inp["l1_ffn_w_down"] = nrm((FFN_DIM_2, D), FFN_DIM_2 ** -0.5)
    return inp

def second_block(x, c, ctx, c_ctx,
              l0_ada_w, l0_ada_b, l0_norm_mix, l0_norm_ffn, l0_w_in, l0_pool_w, l0_pool_scale,
              l0_q_gain, l0_k_gain, l0_w_out, l0_ffn_w_gate, l0_ffn_w_up, l0_ffn_w_down,
              l1_ada_w, l1_ada_b, l1_norm_mix, l1_norm_ffn, l1_w_in, l1_mla_q_a_gain, l1_mla_kv_a_gain,
              l1_mla_w_uq, l1_mla_w_ukv, l1_mla_q_gain, l1_mla_k_gain, l1_na_q_gain, l1_na_k_gain,
              l1_na_rpb, l1_w_out, l1_ffn_w_gate, l1_ffn_w_up, l1_ffn_w_down):
    S = x.shape[1]
    tok = jnp.arange(S, dtype=jnp.int32)
    row = tok // GRID_W
    col = tok % GRID_W
    layers = [
        (l0_ada_w, l0_ada_b, l0_norm_mix, l0_norm_ffn, l0_ffn_w_gate, l0_ffn_w_up, l0_ffn_w_down,
         mixer_pool_gqa, (l0_w_in, l0_pool_w, l0_pool_scale, l0_q_gain, l0_k_gain, l0_w_out)),
        (l1_ada_w, l1_ada_b, l1_norm_mix, l1_norm_ffn, l1_ffn_w_gate, l1_ffn_w_up, l1_ffn_w_down,
         mixer_mla_na, (l1_w_in, l1_mla_q_a_gain, l1_mla_kv_a_gain, l1_mla_w_uq, l1_mla_w_ukv,
                        l1_mla_q_gain, l1_mla_k_gain, l1_na_q_gain, l1_na_k_gain, l1_na_rpb, l1_w_out)),
    ]
    xc = ctx
    for i in range(DEPTH):
        ada_w, ada_b, n_mix, n_ffn, wg, wu, wd, mixer, mparams = layers[i]
        need_ctx = i < DEPTH - 1
        sh1, sc1, g1, sh2, sc2, g2 = adaln(c, ada_w, ada_b)
        csh1, csc1, cg1, csh2, csc2, cg2 = adaln(c_ctx[None, :], ada_w, ada_b)
        h = modulate(x, n_mix, sh1, sc1)
        hc = modulate(xc, n_mix, csh1, csc1)
        o, oc = mixer(h, hc, row, col, need_ctx, *mparams)
        x = x + g1 * o
        x = x + g2 * swiglu_2(modulate(x, n_ffn, sh2, sc2), wg, wu, wd)
        if need_ctx:
            xc = xc + cg1 * oc
            xc = xc + cg2 * swiglu_2(modulate(xc, n_ffn, csh2, csc2), wg, wu, wd)
    return x


def setup_inputs(seed=0):
    out = dict(first_inputs(seed))
    for name, value in second_inputs(seed + 1).items():
        if name != "x":
            out[name + "_2"] = value
    return out


def reference(
    x, positions, e_ln_mix, e_w_in, e_conv_w, e_conv_b, e_gate_a_w, e_gate_a_b, e_gate_x_w,
    e_gate_x_b, e_lru_lambda, e_shift_mu, e_w0, e_w2, e_a0, e_a2, e_g2, e_k_k, e_k_a, e_r_k,
    e_gn_w, e_gn_b, e_w_out, e_ln_ffn, e_ffn_gate, e_ffn_up, e_ffn_down, o_ln_mix, o_w_qkv,
    o_q_norm, o_k_norm, o_lambda_q1, o_lambda_k1, o_lambda_q2, o_lambda_k2, o_subln, o_w_o,
    o_ln_ffn, o_router, o_moe_gate, o_moe_up, o_moe_down, c_2, ctx_2, c_ctx_2, l0_ada_w_2,
    l0_ada_b_2, l0_norm_mix_2, l0_norm_ffn_2, l0_w_in_2, l0_pool_w_2, l0_pool_scale_2,
    l0_q_gain_2, l0_k_gain_2, l0_w_out_2, l0_ffn_w_gate_2, l0_ffn_w_up_2, l0_ffn_w_down_2,
    l1_ada_w_2, l1_ada_b_2, l1_norm_mix_2, l1_norm_ffn_2, l1_w_in_2, l1_mla_q_a_gain_2,
    l1_mla_kv_a_gain_2, l1_mla_w_uq_2, l1_mla_w_ukv_2, l1_mla_q_gain_2, l1_mla_k_gain_2,
    l1_na_q_gain_2, l1_na_k_gain_2, l1_na_rpb_2, l1_w_out_2, l1_ffn_w_gate_2, l1_ffn_w_up_2,
    l1_ffn_w_down_2,
):
    x = first_block(
        x, positions, e_ln_mix, e_w_in, e_conv_w, e_conv_b, e_gate_a_w, e_gate_a_b, e_gate_x_w,
        e_gate_x_b, e_lru_lambda, e_shift_mu, e_w0, e_w2, e_a0, e_a2, e_g2, e_k_k, e_k_a, e_r_k,
        e_gn_w, e_gn_b, e_w_out, e_ln_ffn, e_ffn_gate, e_ffn_up, e_ffn_down, o_ln_mix, o_w_qkv,
        o_q_norm, o_k_norm, o_lambda_q1, o_lambda_k1, o_lambda_q2, o_lambda_k2, o_subln, o_w_o,
        o_ln_ffn, o_router, o_moe_gate, o_moe_up, o_moe_down,
    )
    return second_block(
        x, c_2, ctx_2, c_ctx_2, l0_ada_w_2, l0_ada_b_2, l0_norm_mix_2, l0_norm_ffn_2, l0_w_in_2,
        l0_pool_w_2, l0_pool_scale_2, l0_q_gain_2, l0_k_gain_2, l0_w_out_2, l0_ffn_w_gate_2,
        l0_ffn_w_up_2, l0_ffn_w_down_2, l1_ada_w_2, l1_ada_b_2, l1_norm_mix_2, l1_norm_ffn_2,
        l1_w_in_2, l1_mla_q_a_gain_2, l1_mla_kv_a_gain_2, l1_mla_w_uq_2, l1_mla_w_ukv_2,
        l1_mla_q_gain_2, l1_mla_k_gain_2, l1_na_q_gain_2, l1_na_k_gain_2, l1_na_rpb_2,
        l1_w_out_2, l1_ffn_w_gate_2, l1_ffn_w_up_2, l1_ffn_w_down_2,
    )


_drawn_inputs = setup_inputs


def setup_inputs(seed=0):
    import zlib

    import numpy as np

    out = dict(_drawn_inputs(seed))
    spreads = {}
    factors = {'e_gate_a_b': 8.0,
     'e_gate_x_b': 8.0,
     'e_k_k': 4.963,
     'e_k_a': 2.825,
     'e_gn_w': 3.714,
     'e_gn_b': 3.824,
     'o_k_norm': 3.162,
     'o_lambda_q1': 2.693,
     'o_subln': 3.998,
     'ctx_2': 3.295,
     'l0_ada_b_2': 4.057,
     'l0_norm_mix_2': 5.975,
     'l0_norm_ffn_2': 2.684,
     'l0_pool_scale_2': 5.824,
     'l0_q_gain_2': 8.0,
     'l0_k_gain_2': 8.0,
     'l1_ada_b_2': 4.533,
     'l1_norm_mix_2': 8.0,
     'l1_norm_ffn_2': 2.964,
     'l1_mla_q_a_gain_2': 8.0,
     'l1_mla_kv_a_gain_2': 8.0,
     'l1_mla_w_uq_2': 4.619,
     'l1_mla_q_gain_2': 8.0,
     'l1_mla_k_gain_2': 8.0,
     'l1_na_q_gain_2': 8.0,
     'l1_na_k_gain_2': 8.0,
     'l1_na_rpb_2': 40.765}
    for name, (base, spread) in spreads.items():
        noise = np.random.default_rng([zlib.crc32(name.encode()), seed]).standard_normal(out[name].shape)
        drawn = base * np.exp(spread * noise) if base else spread * noise
        out[name] = jnp.asarray(drawn.astype(out[name].dtype))
    for name, factor in factors.items():
        out[name] = (out[name] * factor).astype(out[name].dtype)
    return out
```

```python
import math

import numpy as np

import concourse.bass as bass
from concourse import mybir
from contextlib import ExitStack

P = 128
D = 1024
KD = D // P
T = 256
NT = T // P
F_FFN = 2816
N_EXP = 8
F_EXP = 3584
RING = 4
SLOT = 3 * D
FBLK = 128
NB_FFN = F_FFN // FBLK
NB_EXP = F_EXP // FBLK
LAMBDA_INIT = 0.8 - 0.6 * math.exp(-0.3)
NEG = -1.0e30
CH = 64
EXP_M_HALF = math.exp(-0.5)
EVEN_IN = 2816
QKV = 3072
L0_IN = 1536
L1_IN = 2208
COLS = 384

HEADS0 = (0, 3, 1, 4, 2, 5, 6, 9, 7, 10, 8, 11)

STREAM = [
    ("ada0", 6 * D // COLS), ("ada1", 6 * D // COLS),
    ("e_in", -(-EVEN_IN // COLS)), ("e_out", 3), ("e_ffn", NB_FFN),
    ("qkv", QKV // COLS), ("o_out", 3),
    ("l0_in", L0_IN // COLS), ("l0_out", 3), ("l0_ffn", NB_FFN), ("l0_ffn_ctx", NB_FFN),
    ("l1_in", -(-L1_IN // COLS)), ("l1_uq", 1), ("l1_ukv", 1), ("l1_out", 3), ("l1_ffn", NB_FFN),
]
FIRST = {}
N_SLOTS = 0
for _name, _n in STREAM:
    FIRST[_name] = N_SLOTS
    N_SLOTS += _n
N_SLOTS_PADDED = -(-N_SLOTS // RING) * RING
MOE_SLOT0 = N_SLOTS_PADDED
N_STREAM = N_SLOTS_PADDED + N_EXP * NB_EXP
G_MOE = FIRST["l0_in"] // RING
G_EXP = NB_EXP // RING
assert FIRST["l0_in"] % RING == 0 and NB_EXP % RING == 0
CAP = P
MAX_VISITS = N_EXP + 3

VECS = [("e_ln_mix", 8), ("e_ln_ffn", 8), ("o_ln_mix", 8), ("o_ln_ffn", 8),
        ("l0_norm_mix_2", 8), ("l0_norm_ffn_2", 8), ("l1_norm_mix_2", 8), ("l1_norm_ffn_2", 8),
        ("e_conv_w", 16), ("e_conv_b", 4), ("e_gate_a_b", 4), ("e_gate_x_b", 4), ("e_lru_lambda", 4),
        ("e_shift_mu", 14), ("e_w0", 4), ("e_a0", 4), ("e_k_k", 4), ("e_k_a", 4), ("e_r_k", 4),
        ("e_gn_w", 4), ("e_gn_b", 4), ("cond", 16), ("l0_ada_b_2", 48), ("l1_ada_b_2", 48),
        ("l1_mla_q_a_gain_2", 3), ("l1_mla_kv_a_gain_2", 2), ("l0_pool_scale_2", 2)]
MATS = [("gate_a", 512), ("gate_x", 512), ("w2a2", 512), ("g2", 512), ("router", 64), ("pool_w", 256)]
ROWS = [("o_q_norm", 64), ("o_k_norm", 64), ("o_subln", 128), ("o_lambda_q1", 64), ("o_lambda_k1", 64),
        ("o_lambda_q2", 64), ("o_lambda_k2", 64), ("l0_q_gain_2", 64), ("l0_k_gain_2", 64),
        ("l1_mla_q_gain_2", 96), ("l1_mla_k_gain_2", 96), ("l1_na_q_gain_2", 64), ("l1_na_k_gain_2", 64)]
PACK = {}
N_PACK = 0
for _name, _n in VECS + MATS + ROWS:
    PACK[_name] = (N_PACK, _n)
    N_PACK += _n
CONSTS = [("ident", 128), ("ones", 128), ("headones", 128), ("mask4", 512), ("level", 6 * 128),
          ("scanmask", T), ("causal", 128), ("rope64", 2 * NT * 32), ("rope32", 2 * NT * 16),
          ("iota", 128), ("freq", 8)]
CONST = {}
N_CONST = 0
for _name, _n in CONSTS:
    CONST[_name] = (N_CONST, _n)
    N_CONST += _n
N_BAND = 4 * NT * T
N_BIAS = NT * 8 * T


def program(nc, x_in, ctx_in, pos_in, pack_in, const_in, band_in, bias_in, stream_in, out):
    f32 = mybir.dt.float32
    i32 = mybir.dt.int32
    u32 = mybir.dt.uint32
    ALU = mybir.AluOpType
    ACT = mybir.ActivationFunctionType
    AX = mybir.AxisListType
    MUL, ADD, SUB, MAX, MIN = ALU.mult, ALU.add, ALU.subtract, ALU.max, ALU.min

    ctx = ExitStack()
    with ctx:
        def sb(name, cols, dt=f32):
            return ctx.enter_context(nc.sbuf_tensor(name, [P, cols], dt))

        ring = sb("ring", RING * SLOT)
        x = sb("x", NT * D)
        xc = sb("xc", NT * D)
        pack = sb("pack", N_PACK)
        const = sb("const", N_CONST)
        mods = sb("mods", 2 * 48 * 2)
        geff = sb("geff", 2 * 2 * 2 * 8)
        small = sb("small", 768)
        ARENA = (nc.sbuf_usable_end - 16512) // 4 - (RING * SLOT + 2 * NT * D + N_PACK + N_CONST + 192 + 64 + 768) - 40
        arena = sb("arena", ARENA)
        psum = ctx.enter_context(nc.psum_tensor("psum", [P, 8, 512], f32))

        sems = {}

        def sem(name):
            if name not in sems:
                sems[name] = ctx.enter_context(nc.semaphore(name))
            return sems[name]

        w_ready = [sem(f"w_ready{r}") for r in range(RING)]
        w_used = [sem(f"w_used{r}") for r in range(RING)]
        e_ready = [sem(f"expert_ready{r}") for r in range(RING)]
        e_used = [sem(f"expert_used{r}") for r in range(RING)]

        def ar(o, n, spec=None, **kw):
            assert o + n <= ARENA, (o, n, ARENA)
            v = arena[:, o:o + n]
            return v.rearrange(spec, **kw) if spec else v

        def vec(name, i=0, n=1):
            o = PACK[name][0] + i
            return pack[:, o:o + n]

        def mat(name):
            o, n = PACK[name]
            return pack[:, o:o + n]

        def cst(name):
            o, n = CONST[name]
            return const[:, o:o + n]

        ident = cst("ident")
        slot_of = [ring[:, r * SLOT:(r + 1) * SLOT] for r in range(RING)]
        x_tm = x[:, :].rearrange("p (j d) -> p j d", j=NT)
        xc_tm = xc[:, :].rearrange("p (j d) -> p j d", j=NT)
        mod = [mods[:, 96 * l:96 * l + 96].rearrange("p (c n) -> p c n", n=2) for l in range(2)]

        def ge(layer, which, cond, c):
            o = ((layer * 2 + which) * 2 + cond) * 8 + c
            return geff[:, o:o + 1]

        O_XN, O_HT, O_W = 0, 2048, 6144
        xn = ar(O_XN, 2048, "p (j d) -> p j d", j=NT)
        hT = ar(O_HT, 4096, "p (k t) -> p k t", k=KD)
        ebuf = ar(O_W, 512, "p (b t) -> p b t", b=2)
        hbuf = ar(O_W + 512, 512, "p (b t) -> p b t", b=2)

        counts = {}

        def step(eng, ins, name):
            ins.then_inc(sem(name), 1)
            counts[name] = counts.get(name, 0) + 1
            eng.wait_ge(sem(name), counts[name])

        def slot_ready(pe, n):
            pe.wait_ge(w_ready[n % RING], 16 * (n // RING + 1))

        def slot_used(eng, n):
            eng.wait_ge(w_used[n % RING], n // RING + 1)

        block = ctx.enter_context(nc.Block())

        SM = {}
        sm_at = [0]

        def sm(name, n):
            if name not in SM:
                SM[name] = small[:, sm_at[0]:sm_at[0] + n]
                sm_at[0] += n
                assert sm_at[0] <= 768, name
            return SM[name]

        ss, ms, std, rstd = sm("ss", 2), sm("ms", 2), sm("std", 2), sm("rstd", 2)
        scT = sm("scT", 16)

        def norm_dve(dve, k, src, gain, shift, off):
            for j in range(NT):
                step(dve, dve.tensor_tensor_reduce(xn[:, j, :], src[:, j, :], src[:, j, :], 1.0, 0.0, MUL, ADD,
                                                   ss[:, j:j + 1]), "dve_step")
            step(dve, dve.tensor_scalar(ms, ss, 1.0 / D, 1e-6, MUL, ADD), "norm_ms")
            dve.wait_ge(sem("norm_std"), k + 1)
            step(dve, dve.reciprocal(rstd, std), "dve_step")
            dve.tensor_scalar(xn[:, 0, :], src[:, 0, :], rstd[:, 0:1], None, MUL)
            step(dve, dve.tensor_scalar(xn[:, 1, :], src[:, 1, :], rstd[:, 1:2], None, MUL), "norm_xn")
            for c in range(KD):
                if c % 2 == 0:
                    dve.wait_ge(sem("norm_tr"), 4 * k + c // 2 + 1)
                src_ps = psum[:, c // 2, (c % 2) * T:(c % 2) * T + T]
                ins = dve.tensor_scalar(hT[:, c, off:off + T], src_ps, gain(c), shift(c) if shift else None, MUL,
                                        *([ADD] if shift else []))
            step(dve, ins, "norm_hT")

        def norm_act(act, k):
            act.wait_ge(sem("norm_ms"), k + 1)
            act.activation(std, ms, ACT.Sqrt).then_inc(sem("norm_std"), 1)

        def norm_pe(pe, k):
            pe.wait_ge(sem("norm_xn"), k + 1)
            for c in range(KD):
                for j in range(NT):
                    ins = pe.transpose(psum[:, c // 2, (c % 2) * T + j * P:(c % 2) * T + j * P + P],
                                       xn[:, j, c * P:(c + 1) * P], ident)
                if c % 2:
                    ins.then_inc(sem("norm_tr"), 1)

        def runs(nb):
            return (nb - 2) // RING, 2 + (nb - 2) // RING * RING

        def gate_up_pe(pe, i, r, blk, turn, off):
            pe.wait_ge(w_ready[r], turn * 16 + 16)
            if not (isinstance(blk, int) and blk < 2):
                pe.wait_ge(sem("h_done"), blk - 1)
            w = slot_of[r]
            for part in range(2):
                for k in range(KD):
                    ins = pe.matmul(psum[:, 4 + i % 2, part * T:part * T + T],
                                    w[:, part * D + k * P:part * D + (k + 1) * P], hT[:, k, off:off + T],
                                    start=(k == 0), stop=(k == KD - 1))
            ins.then_inc(sem("gu_done"), 1)

        def down_pe(pe, i, r, blk, first, last):
            pe.wait_ge(sem("h_done"), blk + 1)
            w = slot_of[r]
            for j in range(NT):
                for hf in range(2):
                    ins = pe.matmul(psum[:, 2 * j + hf, :], hbuf[:, i % 2, j * P:(j + 1) * P],
                                    w[:, 2 * D + hf * 512:2 * D + (hf + 1) * 512], start=first, stop=last)
            ins.then_inc(w_used[r], 1)

        def ffn_pe(pe, n0, b0, nb, off):
            t0 = n0 // RING
            ph = n0 % RING
            loops, tail = runs(nb)

            def gu(i, it=0):
                gate_up_pe(pe, i, (ph + i) % RING, it * RING + (b0 + i), it + (t0 + (ph + i) // RING), off)

            def dn(i, it=0):
                down_pe(pe, i, (ph + i) % RING, it * RING + (b0 + i), i == 0, isinstance(it, int) and i == nb - 1)

            gu(0)
            gu(1)
            dn(0)
            with pe.Fori(0, loops) as it:
                for u in range(RING):
                    gu(2 + u, it)
                    dn(1 + u, it)
            for i in range(tail, nb):
                gu(i)
                dn(i - 1)
            dn(nb - 1)

        def block_act(act, i, blk):
            act.wait_ge(sem("gu_done"), blk + 1)
            if not (isinstance(blk, int) and blk < 2):
                act.wait_ge(sem("h_done"), blk - 1)
            act.activation(ebuf[:, i % 2, :], psum[:, 4 + i % 2, 0:T], ACT.Silu).then_inc(sem("ffn_silu"), 1)

        def block_dve(dve, i, blk, r, turn, old):
            dve.wait_ge(sem("ffn_silu"), blk + 1)
            if old:
                dve.wait_ge(w_used[r], turn + 1)
            dve.tensor_tensor(hbuf[:, i % 2, :], ebuf[:, i % 2, :], psum[:, 4 + i % 2, T:2 * T], MUL)\
               .then_inc(sem("h_done"), 1)

        def ffn_act(act, b0, nb):
            loops, tail = runs(nb)
            for i in range(2):
                block_act(act, i, b0 + i)
            with act.Fori(0, loops) as it:
                for u in range(RING):
                    block_act(act, u, it * RING + (b0 + 2 + u))
            for i in range(tail, nb):
                block_act(act, i, b0 + i)

        def ffn_dve(dve, n0, b0, nb):
            t0 = n0 // RING
            ph = n0 % RING
            loops, tail = runs(nb)

            def one(i, it=0):
                r = (ph + i - 2) % RING
                block_dve(dve, i, it * RING + (b0 + i), r, it + (t0 + (ph + i - 2) // RING) if i >= 2 else 0, i >= 2)

            one(0)
            one(1)
            with dve.Fori(0, loops) as it:
                for u in range(RING):
                    one(2 + u, it)
            for i in range(tail, nb):
                one(i)

        B0 = {}
        nblocks = 0
        for name, n in (("e_ffn", NB_FFN), ("l0_ffn", NB_FFN), ("l0_ffn_ctx", NB_FFN),
                        ("l1_ffn", NB_FFN)):
            B0[name] = nblocks
            nblocks += n

        def add_tokens(dve, dst, scale_row=None, tmp=None):
            for j in range(NT):
                src = psum[:, 2 * j:2 * j + 2, :].rearrange("p b n -> p (b n)")
                if scale_row is not None:
                    step(dve, dve.tensor_tensor(tmp, src, scale_row, MUL), "dve_step")
                    src = tmp
                step(dve, dve.tensor_tensor(dst[:, j, :], dst[:, j, :], src, ADD), "dve_step")

        def out_proj_pe(pe, n0, lhs, tiles):
            for s in range(3):
                slot_ready(pe, n0 + s)
                w = slot_of[(n0 + s) % RING]
                for k in range(3 * s, min(3 * s + 3, KD)):
                    for j in range(tiles):
                        for hf in range(2):
                            o = (k - 3 * s) * D + hf * 512
                            ins = pe.matmul(psum[:, 2 * j + hf, :], lhs[:, k, j * P:(j + 1) * P], w[:, o:o + 512],
                                            start=(k == 0), stop=(k == KD - 1))
                ins.then_inc(w_used[(n0 + s) % RING], 1)

        def ada_act(act):
            act.wait_ge(sem("pack_in"), 16)
            act.activation(scT, vec("cond", 0, 16), ACT.Silu).then_inc(sem("ada_silu"), 1)

        def ada_pe(pe):
            pe.wait_ge(sem("ada_silu"), 1)
            for l in range(2):
                n0 = FIRST[f"ada{l}"]
                for s in range(6 * D // COLS):
                    slot_ready(pe, n0 + s)
                    w = slot_of[(n0 + s) % RING]
                    for cc in range(COLS // P):
                        o = (3 * s + cc) * 2
                        for k in range(KD):
                            ins = pe.matmul(psum[:, l, o:o + 2], w[:, k * COLS + cc * P:k * COLS + (cc + 1) * P],
                                            scT[:, 2 * k:2 * k + 2], start=(k == 0), stop=(k == KD - 1))
                    ins.then_inc(w_used[(n0 + s) % RING], 1)

        def ada_mods_dve(dve):
            for l in range(2):
                slot_used(dve, FIRST[f"ada{l}"] + 6 * D // COLS - 1)
                b = vec(f"l{l}_ada_b_2", 0, 48).unsqueeze(2).to_broadcast([P, 48, 2])
                step(dve, dve.tensor_tensor(mod[l], psum[:, l, 0:96].rearrange("p (c n) -> p c n", n=2), b, ADD),
                     "dve_step")
                for which in range(2):
                    g = vec(f"l{l}_norm_{('mix', 'ffn')[which]}_2", 0, 8)
                    for cond in range(2):
                        o = ((l * 2 + which) * 2 + cond) * 8
                        sc = mod[l][:, 8 * (3 * which + 1):8 * (3 * which + 1) + 8, cond]
                        step(dve, dve.scalar_tensor_tensor(geff[:, o:o + 8], sc, 1.0, g, ADD, MUL), "dve_step")

        O_PJ, O_PS, O_YT, O_BON, O_GG, O_PR, O_BM, O_KM, O_MISC = 6144, 11864, 15448, 17496, 18520, 19544, 21592, 22616, 23640
        pj = ar(O_PJ, 22 * 260, "p (c t) -> p c t", c=22)
        ps = ar(O_PS, 14 * T, "p (c t) -> p c t", c=14)
        yT = ar(O_YT, 2048, "p (c t) -> p c t", c=8)
        bon = ar(O_BON, 1024, "p (c t) -> p c t", c=4)
        gg = ar(O_GG, 1024, "p (c t) -> p c t", c=4)
        PR = ar(O_PR, 2048, "p (c j w t) -> p c j w t", c=4, j=2, w=2)
        Bm = ar(O_BM, 1024, "p (c t) -> p c t", c=4)
        Km = ar(O_KM, 1024, "p (c t) -> p c t", c=4)
        eC = ar(O_MISC, 16, "p (c n) -> p c n", c=4)
        Ms = ar(O_MISC + 16, 256, "p (c v) -> p c v", c=4)
        oT = ar(O_MISC + 272, 1024, "p (c t) -> p c t", c=4)
        Ysb = ar(O_MISC + 1296, 512)
        t1, t2, t3, t4, t5, t6 = [ar(1024 * i, 1024, "p (c t) -> p c t", c=4) for i in range(6)]
        Q4 = ar(0, 4096, "p (h m t) -> p h m t", h=8, m=4)
        X, XT, AbT, Yb = [ar(4096 + 1024 * i, 1024, "p (h t) -> p h t", h=8) for i in range(4)]
        tm4 = [ar(8192 + 512 * i, 512) for i in range(4)]
        Vt, Bt, Kt, Pt = tm4
        Ub, GVb = ar(10240, 512), ar(10752, 512)
        WTb = ar(11264, 512, "p (c t) -> p c t", c=4)
        n_e = FIRST["e_in"]
        N_EIN = -(-EVEN_IN // COLS)

        def e_proj_pe(pe):
            pe.wait_ge(sem("norm_hT"), 1)
            for s in range(N_EIN):
                slot_ready(pe, n_e + s)
                if s >= 4:
                    pe.wait_ge(sem("e_proj_ev"), s - 3)
                w = slot_of[(n_e + s) % RING]
                for cc in range(min(3, 22 - 3 * s)):
                    for k in range(KD):
                        ins = pe.matmul(psum[:, 2 * (s % 4) + cc // 2, (cc % 2) * T:(cc % 2) * T + T],
                                        w[:, k * COLS + cc * P:k * COLS + (cc + 1) * P], hT[:, k, 0:T],
                                        start=(k == 0), stop=(k == KD - 1))
                ins.then_inc(w_used[(n_e + s) % RING], 1)

        def e_proj_act(act):
            for s in range(N_EIN):
                slot_used(act, n_e + s)
                n = min(3, 22 - 3 * s)
                src = psum[:, 2 * (s % 4):2 * (s % 4) + 2, :].rearrange("p b n -> p (b n)")[:, 0:n * T]
                act.activation(pj[:, 3 * s:3 * s + n, 4:260], src.rearrange("p (c t) -> p c t", c=n), ACT.Copy)\
                   .then_inc(sem("e_proj_ev"), 1)

        nab, nxb, spl = sm("nab", 4), sm("nxb", 4), sm("spl", 4)
        nw0, na0, omka = sm("nw0", 4), sm("na0", 4), sm("omka", 4)
        lz, lz2, lacc = sm("lz", 4), sm("lz2", 4), sm("lacc", 4)
        lexp = sm("lexp", 4)

        def cols_dve(dve):
            def S(ins, name="dve_step"):
                step(dve, ins, name)
            S(dve.tensor_scalar(nab, vec("e_gate_a_b", 0, 4), -1.0, None, MUL))
            S(dve.tensor_scalar(nxb, vec("e_gate_x_b", 0, 4), -1.0, None, MUL))
            S(dve.tensor_scalar(nw0, vec("e_w0", 0, 4), -1.0, None, MUL))
            S(dve.tensor_scalar(na0, vec("e_a0", 0, 4), -1.0, None, MUL))
            S(dve.tensor_scalar(omka, vec("e_k_a", 0, 4), -1.0, 1.0, MUL, ADD))
            lam = vec("e_lru_lambda", 0, 4)
            S(dve.tensor_scalar(lz, lam, -1.0, None, MUL))
            S(dve.tensor_tensor(lz, lz, lam, MAX), "lru_abs")
            dve.wait_ge(sem("lru_soft"), 1)
            S(dve.tensor_scalar(lz, lexp, 2.0, None, ADD))
            S(dve.reciprocal(lz, lz))
            S(dve.tensor_tensor(lz, lz, lexp, MUL))
            S(dve.tensor_tensor(lz2, lz, lz, MUL))
            S(dve.tensor_scalar(lacc, lz2, 2.0 / 17, 2.0 / 15, MUL, ADD))
            for n in (13, 11, 9, 7, 5, 3, 1):
                S(dve.tensor_tensor(lacc, lacc, lz2, MUL))
                S(dve.tensor_scalar(lacc, lacc, 2.0 / n, None, ADD))
            S(dve.tensor_tensor(lacc, lacc, lz, MUL))
            S(dve.tensor_scalar(lz, lam, -1.0, 0.0, MUL, MAX))
            S(dve.tensor_tensor(lacc, lacc, lz, ADD))
            S(dve.tensor_scalar(spl, lacc, -8.0, None, MUL))

        def lru_dve(dve):
            def S(ins, name="dve_step"):
                step(dve, ins, name)
            dve.wait_ge(sem("e_proj_ev"), N_EIN)
            for c in range(4):
                S(dve.tensor_scalar(t1[:, c, :], pj[:, c, 1:257], vec("e_conv_w", c), vec("e_conv_b", c), MUL, ADD))
            for n in range(1, 4):
                for c in range(4):
                    S(dve.scalar_tensor_tensor(t1[:, c, :], pj[:, c, 1 + n:257 + n], vec("e_conv_w", 4 * n + c),
                                               t1[:, c, :], MUL, ADD), "lru_xc" if (n, c) == (3, 3) else "dve_step")
            dve.wait_ge(sem("lru_exp"), 1)
            for t in (t2, t3):
                S(dve.tensor_scalar(t, t, 1e38, 1.0, MIN, ADD))
                S(dve.reciprocal(t, t))
            for c in range(4):
                S(dve.tensor_scalar(t2[:, c, :], t2[:, c, :], spl[:, c:c + 1], None, MUL),
                  "lru_loga" if c == 3 else "dve_step")
            dve.wait_ge(sem("lru_a"), 1)
            S(dve.tensor_tensor(t6, t4, t4, MUL))
            S(dve.scalar_tensor_tensor(t6, t6, 1.0, t5, ADD, MUL))
            S(dve.tensor_scalar(t6, t6, -1.0, 0.0, MUL, MAX), "lru_m")
            dve.wait_ge(sem("lru_sq"), 1)
            S(dve.tensor_tensor(t5, t5, t3, MUL))
            S(dve.tensor_tensor(t5, t5, t1, MUL))
            for c in range(4):
                S(dve.tensor_tensor_scan(yT[:, c, :], t4[:, c, :], t5[:, c, :], 0.0, MUL, ADD))
            g = pj[:, 4:8, 4:260]
            S(dve.tensor_tensor(t1, g, g, MUL))
            S(dve.tensor_scalar(t1, t1, 0.044715, 1.0, MUL, ADD))
            S(dve.tensor_tensor(t1, t1, g, MUL), "lru_z")
            dve.wait_ge(sem("lru_gelu"), 1)
            S(dve.tensor_scalar(t2, t2, 1e38, 1.0, MIN, ADD))
            S(dve.reciprocal(t2, t2))
            S(dve.tensor_tensor(t2, t2, g, MUL))
            S(dve.tensor_tensor(yT[:, 0:4, :], yT[:, 0:4, :], t2, MUL))

        def lru_pe(pe):
            pe.wait_ge(sem("lru_xc"), 1)
            for q, name in enumerate(("gate_a", "gate_x")):
                for c in range(4):
                    ins = pe.matmul(psum[:, 2 * q + c // 2, (c % 2) * T:(c % 2) * T + T],
                                    mat(name)[:, c * P:(c + 1) * P], t1[:, c, :], start=True, stop=True)
            ins.then_inc(sem("lru_gates"), 1)

        def lru_act(act):
            act.wait_ge(sem("lru_gates"), 1)
            for q, (t, b) in enumerate(((t2, nab), (t3, nxb))):
                for c in range(4):
                    ins = act.activation(t[:, c, :], psum[:, 2 * q + c // 2, (c % 2) * T:(c % 2) * T + T], ACT.Exp,
                                         bias=b[:, c:c + 1], scale=-1.0)
            ins.then_inc(sem("lru_exp"), 1)
            act.wait_ge(sem("lru_loga"), 1)
            act.activation(t4, t2, ACT.Exp)
            act.activation(t5, t2, ACT.Tanh).then_inc(sem("lru_a"), 1)
            act.wait_ge(sem("lru_m"), 1)
            act.activation(t5, t6, ACT.Sqrt).then_inc(sem("lru_sq"), 1)
            act.wait_ge(sem("lru_z"), 1)
            act.activation(t2, t1, ACT.Exp, scale=-2.0 * math.sqrt(2.0 / math.pi)).then_inc(sem("lru_gelu"), 1)

        def rwkv_in_dve(dve):
            def S(ins, name="dve_step"):
                step(dve, ins, name)
            S(dve.tensor_tensor(ps, pj[:, 8:22, 3:259], pj[:, 8:22, 4:260], SUB))
            for c in range(14):
                S(dve.scalar_tensor_tensor(ps[:, c, :], ps[:, c, :], vec("e_shift_mu", c), pj[:, 8 + c, 4:260],
                                           MUL, ADD), "rw_shift" if c == 13 else "dve_step")
            dve.wait_ge(sem("rw_act1"), 1)
            sg = ar(256, 256)
            S(dve.tensor_scalar(sg, sg, 1e38, 1.0, MIN, ADD))
            S(dve.reciprocal(sg, sg), "rw_sg")
            dve.wait_ge(sem("rw_act2"), 1)
            for t in (t2, t3):
                S(dve.tensor_scalar(t, t, 1e38, 1.0, MIN, ADD))
                S(dve.reciprocal(t, t))
            S(dve.tensor_scalar(t2, t2, -EXP_M_HALF, None, MUL))
            for c in range(4):
                S(dve.tensor_tensor_scan(t4[:, c, :], cst("scanmask"), t2[:, c, :], 0.0, MUL, ADD))
            S(dve.tensor_tensor(t2, t4, t2, SUB))
            r, k, v = ps[:, 0:4, :], ps[:, 4:8, :], ps[:, 8:12, :]
            for c in range(4):
                S(dve.tensor_scalar(t5[:, c, :], k[:, c, :], vec("e_k_k", c), None, MUL))
            S(dve.tensor_tensor(t6, t5, t5, MUL), "rw_kk2")
            dve.wait_ge(sem("rw_norm"), 1)
            S(dve.tensor_scalar(t6, t6, 1e-12, None, MAX))
            S(dve.reciprocal(t6, t6))
            S(dve.tensor_tensor(t5, t5, t6, MUL))
            for c in range(4):
                S(dve.tensor_scalar(t1[:, c, :], t3[:, c, :], vec("e_k_a", c), omka[:, c:c + 1], MUL, ADD))
            S(dve.tensor_tensor(t1, t1, k, MUL))
            S(dve.tensor_tensor(t6, r, t1, MUL))
            for c in range(4):
                S(dve.tensor_scalar(t6[:, c, :], t6[:, c, :], vec("e_r_k", c), None, MUL),
                  "rw_bonus" if c == 3 else "dve_step")
            dve.wait_ge(sem("rw_bonus_ps"), 1)
            S(dve.tensor_tensor(bon, psum[:, 0:2, :].rearrange("p b (c t) -> p (b c) t", c=2), v, MUL))
            dve.wait_ge(sem("rw_exps"), 1)
            tv = [t.rearrange("p c (j t) -> p c j t", j=NT) for t in (t2, t5, t6, r)]
            for j in range(NT):
                S(dve.tensor_tensor(PR[:, :, j, 0, :], tv[0][:, :, j, :], tv[1][:, :, j, :], MUL))
                S(dve.tensor_tensor(PR[:, :, j, 1, :], tv[2][:, :, j, :], tv[3][:, :, j, :], MUL))
            S(dve.tensor_tensor(t3, t3, t5, MUL))
            S(dve.tensor_tensor(Bm, t3, t4, MUL))
            S(dve.tensor_tensor(Km, t1, t4, MUL))
            S(dve.tensor_copy(eC, t6[:, :, CH - 1:T:CH]))
            S(dve.memset(Ms, 0.0), "rw_fm")

        def rwkv_in_act(act):
            act.wait_ge(sem("rw_shift"), 1)
            act.activation(arena[0:64, 0:256], ps[0:64, 12, :], ACT.Tanh)
            act.activation(ar(256, 256), ps[:, 13, :], ACT.Exp, scale=-1.0).then_inc(sem("rw_act1"), 1)
            act.wait_ge(sem("rw_lora"), 1)
            for q, (t, b) in enumerate(((t2, nw0), (t3, na0))):
                for c in range(4):
                    act.activation(t[:, c, :], psum[:, 2 * q + c // 2, (c % 2) * T:(c % 2) * T + T], ACT.Exp,
                                   bias=b[:, c:c + 1], scale=-1.0)
            act.activation(gg, psum[:, 4:6, :].rearrange("p b (c t) -> p (b c) t", c=2), ACT.Copy)\
               .then_inc(sem("rw_act2"), 1)
            act.wait_ge(sem("rw_n2"), 1)
            act.activation(t6, psum[:, 6:8, :].rearrange("p b (c t) -> p (b c) t", c=2), ACT.Sqrt)\
               .then_inc(sem("rw_norm"), 1)
            act.wait_ge(sem("rw_bonus_ps"), 1)
            act.activation(t2, t2, ACT.Exp)
            step(act, act.activation(t6, t4, ACT.Exp), "act_step")
            act.activation(t4, t4, ACT.Exp, scale=-1.0).then_inc(sem("rw_exps"), 1)

        def rwkv_in_pe(pe):
            pe.wait_ge(sem("rw_act1"), 1)
            pe.wait_ge(sem("rw_sg"), 1)
            w2a2 = mat("w2a2")
            for c in range(4):
                at = (c % 2) * T
                pe.matmul(psum[:, c // 2, at:at + T], w2a2[0:64, c * P:(c + 1) * P], arena[0:64, 0:256],
                          start=True, stop=True)
                pe.matmul(psum[:, 2 + c // 2, at:at + T], w2a2[64:128, c * P:(c + 1) * P], ps[64:128, 12, :],
                          start=True, stop=True)
                ins = pe.matmul(psum[:, 4 + c // 2, at:at + T], mat("g2")[:, c * P:(c + 1) * P], ar(256, 256),
                                start=True, stop=True)
            ins.then_inc(sem("rw_lora"), 1)
            for src, bank, wait, done in ((t6, 6, "rw_kk2", "rw_n2"), (t6, 0, "rw_bonus", "rw_bonus_ps")):
                pe.wait_ge(sem(wait), 1)
                for b in range(2):
                    ins = pe.matmul(psum[:, bank + b, :], cst("headones"),
                                    src[:, 2 * b:2 * b + 2, :].rearrange("p c t -> p (c t)"), start=True, stop=True)
                ins.then_inc(sem(done), 1)

        def hd(h):
            return 64 * (h % 2), h // 2

        def yo(h):
            return (h % 2) * 256 + (h // 2) * 64

        def rwkv_tile_pe(pe, j):
            if j == 0:
                pe.wait_ge(sem("rw_fm"), 1)
            else:
                pe.wait_ge(sem("seq_m"), 2 * j)
            tk = slice(j * P, (j + 1) * P)
            for a in range(4):
                for c in range(4):
                    src = (ps[:, 8 + c, tk], Bm[:, c, tk], Km[:, c, tk], PR[:, c, j, 0, :])[a]
                    ins = pe.transpose(psum[:, a, c * P:(c + 1) * P], src, ident)
            ins.then_inc(sem("rw_tm"), 1)
            for h in range(8):
                pb, c = hd(h)
                if h >= 4 or j:
                    pe.wait_ge(sem("rw_qev"), 8 * j + h - 3)
                rhs = PR[pb:pb + 64, c, j, :, :].rearrange("p w t -> p (w t)")
                pe.matmul(psum[:, 4 + h % 4, 0:256], Bm[pb:pb + 64, c, tk], rhs, start=True, stop=True)
                pe.matmul(psum[:, 4 + h % 4, 256:512], Km[pb:pb + 64, c, tk], rhs, start=True, stop=True)\
                  .then_inc(sem("rw_q"), 1)
            pe.wait_ge(sem("rw_tmev"), j + 1)
            for l in range(6):
                for g in range(2):
                    n = (6 * j + l) * 2 + g
                    pe.wait_ge(sem("inv_a"), n + 1)
                    for h in range(4 * g, 4 * g + 4):
                        o = (h % 4) * P
                        ins = pe.matmul(psum[:, 4 * g, o:o + P], AbT[:, h, :], X[:, h, :], start=True, stop=True)
                    ins.then_inc(sem("inv_y"), 1)
                for g in range(2):
                    n = (6 * j + l) * 2 + g
                    pe.wait_ge(sem("inv_yc"), n + 1)
                    for h in range(4 * g, 4 * g + 4):
                        o = (h % 4) * P
                        pe.matmul(psum[:, 4 * g + 1, o:o + P], XT[:, h, :], Yb[:, h, :], start=True, stop=True)
                        ins = pe.matmul(psum[:, 4 * g + 2, o:o + P], Yb[:, h, :], XT[:, h, :], start=True, stop=True)
                    ins.then_inc(sem("inv_xy"), 1)
            pe.wait_ge(sem("inv_x"), j + 1)
            for h in range(8):
                ins = pe.matmul(psum[:, 3, h * 64:h * 64 + 64], Q4[:, h, 2, :], Vt[:, h * 64:h * 64 + 64],
                                start=True, stop=True)
            ins.then_inc(sem("rw_gv"), 1)
            for h in range(8):
                pb, c = hd(h)
                ins = pe.matmul(psum[pb:pb + 64, 0, c * P:(c + 1) * P], Pt[:, h * 64:h * 64 + 64], XT[:, h, :],
                                start=True, stop=True)
            pe.wait_ge(sem("rw_gvev"), j + 1)
            for h in range(8):
                ins = pe.matmul(psum[:, 7, yo(h):yo(h) + 64], XT[:, h, :], GVb[:, h * 64:h * 64 + 64],
                                start=True, stop=True)
            ins.then_inc(sem("rw_uw"), 1)
            pe.wait_ge(sem("rw_uwev"), j + 1)
            for cc in range(2):
                n, tb = 2 * j + cc, CH * cc
                if n:
                    pe.wait_ge(sem("seq_m"), n)
                for h in range(8):
                    pb, c = hd(h)
                    ins = pe.matmul(psum[tb:tb + 64, 1 + 5 * (h % 2), c * 64:c * 64 + 64],
                                    WTb[pb:pb + 64, c, tb:tb + 64], Ms[pb:pb + 64, c, :], start=True, stop=True)
                ins.then_inc(sem("seq_y"), 1)
                for h in range(8):
                    pb, c = hd(h)
                    pe.matmul(psum[pb:pb + 64, 2 + h % 2, c * 64:c * 64 + 64], Ms[pb:pb + 64, c, :],
                              PR[pb:pb + 64, c, j, 1, tb:tb + 64], start=True, stop=True)
                pe.wait_ge(sem("seq_yv"), n + 1)
                for h in range(8):
                    pb, c = hd(h)
                    hs, ys = slice(h * 64, h * 64 + 64), slice(yo(h), yo(h) + 64)
                    o = psum[pb:pb + 64, 4, c * 64:c * 64 + 64]
                    pe.matmul(o, Ysb[tb:tb + 64, ys], Q4[tb:tb + 64, h, 1, tb:tb + 64], start=True, stop=False)
                    pe.matmul(o, Vt[tb:tb + 64, hs], Q4[tb:tb + 64, h, 3, tb:tb + 64], start=False, stop=True)
                    o = psum[pb:pb + 64, 5, c * 64:c * 64 + 64]
                    pe.matmul(o, Bt[tb:tb + 64, hs], Ysb[tb:tb + 64, ys], start=True, stop=False)
                    ins = pe.matmul(o, Kt[tb:tb + 64, hs], Vt[tb:tb + 64, hs], start=False, stop=True)
                ins.then_inc(sem("seq_o"), 1)

        def rwkv_tile_act(act, j):
            act.wait_ge(sem("rw_tm"), j + 1)
            if j:
                act.wait_ge(sem("seq_m"), 2)
            for a in range(4):
                ins = act.activation(tm4[a], psum[:, a, :], ACT.Copy)
            ins.then_inc(sem("rw_tmev"), 1)
            for l in range(6):
                for g in range(2):
                    act.wait_ge(sem("inv_y"), (6 * j + l) * 2 + g + 1)
                    act.activation(Yb[:, 4 * g:4 * g + 4, :], psum[:, 4 * g, :].rearrange("p (h t) -> p h t", h=4),
                                   ACT.Copy).then_inc(sem("inv_yc"), 1)
            act.wait_ge(sem("rw_gv"), j + 1)
            act.activation(GVb, psum[:, 3, :], ACT.Copy).then_inc(sem("rw_gvev"), 1)
            act.wait_ge(sem("rw_uw"), j + 1)
            act.activation(WTb, psum[:, 0, :].rearrange("p (c t) -> p c t", c=4), ACT.Copy)
            act.activation(Ub, psum[:, 7, :], ACT.Copy).then_inc(sem("rw_uwev"), 1)

        def rwkv_tile_dve(dve, j):
            def S(ins, name="dve_step"):
                step(dve, ins, name)
            for h in range(8):
                dve.wait_ge(sem("rw_q"), 8 * j + h + 1)
                S(dve.tensor_tensor(Q4[:, h, :, :].rearrange("p m t -> p (m t)"), psum[:, 4 + h % 4, :], cst("mask4"),
                                    MUL), "rw_qev")
            eye = ident.unsqueeze(1).to_broadcast([P, 8, P])
            S(dve.tensor_copy(X, eye))
            S(dve.tensor_copy(XT, eye))
            for l in range(6):
                lv = cst("level")[:, l * P:(l + 1) * P].unsqueeze(1).to_broadcast([P, 4, P])
                for g in range(2):
                    hs = slice(4 * g, 4 * g + 4)
                    S(dve.tensor_tensor(AbT[:, hs, :], Q4[:, hs, 0, :], lv, MUL), "inv_a")
                for g in range(2):
                    hs = slice(4 * g, 4 * g + 4)
                    dve.wait_ge(sem("inv_xy"), (6 * j + l) * 2 + g + 1)
                    for m, t in ((1, X), (2, XT)):
                        S(dve.tensor_tensor(t[:, hs, :], t[:, hs, :],
                                            psum[:, 4 * g + m, :].rearrange("p (h t) -> p h t", h=4), SUB),
                          "inv_x" if (l, g, m) == (5, 1, 2) else "dve_step")
            for cc in range(2):
                n, tb = 2 * j + cc, CH * cc
                rows = slice(tb, tb + CH)
                dve.wait_ge(sem("seq_y"), n + 1)
                for q, bank in enumerate((1, 6)):
                    qs = slice(256 * q, 256 * q + 256)
                    S(dve.scalar_tensor_tensor(Ysb[rows, qs], psum[rows, bank, 0:256], -1.0, Ub[rows, qs], MUL, SUB),
                      "seq_yv" if q else "dve_step")
                dve.wait_ge(sem("seq_o"), n + 1)
                on = oT[:, :, n * CH:(n + 1) * CH]
                S(dve.tensor_copy(on, psum[:, 4, 0:256].rearrange("p (c t) -> p c t", c=4)))
                for q in range(2):
                    hr = slice(64 * q, 64 * q + 64)
                    S(dve.tensor_tensor(on[hr], on[hr], psum[hr, 2 + q, 0:256].rearrange("p (c t) -> p c t", c=4), ADD))
                S(dve.tensor_tensor(Ms, Ms, psum[:, 5, 0:256].rearrange("p (c v) -> p c v", c=4), ADD))
                S(dve.tensor_tensor(Ms, Ms, eC[:, :, n:n + 1].to_broadcast([P, 4, 64]), MUL), "seq_m")

        def rwkv_out_pe(pe):
            pe.wait_ge(sem("seq_m"), 4)
            for b in range(2):
                ins = pe.matmul(psum[:, b, :], cst("headones"), oT[:, 2 * b:2 * b + 2, :].rearrange("p c t -> p (c t)"),
                                start=True, stop=True)
            ins.then_inc(sem("gn_mean"), 1)
            pe.wait_ge(sem("gn_sq"), 1)
            for b in range(2):
                ins = pe.matmul(psum[:, 2 + b, :], cst("headones"),
                                t1[:, 2 * b:2 * b + 2, :].rearrange("p c t -> p (c t)"), start=True, stop=True)
            ins.then_inc(sem("gn_var"), 1)
            pe.wait_ge(sem("e_y"), 1)
            out_proj_pe(pe, FIRST["e_out"], yT, NT)

        def rwkv_out_dve(dve):
            def S(ins, name="dve_step"):
                step(dve, ins, name)
            dve.wait_ge(sem("gn_mean"), 1)
            S(dve.scalar_tensor_tensor(oT, psum[:, 0:2, :].rearrange("p b (c t) -> p (b c) t", c=2), -1.0 / 64, oT,
                                       MUL, ADD))
            S(dve.tensor_tensor(t1, oT, oT, MUL), "gn_sq")
            dve.wait_ge(sem("gn_var"), 1)
            S(dve.tensor_scalar(t2, psum[:, 2:4, :].rearrange("p b (c t) -> p (b c) t", c=2), 1.0 / 64, 64e-5, MUL, ADD),
              "gn_ms")
            dve.wait_ge(sem("gn_std"), 1)
            S(dve.reciprocal(t2, t2))
            S(dve.tensor_tensor(oT, oT, t2, MUL))
            for c in range(4):
                S(dve.tensor_scalar(oT[:, c, :], oT[:, c, :], vec("e_gn_w", c), vec("e_gn_b", c), MUL, ADD))
            S(dve.tensor_tensor(oT, oT, bon, ADD))
            S(dve.tensor_tensor(yT[:, 4:8, :], oT, gg, MUL), "e_y")
            slot_used(dve, FIRST["e_out"] + 2)
            add_tokens(dve, x_tm)

        def rwkv_out_act(act):
            act.wait_ge(sem("gn_ms"), 1)
            act.activation(t2, t2, ACT.Sqrt).then_inc(sem("gn_std"), 1)

        def tm_proj_pe(pe, tag, n0, widths, lhs, tiles, nk=KD, base=0):
            for s, w in enumerate(widths):
                slot_ready(pe, n0 + s)
                if base + s >= 2:
                    pe.wait_ge(sem(f"{tag}_ev"), base + s - 1)
                for j in range(tiles[s]):
                    for k in range(nk):
                        ins = pe.matmul(psum[:, 4 * ((base + s) % 2) + j, 0:w], lhs[:, k, j * P:(j + 1) * P],
                                        slot_of[(n0 + s) % RING][:, k * w:(k + 1) * w],
                                        start=(k == 0), stop=(k == nk - 1))
                ins.then_inc(w_used[(n0 + s) % RING], 1)

        def tm_proj_act(act, tag, n0, widths, dst, tiles):
            at = 0
            for s, w in enumerate(widths):
                slot_used(act, n0 + s)
                b = 4 * (s % 2)
                act.activation(dst[:, 0:tiles[s], at:at + w], psum[:, b:b + tiles[s], 0:w], ACT.Copy)\
                   .then_inc(sem(f"{tag}_ev"), 1)
                at += w

        hn_ss, hn_std = sm("hn_ss", 64), sm("hn_std", 64)

        def head_norm_dve(dve, q, v, sq, groups, width, gain):
            step(dve, dve.tensor_tensor(sq, v, v, MUL), "dve_step")
            step(dve, dve.tensor_reduce(hn_ss[:, 0:groups], sq, AX.X, ADD), "dve_step")
            step(dve, dve.tensor_scalar(hn_ss[:, 0:groups], hn_ss[:, 0:groups], 1.0 / width, 1e-6, MUL, ADD), "hn_ms")
            dve.wait_ge(sem("hn_std"), q + 1)
            step(dve, dve.reciprocal(hn_std[:, 0:groups], hn_std[:, 0:groups]), "dve_step")
            step(dve, dve.tensor_tensor(v, v, hn_std[:, 0:groups].unsqueeze(2).to_broadcast([P, groups, width]), MUL),
                 "dve_step")
            if gain is not None:
                step(dve, dve.tensor_tensor(v, v, gain.unsqueeze(1).to_broadcast([P, groups, width]), MUL), "dve_step")

        def head_norm_act(act, q, groups):
            act.wait_ge(sem("hn_ms"), q + 1)
            act.activation(hn_std[:, 0:groups], hn_ss[:, 0:groups], ACT.Sqrt).then_inc(sem("hn_std"), 1)

        def rope_dve(dve, x1, x2, cos, sin, tmp, shape):
            a, b = tmp
            step(dve, dve.tensor_tensor(a, x1, sin, MUL), "dve_step")
            step(dve, dve.tensor_tensor(b, x2, sin, MUL), "dve_step")
            step(dve, dve.tensor_tensor(x1, x1, cos, MUL), "dve_step")
            step(dve, dve.tensor_tensor(x2, x2, cos, MUL), "dve_step")
            step(dve, dve.tensor_tensor(x1, x1, b, SUB), "dve_step")
            step(dve, dve.tensor_tensor(x2, x2, a, ADD), "dve_step")

        qkv = ar(6144, 6144, "p (j n) -> p j n", j=NT)
        dQT = ar(12288, 2048, "p (c t) -> p c t", c=8)
        dKT = ar(14336, 2048, "p (c t) -> p c t", c=8)
        dS = ar(16384, 2048, "p (g k) -> p g k", g=8)
        dsq = ar(18432, 2048)
        dA = ar(20480, 1024, "p (h k) -> p h k", h=4)
        dAT = ar(21504, 1024, "p (h b q) -> p h b q", h=4, b=2)
        dO = ar(22528, 2048, "p (j n) -> p j n", j=NT)
        pos_i = sb("pos_i", NT, i32)
        rope_c, rope_s = sm("rope_c", 16), sm("rope_s", 16)
        rp_a, rp_k, rp_r = sm("rp_a", 16), sm("rp_k", 16), sm("rp_r", 16)
        posf = sm("posf", 2)
        lam2, nlam = sm("lam2", 2), sm("nlam", 1)
        subg = sm("subg", 128)
        d_mx, d_rs = sm("d_mx", 8), sm("d_rs", 8)
        junk = sm("junk", 64)

        def diff_cols_dve(dve):
            def S(ins, name="dve_step"):
                step(dve, ins, name)
            S(dve.tensor_copy(posf, pos_i[:, :]))
            for j in range(NT):
                S(dve.tensor_scalar(rp_a[:, 8 * j:8 * j + 8], cst("freq"), posf[:, j:j + 1], None, MUL))
            magic = 1.5 * 2.0 ** 23
            S(dve.tensor_scalar(rp_k, rp_a, 1.0 / (2.0 * math.pi), magic, MUL, ADD))
            S(dve.tensor_scalar(rp_k, rp_k, -magic, None, ADD))
            c1 = 6.28125
            c2 = float(np.float32(2.0 * math.pi - c1))
            c3 = 2.0 * math.pi - c1 - c2
            S(dve.scalar_tensor_tensor(rp_r, rp_k, -c1, rp_a, MUL, ADD))
            S(dve.scalar_tensor_tensor(rp_r, rp_k, -c2, rp_r, MUL, ADD))
            S(dve.scalar_tensor_tensor(rp_r, rp_k, -c3, rp_r, MUL, ADD))
            S(dve.tensor_scalar(rp_r, rp_r, 3.1415925, -3.1415925, MIN, MAX))
            S(dve.tensor_scalar(rp_a, rp_r, -1.0, None, MUL))
            S(dve.tensor_tensor(rp_a, rp_a, rp_r, MAX))
            S(dve.tensor_scalar(rp_a, rp_a, -1.0, math.pi / 2, MUL, ADD))
            for n, (a, b) in enumerate((("o_lambda_q1", "o_lambda_k1"), ("o_lambda_q2", "o_lambda_k2"))):
                S(dve.tensor_tensor_reduce(junk, mat(a), mat(b), 1.0, 0.0, MUL, ADD, lam2[:, n:n + 1]),
                  "df_cols" if n else "dve_step")
            S(dve.tensor_scalar(subg, mat("o_subln"), 1.0 - LAMBDA_INIT, None, MUL))
            dve.wait_ge(sem("df_sin"), 1)
            S(dve.tensor_tensor(nlam, lam2[:, 1:2], lam2[:, 0:1], SUB))
            S(dve.tensor_scalar(nlam, nlam, -LAMBDA_INIT, None, ADD))

        def diff_cols_act(act):
            act.wait_ge(sem("df_cols"), 1)
            act.activation(rope_s, rp_r, ACT.Sin)
            act.activation(rope_c, rp_a, ACT.Sin)
            act.activation(lam2, lam2, ACT.Exp).then_inc(sem("df_sin"), 1)

        def diff_dve(dve):
            def S(ins, name="dve_step"):
                step(dve, ins, name)
            diff_cols_dve(dve)
            dve.wait_ge(sem("qkv_ev"), QKV // COLS)
            for j in range(NT):
                v = qkv[:, j, 0:2048].rearrange("p (g d) -> p g d", g=32)
                head_norm_dve(dve, j, v, dsq.rearrange("p (g d) -> p g d", g=32), 32, 64, None)
                for part, name in enumerate(("o_q_norm", "o_k_norm")):
                    w = v[:, 16 * part:16 * part + 16, :]
                    S(dve.tensor_tensor(w, w, mat(name).unsqueeze(1).to_broadcast([P, 16, 64]), MUL))
                cos, sin = [t[:, 8 * j:8 * j + 8].unsqueeze(1).to_broadcast([P, 32, 8]) for t in (rope_c, rope_s)]
                tmp = [dsq[:, 256 * i:256 * i + 256].rearrange("p (g d) -> p g d", g=32) for i in range(2)]
                rope_dve(dve, v[:, :, 0:8], v[:, :, 8:16], cos, sin, tmp, None)
            dve.sem_inc(sem("df_rope"), 1)
            dve.wait_ge(sem("df_tr"), 2)
            S(dve.tensor_copy(dKT, psum[:, 4:8, :].rearrange("p b (c t) -> p (b c) t", c=2)), "k_fm")
            for n in range(4):
                j, half = n // 2, n % 2
                w = P * (j + 1)
                src = psum[:, 0:4, :].rearrange("p b (u k) -> p (b u) k", u=2)
                dve.wait_ge(sem("df_s"), n + 1)
                mask = cst("causal").unsqueeze(1).to_broadcast([P, 8, P])
                S(dve.scalar_tensor_tensor(dS[:, :, w - P:w], src[:, :, w - P:w], 0.125, mask, MUL, ADD))
                if j:
                    S(dve.tensor_scalar(dS[:, :, 0:P], src[:, :, 0:P], 0.125, None, MUL))
                S(dve.tensor_reduce(d_mx, dS[:, :, 0:w], AX.X, MAX))
                S(dve.tensor_scalar(d_mx, d_mx, -1.0, None, MUL), "df_max")
                dve.wait_ge(sem("df_exp"), n + 1)
                S(dve.reciprocal(d_rs, d_rs))
                S(dve.tensor_scalar(d_rs[:, 4:8], d_rs[:, 4:8], nlam[:, 0:1], None, MUL))
                S(dve.tensor_tensor(dS[:, :, 0:w], dS[:, :, 0:w], d_rs.unsqueeze(2).to_broadcast([P, 8, w]), MUL))
                S(dve.tensor_tensor(dA[:, :, 0:w], dS[:, 0:4, 0:w], dS[:, 4:8, 0:w], ADD), "df_attn")
                dve.wait_ge(sem("df_pv"), n + 1)
                S(dve.tensor_copy(dO[:, j, 512 * half:512 * half + 512], psum[:, 6, :]), "df_o")
            v = ar(22528, 2048, "p (g d) -> p g d", g=16)
            head_norm_dve(dve, 2, v, dsq.rearrange("p (g d) -> p g d", g=16), 16, 128, subg)
            dve.sem_inc(sem("df_on"), 1)
            dve.wait_ge(sem("mix_tr"), 1)
            S(dve.tensor_copy(hT[:, :, 0:T], psum[:, 0:4, :].rearrange("p b (c t) -> p (b c) t", c=2)), "df_y")
            slot_used(dve, FIRST["o_out"] + 2)
            add_tokens(dve, x_tm)

        def diff_act(act):
            diff_cols_act(act)
            tm_proj_act(act, "qkv", FIRST["qkv"], [COLS] * (QKV // COLS), qkv, [NT] * (QKV // COLS))
            for j in range(NT):
                head_norm_act(act, j, 32)
            act.wait_ge(sem("df_tr"), 1)
            act.activation(dQT, psum[:, 0:4, :].rearrange("p b (c t) -> p (b c) t", c=2), ACT.Copy)\
               .then_inc(sem("q_fm"), 1)
            for n in range(4):
                w = P * (n // 2 + 1)
                act.wait_ge(sem("df_max"), n + 1)
                for g in range(8):
                    ins = act.activation(dS[:, g, 0:w], dS[:, g, 0:w], ACT.Exp, bias=d_mx[:, g:g + 1],
                                         accum_out=d_rs[:, g:g + 1])
                ins.then_inc(sem("df_exp"), 1)
                act.wait_ge(sem("df_t"), n + 1)
                src = psum[:, 4:6, :].rearrange("p b (h k q) -> p (b h) k q", h=2, k=2)
                nb = n // 2 + 1
                act.activation(dAT[:, :, 0:nb, :], src[:, :, 0:nb, :], ACT.Copy).then_inc(sem("df_tev"), 1)
            head_norm_act(act, 2, 16)

        def diff_pe(pe):
            pe.wait_ge(sem("norm_hT"), 3)
            tm_proj_pe(pe, "qkv", FIRST["qkv"], [COLS] * (QKV // COLS), hT, [NT] * (QKV // COLS))
            pe.wait_ge(sem("df_rope"), 1)
            for part in range(2):
                for c in range(8):
                    for j in range(NT):
                        at = (c % 2) * T + j * P
                        ins = pe.transpose(psum[:, 4 * part + c // 2, at:at + P],
                                           qkv[:, j, part * D + c * P:part * D + (c + 1) * P], ident)
                ins.then_inc(sem("df_tr"), 1)
            pe.wait_ge(sem("q_fm"), 1)
            pe.wait_ge(sem("k_fm"), 1)
            for n in range(4):
                j, half = n // 2, n % 2
                if n:
                    pe.wait_ge(sem("df_o"), n)
                for part in range(2):
                    for hl in range(4):
                        h, pb = 4 * half + hl, 64 * part
                        at = (hl % 2) * T
                        ins = pe.matmul(psum[:, 2 * part + hl // 2, at:at + P * (j + 1)],
                                        dQT[pb:pb + 64, h, j * P:(j + 1) * P], dKT[pb:pb + 64, h, 0:P * (j + 1)],
                                        start=True, stop=True)
                ins.then_inc(sem("df_s"), 1)
                pe.wait_ge(sem("df_attn"), n + 1)
                for hl in range(4):
                    for b in range(j + 1):
                        at = (hl % 2) * T + b * P
                        ins = pe.transpose(psum[:, 4 + hl // 2, at:at + P], dA[:, hl, b * P:(b + 1) * P], ident)
                ins.then_inc(sem("df_t"), 1)
                pe.wait_ge(sem("df_tev"), n + 1)
                for hl in range(4):
                    h = 4 * half + hl
                    for b in range(j + 1):
                        ins = pe.matmul(psum[:, 6, hl * P:(hl + 1) * P], dAT[:, hl, b, :],
                                        qkv[:, b, 2 * D + h * P:2 * D + (h + 1) * P], start=(b == 0), stop=(b == j))
                ins.then_inc(sem("df_pv"), 1)
            pe.wait_ge(sem("df_on"), 1)
            for c in range(8):
                for j in range(NT):
                    at = (c % 2) * T + j * P
                    ins = pe.transpose(psum[:, c // 2, at:at + P], dO[:, j, c * P:(c + 1) * P], ident)
            ins.then_inc(sem("mix_tr"), 1)
            pe.wait_ge(sem("df_y"), 1)
            out_proj_pe(pe, FIRST["o_out"], hT, NT)

        logit = sm("logit", 16)
        top = sm("top", 16)
        topf = sm("topf", 4)
        gts = sm("gts", 4)
        oneh = sm("oneh", 8)
        over, rank = sm("over", 8), sm("rank", 8)
        topi = sb("topi", 16, u32)
        plan_i = ar(9888, 16).bitcast(i32)
        plan_f = sm("plan_f", 16)
        xe = ar(6144, KD * CAP, "p (k s) -> p k s", k=KD)
        pick = ar(7168, NT * CAP, "p (j s) -> p j s", j=NT)
        give = ar(7424, NT * CAP, "p (j s) -> p j s", j=NT)
        giveT = ar(7680, NT * CAP, "p (j t) -> p j t", j=NT)
        oute = ar(7936, D)
        before = ar(8960, P)
        NV = MAX_VISITS + 1
        sel, pos, wgt = [ar(9088 + 16 * i, 16, "p (e j) -> p e j", j=NT) for i in range(3)]
        vsel, vpos, vwgt = [ar(9152 + 2 * NV * i, 2 * NV) for i in range(3)]
        me, mh = ar(9344, 2 * CAP, "p (b t) -> p b t", b=2), ar(9600, 2 * CAP, "p (b t) -> p b t", b=2)
        tot = ar(9856, 8)
        pick_tmp = ar(9872, 16)

        def moe_count(eng):
            eng.wait_ge(sem("moe_plan"), 1)
            return eng.value_load(plan_i[0:1, 0:1], min_val=N_EXP, max_val=MAX_VISITS)

        def moe_gather_pe(pe, v):
            pe.wait_ge(sem("moe_pick"), v + 1)
            for half in range(2):
                for c in range(4):
                    k = 4 * half + c
                    for j in range(NT):
                        ins = pe.matmul(psum[:, 6 + half, c * CAP:(c + 1) * CAP], xn[:, j, k * P:(k + 1) * P],
                                        pick[:, j, :], start=(j == 0), stop=(j == NT - 1))
                ins.then_inc(sem("moe_gather"), 1)

        def moe_gate_up_pe(pe, i, r, blk, turn):
            pe.wait_ge(e_ready[r], turn * 16 + 16)
            if not (isinstance(i, int) and i < 2):
                pe.wait_ge(sem("moe_h"), blk - 1)
            w = slot_of[r]
            for part in range(2):
                for k in range(KD):
                    ins = pe.matmul(psum[:, 6 + r % 2, part * CAP:part * CAP + CAP],
                                    w[:, part * D + k * P:part * D + (k + 1) * P], xe[:, k, :],
                                    start=(k == 0), stop=(k == KD - 1))
            if i == 0:
                for j in range(NT):
                    ins = pe.transpose(psum[:, 6, (2 + j) * P:(3 + j) * P], give[:, j, :], ident)
            ins.then_inc(sem("moe_gu"), 1)

        def moe_down_pe(pe, r, blk, first, last):
            pe.wait_ge(sem("moe_h"), blk + 1)
            w = slot_of[r]
            for hf in range(2):
                ins = pe.matmul(psum[:, 4 + hf, :], mh[:, r % 2, :], w[:, 2 * D + hf * 512:2 * D + (hf + 1) * 512],
                                start=first, stop=last)
            ins.then_inc(e_used[r], 1)

        def moe_pe(pe):
            pe.wait_ge(sem("norm_hT"), 4)
            for j in range(NT):
                for k in range(KD):
                    ins = pe.matmul(psum[:, 6, 8 * j:8 * j + 8], hT[:, k, j * P:(j + 1) * P],
                                    mat("router")[:, 8 * k:8 * k + 8], start=(k == 0), stop=(k == KD - 1))
            ins.then_inc(sem("moe_logits"), 1)
            pe.wait_ge(sem("moe_sel"), 1)
            for j in range(NT):
                for hf in range(2):
                    pe.matmul(psum[:, 2 * j + hf, :], giveT[:, 0, :], x_tm[:, j, hf * 512:(hf + 1) * 512],
                              start=True, stop=False)
            pe.matmul(psum[:, 7, 0:8], before, sel[:, :, 0], start=True, stop=True)
            pe.matmul(psum[:, 7, 8:16], cst("ones"), sel[:, :, 0], start=True, stop=False)
            pe.matmul(psum[:, 7, 8:16], before, sel[:, :, 1], start=False, stop=True)
            for j in range(NT):
                ins = pe.matmul(psum[:, 7, 16:24], cst("ones"), sel[:, :, j], start=(j == 0), stop=(j == NT - 1))
            ins.then_inc(sem("moe_pos"), 1)
            n_visits = moe_count(pe)
            moe_gather_pe(pe, 0)
            with pe.Fori(0, n_visits) as v:
                b0, t0 = v * NB_EXP, v * G_EXP
                pe.wait_ge(sem("moe_xe_act"), v + 1)
                pe.wait_ge(sem("moe_xe_dve"), v + 1)
                moe_gate_up_pe(pe, 0, 0, b0, t0)
                moe_gate_up_pe(pe, 1, 1, b0 + 1, t0)
                moe_down_pe(pe, 0, b0, True, False)
                for i in range(2, RING):
                    moe_gate_up_pe(pe, i, i, b0 + i, t0)
                    moe_down_pe(pe, i - 1, b0 + (i - 1), False, False)
                with pe.Fori(1, G_EXP) as g:
                    for u in range(RING):
                        blk = v * NB_EXP + g * RING + u
                        moe_gate_up_pe(pe, None, u, blk, v * G_EXP + g)
                        moe_down_pe(pe, (u - 1) % RING, blk - 1, False, False)
                moe_down_pe(pe, RING - 1, v * NB_EXP + (NB_EXP - 1), False, True)
                moe_gather_pe(pe, v + 1)
                pe.wait_ge(sem("moe_out_act"), v + 1)
                pe.wait_ge(sem("moe_out_dve"), v + 1)
                for j in range(NT):
                    for hf in range(2):
                        pe.matmul(psum[:, 2 * j + hf, :], giveT[:, j, :], oute[:, hf * 512:(hf + 1) * 512],
                                  start=False, stop=False)
            for j in range(NT):
                for hf in range(2):
                    ins = pe.matmul(psum[:, 2 * j + hf, :], ident, x_tm[:, j, hf * 512:(hf + 1) * 512],
                                    start=False, stop=True)
            ins.then_inc(sem("moe_sum"), 1)

        def moe_block_act(act, i, r, blk):
            act.wait_ge(sem("moe_gu"), blk + 1)
            if not (isinstance(i, int) and i < 2):
                act.wait_ge(sem("moe_h"), blk - 1)
            act.activation(me[:, r % 2, :], psum[:, 6 + r % 2, 0:CAP], ACT.Silu).then_inc(sem("moe_silu"), 1)

        def moe_xe_act(act, v):
            act.wait_ge(sem("moe_gather"), 2 * v + 2)
            for c in range(4):
                ins = act.activation(xe[:, 4 + c, :], psum[:, 7, c * CAP:(c + 1) * CAP], ACT.Copy,
                                     scale=vec("o_ln_ffn", 4 + c))
            ins.then_inc(sem("moe_xe_act"), 1)

        def moe_act(act):
            act.wait_ge(sem("moe_top"), 1)
            act.activation(gts[:, 0:2], gts[:, 2:4], ACT.Exp).then_inc(sem("moe_exp"), 1)
            n_visits = moe_count(act)
            moe_xe_act(act, 0)
            with act.Fori(0, n_visits) as v:
                for i in range(RING):
                    moe_block_act(act, i, i, v * NB_EXP + i)
                with act.Fori(1, G_EXP) as g:
                    for u in range(RING):
                        moe_block_act(act, None, u, v * NB_EXP + g * RING + u)
                act.wait_ge(e_used[RING - 1], v * G_EXP + G_EXP)
                act.activation(oute[:, 0:512], psum[:, 4, :], ACT.Copy).then_inc(sem("moe_out_act"), 1)
                moe_xe_act(act, v + 1)

        def moe_pick_dve(dve, v):
            for j in range(NT):
                at = bass.ds(v * NT + j, 1) if not isinstance(v, int) else slice(v * NT + j, v * NT + j + 1)
                dve.tensor_scalar(give[:, j, :], cst("iota"), vpos[:, at], vwgt[:, at], ALU.is_equal, MUL)
                ins = dve.tensor_scalar(pick[:, j, :], cst("iota"), vpos[:, at], vsel[:, at], ALU.is_equal, MUL)
            ins.then_inc(sem("moe_pick"), 1)

        def moe_xe_dve(dve, v):
            dve.wait_ge(sem("moe_gather"), 2 * v + 1)
            for c in range(4):
                ins = dve.tensor_scalar(xe[:, c, :], psum[:, 6, c * CAP:(c + 1) * CAP], vec("o_ln_ffn", c), None, MUL)
            ins.then_inc(sem("moe_xe_dve"), 1)

        def moe_block_dve(dve, i, r, blk, turn):
            dve.wait_ge(sem("moe_silu"), blk + 1)
            if turn is not None:
                dve.wait_ge(e_used[(r - 2) % RING], turn + 1)
            if i == 0:
                dve.tensor_copy(giveT, psum[:, 6, NT * P:2 * NT * P].rearrange("p (j t) -> p j t", j=NT))
            dve.tensor_tensor(mh[:, r % 2, :], me[:, r % 2, :], psum[:, 6 + r % 2, CAP:2 * CAP], MUL)\
               .then_inc(sem("moe_h"), 1)

        def moe_plan_dve(dve):
            def S(ins, name="dve_step"):
                step(dve, ins, name)
            iota8 = cst("iota")[:, 0:N_EXP]
            S(dve.tensor_scalar(before, cst("causal"), 0.0, None, ALU.is_lt))
            S(dve.memset(giveT[:, 0, :], 0.0))
            dve.wait_ge(sem("moe_logits"), 1)
            S(dve.tensor_copy(logit, psum[:, 6, 0:16]))
            for j in range(NT):
                S(dve.max(top[:, 8 * j:8 * j + 8], logit[:, 8 * j:8 * j + 8]))
                S(dve.max_index(topi[:, 8 * j:8 * j + 8], top[:, 8 * j:8 * j + 8], logit[:, 8 * j:8 * j + 8]))
                S(dve.tensor_copy(topf[:, 2 * j:2 * j + 2], topi[:, 8 * j:8 * j + 2]))
                S(dve.tensor_tensor(gts[:, 2 + j:3 + j], top[:, 8 * j + 1:8 * j + 2], top[:, 8 * j:8 * j + 1], SUB),
                  "moe_top" if j else "dve_step")
            for j in range(NT):
                S(dve.tensor_scalar(oneh, iota8, topf[:, 2 * j:2 * j + 1], None, ALU.is_equal))
                S(dve.scalar_tensor_tensor(sel[:, :, j], iota8, topf[:, 2 * j + 1:2 * j + 2], oneh, ALU.is_equal, MAX),
                  "moe_sel" if j else "dve_step")
            dve.wait_ge(sem("moe_exp"), 1)
            S(dve.tensor_scalar(gts[:, 2:4], gts[:, 0:2], 1.0, None, ADD))
            S(dve.reciprocal(gts[:, 2:4], gts[:, 2:4]))
            S(dve.tensor_tensor(gts[:, 0:2], gts[:, 0:2], gts[:, 2:4], MUL))
            for j in range(NT):
                S(dve.tensor_scalar(oneh, iota8, topf[:, 2 * j + 1:2 * j + 2], gts[:, j:j + 1], ALU.is_equal, MUL))
                S(dve.tensor_scalar(wgt[:, :, j], iota8, topf[:, 2 * j:2 * j + 1], gts[:, 2 + j:3 + j],
                                    ALU.is_equal, MUL))
                S(dve.tensor_tensor(wgt[:, :, j], wgt[:, :, j], oneh, ADD))
            dve.wait_ge(sem("moe_pos"), 1)
            for j in range(NT):
                S(dve.tensor_copy(pos[:, :, j], psum[:, 7, 8 * j:8 * j + 8]))
            S(dve.tensor_scalar(over, psum[:, 7, 16:24], float(CAP), None, ALU.is_gt))
            S(dve.memset(rank[:, 0:1], 0.0))
            for e in range(1, N_EXP):
                S(dve.tensor_tensor(rank[:, e:e + 1], rank[:, e - 1:e], over[:, e - 1:e], ADD))
            S(dve.tensor_tensor(plan_f[:, 0:1], rank[:, 7:8], over[:, 7:8], ADD))
            S(dve.tensor_scalar(plan_f[:, 0:1], plan_f[:, 0:1], float(N_EXP), None, ADD))
            for dst, src in ((vsel, sel), (vpos, pos), (vwgt, wgt)):
                S(dve.memset(dst[:, 2 * N_EXP:2 * NV], 0.0))
                S(dve.tensor_copy(dst[:, 0:2 * N_EXP], src.rearrange("p e j -> p (e j)")))
            S(dve.tensor_copy(plan_f[:, 1:9], iota8))
            for n in range(MAX_VISITS - N_EXP):
                S(dve.scalar_tensor_tensor(oneh, rank, float(n), over, ALU.is_equal, MUL))
                S(dve.tensor_tensor_reduce(pick_tmp[:, 0:8], oneh, iota8, 1.0, 0.0, MUL, ADD,
                                           plan_f[:, 9 + n:10 + n]))
                for dst, src in ((vsel, sel), (vpos, pos), (vwgt, wgt)):
                    for j in range(NT):
                        o = 2 * (N_EXP + n) + j
                        S(dve.tensor_tensor_reduce(pick_tmp[:, 0:8], oneh, src[:, :, j], 1.0, 0.0, MUL, ADD,
                                                   dst[:, o:o + 1]))
            S(dve.tensor_scalar(vpos[:, 2 * N_EXP:2 * MAX_VISITS], vpos[:, 2 * N_EXP:2 * MAX_VISITS], -float(CAP), None,
                                ADD))
            S(dve.tensor_copy(plan_i[:, 0:12], plan_f[:, 0:12]), "moe_plan")

        def moe_dve(dve):
            moe_plan_dve(dve)
            n_visits = moe_count(dve)
            moe_pick_dve(dve, 0)
            moe_xe_dve(dve, 0)
            with dve.Fori(0, n_visits) as v:
                for i in range(RING):
                    moe_block_dve(dve, i, i, v * NB_EXP + i, v * G_EXP if i >= 2 else None)
                moe_pick_dve(dve, v + 1)
                with dve.Fori(1, G_EXP) as g:
                    for u in range(RING):
                        turn = v * G_EXP + g
                        moe_block_dve(dve, None, u, v * NB_EXP + g * RING + u, turn - 1 if u < 2 else turn)
                dve.wait_ge(e_used[RING - 1], v * G_EXP + G_EXP)
                dve.tensor_copy(oute[:, 512:1024], psum[:, 5, :]).then_inc(sem("moe_out_dve"), 1)
                moe_xe_dve(dve, v + 1)
            dve.wait_ge(sem("moe_sum"), 1)
            for j in range(NT):
                step(dve, dve.tensor_copy(x_tm[:, j, :], psum[:, 2 * j:2 * j + 2, :].rearrange("p b n -> p (b n)")),
                     "dve_step")

        def spread_dve(dve, q, layer, idx, cond, dst, diag):
            d3 = diag.rearrange("p (c n) -> p c n", c=8)
            for c in range(8):
                ins = dve.tensor_scalar(d3[:, c, :], ident, mod[layer][:, 8 * idx + c, cond:cond + 1], None, MUL)
            step(dve, ins, "spread_diag")
            dve.wait_ge(sem("spread_ps"), q + 1)
            step(dve, dve.tensor_copy(dst, psum[:, 6:8, :].rearrange("p b n -> p (b n)")), "spread_ev")

        def spread_pe(pe, q, diag):
            pe.wait_ge(sem("spread_diag"), q + 1)
            for b in range(2):
                ins = pe.matmul(psum[:, 6 + b, :], cst("ones"), diag[:, 512 * b:512 * b + 512], start=True, stop=True)
            ins.then_inc(sem("spread_ps"), 1)

        at_mx, at_rs, at_rc = sm("at_mx", 4), sm("at_rs", 8), sm("at_rc", 4)
        at_n = {"pe": 0, "act": 0, "dve": 0}

        def attn_pe(pe, rounds, probs, pT):
            r0 = at_n["pe"]
            at_n["pe"] += len(rounds)

            def scores(n):
                rd = rounds[n]
                for i in range(4):
                    ins = pe.matmul(psum[:, i, 0:rd["keys"]], rd["q"][i], rd["k"][i], start=True, stop=True)
                ins.then_inc(sem("at_s"), 1)

            scores(0)
            for n, rd in enumerate(rounds):
                nb = rd["keys"] // P
                pe.wait_ge(sem("at_exp"), r0 + n + 1)
                if r0 + n:
                    pe.wait_ge(sem("at_o"), r0 + n)
                for i in range(4):
                    for b in range(nb):
                        ins = pe.transpose(psum[:, 4 + i, b * P:(b + 1) * P], probs[:, i, b * P:(b + 1) * P], ident)
                ins.then_inc(sem("at_t"), 1)
                if n + 1 < len(rounds):
                    scores(n + 1)
                pe.wait_ge(sem("at_teva"), r0 + n + 1)
                pe.wait_ge(sem("at_tevb"), r0 + n + 1)
                for i in range(4):
                    for b in range(nb):
                        ins = pe.matmul(psum[:, 4, 64 * i:64 * i + 64], pT[:, i, b, :], rd["v"][i][b],
                                        start=(b == 0), stop=(b == nb - 1))
                ins.then_inc(sem("at_pv"), 1)

        def attn_act(act, rounds, probs, pT, scale):
            r0 = at_n["act"]
            at_n["act"] += len(rounds)

            def exps(n):
                rd = rounds[n]
                act.wait_ge(sem("at_max"), r0 + n + 1)
                for i in range(4):
                    src = probs[:, i, 0:rd["keys"]] if rd["bias"] is not None else psum[:, i, 0:rd["keys"]]
                    o = 4 * ((r0 + n) % 2) + i
                    ins = act.activation(probs[:, i, 0:rd["keys"]], src, ACT.Exp, bias=at_mx[:, i:i + 1],
                                         scale=1.0 if rd["bias"] is not None else scale, accum_out=at_rs[:, o:o + 1])
                ins.then_inc(sem("at_exp"), 1)

            exps(0)
            for n, rd in enumerate(rounds):
                nb = rd["keys"] // P
                act.wait_ge(sem("at_t"), r0 + n + 1)
                act.activation(pT[:, 0:2, 0:nb, :], psum[:, 4:6, 0:rd["keys"]].rearrange("p i (b q) -> p i b q", q=P),
                               ACT.Copy).then_inc(sem("at_teva"), 1)
                if n + 1 < len(rounds):
                    exps(n + 1)

        def attn_dve(dve, rounds, probs, pT, scale):
            r0 = at_n["dve"]
            at_n["dve"] += len(rounds)

            def S(ins, name="dve_step"):
                step(dve, ins, name)

            def maxima(n):
                rd = rounds[n]
                dve.wait_ge(sem("at_s"), r0 + n + 1)
                src = psum[:, 0:4, 0:rd["keys"]]
                if rd["bias"] is not None:
                    S(dve.scalar_tensor_tensor(probs[:, :, 0:T], src[:, :, 0:T], scale, rd["bias"], MUL, ADD))
                    S(dve.tensor_scalar(probs[:, :, T:2 * T], src[:, :, T:2 * T], scale, None, MUL))
                    src = probs[:, :, 0:rd["keys"]]
                S(dve.tensor_reduce(at_mx, src, AX.X, MAX))
                S(dve.tensor_scalar(at_mx, at_mx, -1.0 if rd["bias"] is not None else -scale, None, MUL), "at_max")

            maxima(0)
            for n, rd in enumerate(rounds):
                nb = rd["keys"] // P
                dve.wait_ge(sem("at_t"), r0 + n + 1)
                S(dve.tensor_copy(pT[:, 2:4, 0:nb, :],
                                  psum[:, 6:8, 0:rd["keys"]].rearrange("p i (b q) -> p i b q", q=P)), "at_tevb")
                o = 4 * ((r0 + n) % 2)
                S(dve.reciprocal(at_rc, at_rs[:, o:o + 4]))
                if n + 1 < len(rounds):
                    maxima(n + 1)
                dve.wait_ge(sem("at_pv"), r0 + n + 1)
                for i in range(4):
                    S(dve.tensor_scalar(rd["o"][i], psum[:, 4, 64 * i:64 * i + 64], at_rc[:, i:i + 1], None, MUL),
                      "at_o" if i == 3 else "dve_step")

        g_in = ar(6144, 6144, "p (j n) -> p j n", j=4)
        gQT = ar(12288, 3072, "p (c t) -> p c t", c=6)
        gKT = ar(15360, 1024, "p (c t) -> p c t", c=2)
        mixT = ar(16384, 4096, "p (c t) -> p c t", c=8)
        g_probs = ar(20480, 2048, "p (i k) -> p i k", i=4)
        g_pT = ar(22528, 2048, "p (i b q) -> p i b q", i=4, b=4)
        gO = ar(24576, 3072, "p (j n) -> p j n", j=4)
        band = ar(27648, 2048, "p (g i t) -> p g i t", g=4, i=2)
        dT = ar(5120, 1024, "p (m c t) -> p m c t", m=2, c=2)
        g_scr = ar(0, 2048)
        gB = [ar(2048, 1024), ar(3072, 1024)]
        gdiag = ar(4096, 1024)
        gtmp = ar(0, 1024)

        def l0_rounds():
            out = []
            for j in range(4):
                keys = 4 * P if j < 2 else 2 * P
                k0 = 4 * P - keys
                for q in range(3):
                    ns = range(4 * q, 4 * q + 4)
                    hs = [HEADS0[n] for n in ns]
                    out.append({"keys": keys, "bias": None,
                                "q": [gQT[64 * (n % 2):64 * (n % 2) + 64, n // 2, j * P:(j + 1) * P] for n in ns],
                                "k": [gKT[64 * (h // 3 % 2):64 * (h // 3 % 2) + 64, h // 6, k0:4 * P] for h in hs],
                                "v": [[g_in[:, b, 1280 + 64 * (h // 3):1344 + 64 * (h // 3)]
                                       for b in range(k0 // P, 4)] for h in hs],
                                "o": [gO[:, j, 64 * h:64 * h + 64] for h in hs]})
            return out

        def l0_pe(pe):
            n0 = FIRST["l0_in"]
            pe.wait_ge(sem("norm_hT"), 6)
            tm_proj_pe(pe, "l0", n0, [COLS] * 4, hT, [4] * 4)
            pe.wait_ge(sem("l0_ev"), 4)
            pe.wait_ge(sem("band_in"), 16)
            for m in range(2):
                for g in range(4):
                    pb = 64 * (g % 2)
                    for i in range(NT):
                        ins = pe.matmul(psum[pb:pb + 64, m, (g // 2) * T:(g // 2) * T + T],
                                        g_in[:, 2 * m + i, 64 * g:64 * g + 64], band[:, g, i, :],
                                        start=(i == 0), stop=(i == NT - 1))
            ins.then_inc(sem("pool_d"), 1)
            pe.wait_ge(sem("pool_dev"), 1)
            for m in range(2):
                for c in range(2):
                    ins = pe.matmul(psum[:, 2 + m, c * T:c * T + T], mat("pool_w")[:, c * P:(c + 1) * P], dT[:, m, c, :],
                                    start=True, stop=True)
            ins.then_inc(sem("pool_y"), 1)
            pe.wait_ge(sem("pool_yev"), 1)
            for j in range(4):
                pe.wait_ge(sem("l0_heads"), j + 1)
                for c in range(8):
                    ins = pe.transpose(psum[:, c, j * P:(j + 1) * P], g_in[:, j, T + c * P:T + (c + 1) * P], ident)
            ins.then_inc(sem("l0_tr"), 1)
            pe.wait_ge(sem("q_fm"), 2)
            pe.wait_ge(sem("k_fm"), 2)
            attn_pe(pe, l0_rounds(), g_probs, g_pT)
            pe.wait_ge(sem("at_o"), at_n["pe"])
            for c in range(6):
                for j in range(4):
                    ins = pe.transpose(psum[:, c, j * P:(j + 1) * P], gO[:, j, c * P:(c + 1) * P], ident)
            ins.then_inc(sem("mix_tr"), 1)
            spread_pe(pe, 0, gdiag)
            pe.wait_ge(sem("spread_ev"), 1)
            spread_pe(pe, 1, gdiag)
            pe.wait_ge(sem("spread_ev"), 2)
            pe.wait_ge(sem("mix_y"), 1)
            out_proj_pe(pe, FIRST["l0_out"], mixT, 4)

        def l0_act(act):
            tm_proj_act(act, "l0", FIRST["l0_in"], [COLS] * 4, g_in, [4] * 4)
            act.wait_ge(sem("pool_d"), 1)
            act.activation(dT.rearrange("p m c t -> p m (c t)"), psum[:, 0:2, :], ACT.Copy).then_inc(sem("pool_dev"), 1)
            for j in range(4):
                head_norm_act(act, 3 + j, 16)
            act.wait_ge(sem("l0_tr"), 1)
            act.activation(gQT, psum[:, 0:6, :], ACT.Copy).then_inc(sem("q_fm"), 1)
            attn_act(act, l0_rounds(), g_probs, g_pT, 0.125)
            act.wait_ge(sem("mix_tr"), 2)
            act.activation(mixT[:, 2:8, :], psum[:, 0:6, :], ACT.Copy).then_inc(sem("mix_y"), 1)

        def l0_dve(dve):
            def S(ins, name="dve_step"):
                step(dve, ins, name)
            dve.wait_ge(sem("pool_y"), 1)
            for m in range(2):
                for c in range(2):
                    S(dve.tensor_scalar(mixT[:, c, m * T:m * T + T], psum[:, 2 + m, c * T:c * T + T],
                                        vec("l0_pool_scale_2", c), None, MUL), "pool_yev" if m * c else "dve_step")
            for j in range(4):
                v = g_in[:, j, T:T + 1024].rearrange("p (g d) -> p g d", g=16)
                head_norm_dve(dve, 3 + j, v, g_scr[:, 0:1024].rearrange("p (g d) -> p g d", g=16), 16, 64, None)
                for a, b, name in ((0, 12, "l0_q_gain_2"), (12, 16, "l0_k_gain_2")):
                    S(dve.tensor_tensor(v[:, a:b, :], v[:, a:b, :],
                                        mat(name).unsqueeze(1).to_broadcast([P, b - a, 64]), MUL))
                if j < 2:
                    axial_dve(dve, v, 16, 64, "rope64", j, 16, g_scr[:, 1024:2048])
                dve.sem_inc(sem("l0_heads"), 1)
            dve.wait_ge(sem("l0_tr"), 1)
            S(dve.tensor_copy(gKT, psum[:, 6:8, :]), "k_fm")
            attn_dve(dve, l0_rounds(), g_probs, g_pT, 0.125)
            for cond in range(2):
                spread_dve(dve, cond, 0, 2, cond, gB[cond], gdiag)
            for m, dst in enumerate((x_tm, xc_tm)):
                slot_used(dve, FIRST["l0_out"] + 2)
                for j in range(NT):
                    S(dve.tensor_tensor(gtmp, psum[:, 4 * m + 2 * j:4 * m + 2 * j + 2, :].rearrange("p b n -> p (b n)"),
                                        gB[m], MUL))
                    S(dve.tensor_tensor(dst[:, j, :], dst[:, j, :], gtmp, ADD))

        def axial_dve(dve, v, groups, width, name, j, half, scratch):
            tab = cst(name)[:, j * 4 * half:(j + 1) * 4 * half].rearrange("p (f a d) -> p f a d", f=2, a=2)
            w = v[:, :, width - 4 * half:width].rearrange("p g (a s d) -> p g a s d", a=2, s=2)
            n = groups * half
            for a in range(2):
                cos, sin = [tab[:, f, a, :].unsqueeze(1).to_broadcast([P, groups, half]) for f in range(2)]
                tmp = [scratch[:, i * n:(i + 1) * n].rearrange("p (g d) -> p g d", g=groups) for i in range(2)]
                rope_dve(dve, w[:, :, a, 0, :], w[:, :, a, 1, :], cos, sin, tmp, None)

        fB, fdiag, ftmp = ar(8192, 1024), ar(9216, 1024), ar(10240, 1024)

        def gated_ffn_pe(pe, q, k, name):
            spread_pe(pe, q, fdiag)
            pe.wait_ge(sem("norm_hT"), k + 1)
            pe.wait_ge(sem("spread_ev"), q + 1)
            ffn_pe(pe, FIRST[name], B0[name], NB_FFN, 0)

        def gated_ffn_dve(dve, q, k, layer, cond, dst, name):
            norm_dve(dve, k, dst, lambda c: ge(layer, 1, cond, c), lambda c: mod[layer][:, 24 + c, cond:cond + 1], 0)
            spread_dve(dve, q, layer, 5, cond, fB, fdiag)
            ffn_dve(dve, FIRST[name], B0[name], NB_FFN)
            slot_used(dve, FIRST[name] + NB_FFN - 1)
            add_tokens(dve, dst, fB, ftmp)

        W_L1 = [COLS] * (L1_IN // COLS) + [L1_IN % COLS]
        TILES_L1 = [2, 2, 4, 4, 4, 4]
        C_CQ, C_NQ, C_CKV, C_KR, C_NK, C_NV = 0, 384, 896, 1152, 1184, 1696
        m_in = ar(6144, 4 * L1_IN, "p (j n) -> p j n", j=4)
        cqT = ar(14976, 768, "p (c t) -> p c t", c=3)
        ckvT = ar(15744, 1024, "p (c t) -> p c t", c=2)
        mkv = ar(16768, 4096, "p (j n) -> p j n", j=4)
        mk = ar(20864, 3072, "p (j n) -> p j n", j=4)
        mkT = ar(23936, 4096, "p (h t) -> p h t", h=8)
        mqT = ar(0, 2048, "p (h t) -> p h t", h=8)
        mq = ar(2048, 1536, "p (j n) -> p j n", j=NT)
        m_scr = ar(4096, 2048)
        mO = ar(2048, 2048, "p (j n) -> p j n", j=NT)
        m_probs = ar(20864, 2048, "p (i k) -> p i k", i=4)
        m_pT = ar(4096, 2048, "p (i b q) -> p i b q", i=4, b=4)
        bias = ar(16768, 4096, "p (j h k) -> p j h k", j=NT, h=8)
        nqT = ar(23936, 1024, "p (c t) -> p c t", c=4)
        nkT = ar(24960, 2048, "p (c t) -> p c t", c=4)
        m_mixT = ar(6144, 2048, "p (c t) -> p c t", c=8)

        def mla_rounds():
            return [{"keys": 4 * P, "bias": None,
                     "q": [mqT[0:96, h, j * P:(j + 1) * P] for h in range(4 * q, 4 * q + 4)],
                     "k": [mkT[0:96, h, :] for h in range(4 * q, 4 * q + 4)],
                     "v": [[mkv[:, b, 128 * h + 64:128 * h + 128] for b in range(4)] for h in range(4 * q, 4 * q + 4)],
                     "o": [mO[:, j, 64 * h:64 * h + 64] for h in range(4 * q, 4 * q + 4)]}
                    for j in range(NT) for q in range(2)]

        def na_rounds():
            def rows(h):
                return slice(64 * (h % 2), 64 * (h % 2) + 64)
            return [{"keys": 4 * P, "bias": bias[:, j, 4 * q:4 * q + 4, :],
                     "q": [nqT[rows(h), h // 2, j * P:(j + 1) * P] for h in range(4 * q, 4 * q + 4)],
                     "k": [nkT[rows(h), h // 2, :] for h in range(4 * q, 4 * q + 4)],
                     "v": [[m_in[:, b, C_NV + 64 * h:C_NV + 64 * h + 64] for b in range(4)]
                           for h in range(4 * q, 4 * q + 4)],
                     "o": [mO[:, j, 512 + 64 * h:576 + 64 * h] for h in range(4 * q, 4 * q + 4)]}
                    for j in range(NT) for q in range(2)]

        def l1_pe(pe):
            pe.wait_ge(sem("norm_hT"), 10)
            tm_proj_pe(pe, "l1", FIRST["l1_in"], W_L1, hT, TILES_L1)
            pe.wait_ge(sem("l1_ev"), len(W_L1))
            pe.wait_ge(sem("l1_low"), 1)
            for c in range(3):
                for j in range(NT):
                    at = (c % 2) * T + j * P
                    pe.transpose(psum[:, c // 2, at:at + P], m_in[:, j, C_CQ + c * P:C_CQ + (c + 1) * P], ident)
            for c in range(2):
                for j in range(4):
                    ins = pe.transpose(psum[:, 2 + c, j * P:(j + 1) * P],
                                       m_in[:, j, C_CKV + c * P:C_CKV + (c + 1) * P], ident)
            ins.then_inc(sem("l1_ltr"), 1)
            pe.wait_ge(sem("l1_lowT"), 1)
            n = FIRST["l1_uq"]
            slot_ready(pe, n)
            for j in range(NT):
                for hf in range(2):
                    for k in range(3):
                        o = k * 768 + hf * COLS
                        ins = pe.matmul(psum[:, 4 + 2 * j + hf, 0:COLS], cqT[:, k, j * P:(j + 1) * P],
                                        slot_of[n % RING][:, o:o + COLS], start=(k == 0), stop=(k == 2))
            ins.then_inc(w_used[n % RING], 1)
            n = FIRST["l1_ukv"]
            slot_ready(pe, n)
            pe.wait_ge(sem("l1_qev"), 1)
            for j in range(4):
                for hf in range(2):
                    for k in range(2):
                        o = k * D + hf * 512
                        ins = pe.matmul(psum[:, 2 * j + hf, :], ckvT[:, k, j * P:(j + 1) * P],
                                        slot_of[n % RING][:, o:o + 512], start=(k == 0), stop=(k == 1))
            ins.then_inc(w_used[n % RING], 1)
            pe.wait_ge(sem("l1_kvev"), 1)
            pe.wait_ge(sem("l1_mq"), 1)
            for h in range(8):
                for j in range(NT):
                    at = (h % 2) * T + j * P
                    ins = pe.transpose(psum[0:96, h // 2, at:at + P], mq[:, j, 96 * h:96 * h + 96], ident)
            ins.then_inc(sem("l1_mqtr"), 1)
            pe.wait_ge(sem("l1_mqT"), 1)
            pe.wait_ge(sem("l1_mk"), 1)
            for h in range(8):
                for j in range(4):
                    ins = pe.transpose(psum[0:96, h, j * P:(j + 1) * P], mk[:, j, 96 * h:96 * h + 96], ident)
            ins.then_inc(sem("l1_mktr"), 1)
            pe.wait_ge(sem("l1_mkT"), 1)
            attn_pe(pe, mla_rounds(), m_probs, m_pT)
            pe.wait_ge(sem("at_o"), at_n["pe"])
            for c in range(4):
                for j in range(NT):
                    at = (c % 2) * T + j * P
                    pe.transpose(psum[:, c // 2, at:at + P], m_in[:, j, C_NQ + c * P:C_NQ + (c + 1) * P], ident)
                for j in range(4):
                    ins = pe.transpose(psum[:, 2 + c, j * P:(j + 1) * P], m_in[:, j, C_NK + c * P:C_NK + (c + 1) * P],
                                       ident)
            ins.then_inc(sem("l1_ntr"), 1)
            pe.wait_ge(sem("l1_nqT"), 1)
            pe.wait_ge(sem("l1_nkT"), 1)
            attn_pe(pe, na_rounds(), m_probs, m_pT)
            pe.wait_ge(sem("at_o"), at_n["pe"])
            for c in range(8):
                for j in range(NT):
                    at = (c % 2) * T + j * P
                    ins = pe.transpose(psum[:, c // 2, at:at + P], mO[:, j, c * P:(c + 1) * P], ident)
            ins.then_inc(sem("mix_tr"), 1)
            spread_pe(pe, 4, fdiag)
            pe.wait_ge(sem("spread_ev"), 5)
            pe.wait_ge(sem("mix_y"), 2)
            out_proj_pe(pe, FIRST["l1_out"], m_mixT, NT)

        def l1_act(act):
            tm_proj_act(act, "l1", FIRST["l1_in"], W_L1, m_in, TILES_L1)
            for q in range(7, 19):
                head_norm_act(act, q, 1 if q < 13 else 8)
            slot_used(act, FIRST["l1_uq"])
            act.activation(mq.rearrange("p j (h n) -> p (j h) n", h=2), psum[:, 4:8, 0:COLS], ACT.Copy)\
               .then_inc(sem("l1_qev"), 1)
            slot_used(act, FIRST["l1_ukv"])
            act.activation(mkv.rearrange("p j (h n) -> p (j h) n", h=2), psum[:, :, :], ACT.Copy)\
               .then_inc(sem("l1_kvev"), 1)
            for q in range(19, 21):
                head_norm_act(act, q, 8)
            act.wait_ge(sem("l1_mqtr"), 1)
            act.activation(mqT[0:96], psum[0:96, 0:4, :].rearrange("p b (h t) -> p (b h) t", h=2), ACT.Copy)\
               .then_inc(sem("l1_mqT"), 1)
            for q in range(21, 25):
                head_norm_act(act, q, 8)
            act.wait_ge(sem("l1_mktr"), 1)
            act.activation(mkT[0:96], psum[0:96, :, :], ACT.Copy).then_inc(sem("l1_mkT"), 1)
            attn_act(act, mla_rounds(), m_probs, m_pT, 96.0 ** -0.5)
            act.wait_ge(sem("l1_ntr"), 1)
            act.activation(nkT, psum[:, 2:6, :], ACT.Copy).then_inc(sem("l1_nkT"), 1)
            attn_act(act, na_rounds(), m_probs, m_pT, 0.125)
            act.wait_ge(sem("mix_tr"), 3)
            act.activation(m_mixT, psum[:, 0:4, :].rearrange("p b (c t) -> p (b c) t", c=2), ACT.Copy)\
               .then_inc(sem("mix_y"), 1)

        def l1_dve(dve):
            def S(ins, name="dve_step"):
                step(dve, ins, name)
            dve.wait_ge(sem("l1_ev"), len(W_L1))
            q = 7
            for j in range(NT):
                head_norm_dve(dve, q, m_in[:, j, C_CQ:C_CQ + 384].unsqueeze(1), m_scr[:, 0:384].unsqueeze(1), 1, 384, None)
                q += 1
            for j in range(4):
                head_norm_dve(dve, q, m_in[:, j, C_CKV:C_CKV + 256].unsqueeze(1), m_scr[:, 0:256].unsqueeze(1), 1, 256,
                              None)
                q += 1
            dve.sem_inc(sem("l1_low"), 1)
            for at, name, tiles in ((C_NQ, "l1_na_q_gain_2", NT), (C_NK, "l1_na_k_gain_2", 4)):
                for j in range(tiles):
                    head_norm_dve(dve, q, m_in[:, j, at:at + 512].rearrange("p (g d) -> p g d", g=8),
                                  m_scr[:, 0:512].rearrange("p (g d) -> p g d", g=8), 8, 64, mat(name))
                    q += 1
            dve.wait_ge(sem("l1_ltr"), 1)
            for c in range(3):
                S(dve.tensor_scalar(cqT[:, c, :], psum[:, c // 2, (c % 2) * T:(c % 2) * T + T],
                                    vec("l1_mla_q_a_gain_2", c), None, MUL))
            for c in range(2):
                S(dve.tensor_scalar(ckvT[:, c, :], psum[:, 2 + c, :], vec("l1_mla_kv_a_gain_2", c), None, MUL),
                  "l1_lowT" if c else "dve_step")
            dve.wait_ge(sem("l1_qev"), 1)
            scr = m_scr[:, 0:768].rearrange("p (g d) -> p g d", g=8)
            for j in range(NT):
                v = mq[:, j, :].rearrange("p (g d) -> p g d", g=8)
                head_norm_dve(dve, q, v, scr, 8, 96, mat("l1_mla_q_gain_2"))
                axial_dve(dve, v, 8, 96, "rope32", j, 8, m_scr[:, 1024:2048])
                q += 1
            dve.sem_inc(sem("l1_mq"), 1)
            dve.wait_ge(sem("l1_kvev"), 1)
            for j in range(4):
                v = mk[:, j, :].rearrange("p (g d) -> p g d", g=8)
                S(dve.tensor_copy(v[:, :, 0:64], mkv[:, j, :].rearrange("p (g d) -> p g d", g=8)[:, :, 0:64]))
                S(dve.tensor_copy(v[:, :, 64:96], m_in[:, j, C_KR:C_KR + 32].unsqueeze(1).to_broadcast([P, 8, 32])))
                head_norm_dve(dve, q, v, scr, 8, 96, mat("l1_mla_k_gain_2"))
                if j < NT:
                    axial_dve(dve, v, 8, 96, "rope32", j, 8, m_scr[:, 1024:2048])
                q += 1
            dve.sem_inc(sem("l1_mk"), 1)
            dve.wait_ge(sem("l1_mkT"), 1)
            attn_dve(dve, mla_rounds(), m_probs, m_pT, 96.0 ** -0.5)
            dve.sem_inc(sem("mla_end"), 1)
            dve.wait_ge(sem("l1_ntr"), 1)
            S(dve.tensor_copy(nqT, psum[:, 0:2, :].rearrange("p b (c t) -> p (b c) t", c=2)), "l1_nqT")
            dve.wait_ge(sem("bias_in"), 16)
            attn_dve(dve, na_rounds(), m_probs, m_pT, 0.125)
            spread_dve(dve, 4, 1, 2, 0, fB, fdiag)
            slot_used(dve, FIRST["l1_out"] + 2)
            add_tokens(dve, x_tm, fB, ftmp)

        @block.sync
        def _(sp):
            for dst, src, name in ((pack, pack_in, "pack_in"), (const, const_in, "const_in"), (x, x_in, "x_in"),
                                   (xc, ctx_in, "ctx_in"), (pos_i, pos_in, "pos_in")):
                sp.dma_start(dst[:, :], src).then_inc(sem(name), 16)
            for r in range(RING):
                sp.dma_start(slot_of[r], stream_in[r]).then_inc(w_ready[r], 16)
            g_end = N_SLOTS_PADDED // RING
            with sp.Fori(1, min(G_MOE, g_end)) as g:
                for r in range(RING):
                    sp.wait_ge(w_used[r], g)
                    sp.dma_start(slot_of[r], stream_in[g * RING + r]).then_inc(w_ready[r], 16)
            for r in range(RING):
                sp.wait_ge(w_used[r], G_MOE)
                sp.dma_start(slot_of[r], stream_in[MOE_SLOT0 + r]).then_inc(e_ready[r], 16)
            with sp.Fori(1, (N_EXP - 1) * G_EXP) as g:
                for r in range(RING):
                    sp.wait_ge(e_used[r], g)
                    sp.dma_start(slot_of[r], stream_in[g * RING + (MOE_SLOT0 + r)]).then_inc(e_ready[r], 16)
            n_visits = moe_count(sp)
            with sp.Fori(N_EXP - 1, n_visits) as v:
                expert = sp.value_load(plan_i[0:1, bass.ds(v + 1, 1)], min_val=0, max_val=N_EXP - 1)
                with sp.Fori(0, G_EXP) as g:
                    for r in range(RING):
                        sp.wait_ge(e_used[r], v * G_EXP + g)
                        sp.dma_start(slot_of[r], stream_in[expert * NB_EXP + g * RING + (MOE_SLOT0 + r)])\
                          .then_inc(e_ready[r], 16)
            for r in range(RING):
                sp.wait_ge(e_used[r], n_visits * G_EXP)
                sp.dma_start(slot_of[r], stream_in[G_MOE * RING + r]).then_inc(w_ready[r], 16)
            with sp.Fori(G_MOE + 1, g_end) as g:
                for r in range(RING):
                    sp.wait_ge(w_used[r], g)
                    sp.dma_start(slot_of[r], stream_in[g * RING + r]).then_inc(w_ready[r], 16)
            sp.wait_ge(sem("x_final"), 1)
            sp.dma_start(out, x[:, :]).then_inc(sem("stored"), 16)
            sp.wait_ge(sem("stored"), 16)

        @block.tensor
        def _(pe):
            pe.wait_ge(sem("pack_in"), 16)
            pe.wait_ge(sem("const_in"), 16)
            ada_pe(pe)
            norm_pe(pe, 0)
            e_proj_pe(pe)
            lru_pe(pe)
            rwkv_in_pe(pe)
            for j in range(NT):
                rwkv_tile_pe(pe, j)
            rwkv_out_pe(pe)
            norm_pe(pe, 1)
            pe.wait_ge(sem("norm_hT"), 2)
            ffn_pe(pe, FIRST["e_ffn"], B0["e_ffn"], NB_FFN, 0)
            norm_pe(pe, 2)
            diff_pe(pe)
            norm_pe(pe, 3)
            moe_pe(pe)
            norm_pe(pe, 4)
            norm_pe(pe, 5)
            l0_pe(pe)
            norm_pe(pe, 6)
            gated_ffn_pe(pe, 2, 6, "l0_ffn")
            norm_pe(pe, 7)
            gated_ffn_pe(pe, 3, 7, "l0_ffn_ctx")
            norm_pe(pe, 8)
            norm_pe(pe, 9)
            l1_pe(pe)
            norm_pe(pe, 10)
            gated_ffn_pe(pe, 5, 10, "l1_ffn")

        @block.gpsimd
        def _(pool):
            pool.wait_ge(sem("norm_hT"), 5)
            pool.dma_start(ar(27648, 2048), band_in).then_inc(sem("band_in"), 16)
            pool.wait_ge(sem("mla_end"), 1)
            pool.dma_start(ar(16768, 4096), bias_in).then_inc(sem("bias_in"), 16)

        @block.scalar
        def _(act):
            ada_act(act)
            act.wait_ge(sem("lru_abs"), 1)
            act.activation(lexp, lz, ACT.Exp, scale=-1.0).then_inc(sem("lru_soft"), 1)
            norm_act(act, 0)
            e_proj_act(act)
            lru_act(act)
            rwkv_in_act(act)
            for j in range(NT):
                rwkv_tile_act(act, j)
            rwkv_out_act(act)
            norm_act(act, 1)
            ffn_act(act, B0["e_ffn"], NB_FFN)
            norm_act(act, 2)
            diff_act(act)
            norm_act(act, 3)
            moe_act(act)
            norm_act(act, 4)
            norm_act(act, 5)
            l0_act(act)
            for k, name in ((6, "l0_ffn"), (7, "l0_ffn_ctx")):
                norm_act(act, k)
                ffn_act(act, B0[name], NB_FFN)
            norm_act(act, 8)
            norm_act(act, 9)
            l1_act(act)
            norm_act(act, 10)
            ffn_act(act, B0["l1_ffn"], NB_FFN)

        @block.vector
        def _(dve):
            for name in ("pack_in", "const_in", "x_in", "ctx_in"):
                dve.wait_ge(sem(name), 16)
            cols_dve(dve)
            ada_mods_dve(dve)
            norm_dve(dve, 0, x_tm, lambda c: vec("e_ln_mix", c), None, 0)
            step(dve, dve.memset(pj[:, :, 0:4], 0.0), "dve_step")
            lru_dve(dve)
            rwkv_in_dve(dve)
            for j in range(NT):
                rwkv_tile_dve(dve, j)
            rwkv_out_dve(dve)
            norm_dve(dve, 1, x_tm, lambda c: vec("e_ln_ffn", c), None, 0)
            ffn_dve(dve, FIRST["e_ffn"], B0["e_ffn"], NB_FFN)
            slot_used(dve, FIRST["e_ffn"] + NB_FFN - 1)
            add_tokens(dve, x_tm)
            dve.wait_ge(sem("pos_in"), 16)
            norm_dve(dve, 2, x_tm, lambda c: vec("o_ln_mix", c), None, 0)
            diff_dve(dve)
            norm_dve(dve, 3, x_tm, lambda c: vec("o_ln_ffn", c), None, 0)
            moe_dve(dve)
            for k, src, cond in ((4, x_tm, 0), (5, xc_tm, 1)):
                norm_dve(dve, k, src, lambda c, cond=cond: ge(0, 0, cond, c),
                         lambda c, cond=cond: mod[0][:, c, cond:cond + 1], T * cond)
            l0_dve(dve)
            gated_ffn_dve(dve, 2, 6, 0, 0, x_tm, "l0_ffn")
            gated_ffn_dve(dve, 3, 7, 0, 1, xc_tm, "l0_ffn_ctx")
            for k, src, cond in ((8, x_tm, 0), (9, xc_tm, 1)):
                norm_dve(dve, k, src, lambda c, cond=cond: ge(1, 0, cond, c),
                         lambda c, cond=cond: mod[1][:, c, cond:cond + 1], T * cond)
            l1_dve(dve)
            gated_ffn_dve(dve, 5, 10, 1, 0, x_tm, "l1_ffn")
            dve.sem_inc(sem("x_final"), 1)


def constants():
    c = np.zeros((P, N_CONST), np.float32)

    def put(name, a):
        o, n = CONST[name]
        c[:, o:o + n] = np.asarray(a, np.float32).reshape(P, n)

    s, t = np.arange(P)[:, None], np.arange(P)[None, :]
    same = s // CH == t // CH
    put("ident", s == t)
    put("ones", np.ones((P, P)))
    put("headones", s // 64 == t // 64)
    put("mask4", np.concatenate([(s < t) & same, (s <= t) & same] * 2, 1))
    put("level", np.concatenate([((t >> l) & 1 == 1) & (s >> l == (t >> l) - 1) for l in range(6)], 1))
    put("scanmask", np.broadcast_to((np.arange(T) % CH != 0)[None], (P, T)))
    put("causal", np.where(t <= s, 0.0, NEG))
    tok = np.arange(T)
    for name, d in (("rope64", 32), ("rope32", 16)):
        inv = (np.float32(10000.0) ** (-np.arange(d // 2, dtype=np.float32) * 2.0 / d)).astype(np.float32)
        ang = np.stack([tok // 64, tok % 64], 1).astype(np.float32)[:, :, None] * inv
        tab = np.stack([np.cos(ang), np.sin(ang)], 1).reshape(NT, P, -1).transpose(1, 0, 2)
        put(name, tab)
    put("iota", np.broadcast_to(np.arange(P)[None], (P, P)))
    put("freq", np.broadcast_to((np.float32(500000.0) ** (-np.arange(0, 16, 2, dtype=np.float32) / 16))[None], (P, 8)))
    band = np.zeros((4, T, T), np.float32)
    for g, w in enumerate((2, 4, 8, 16)):
        lo, hi = np.clip(tok - w // 2, 0, T), np.clip(tok - w // 2 + w, 0, T)
        src = np.arange(T)[:, None]
        band[g] = ((src >= lo) & (src < hi)) / (hi - lo).astype(np.float32) - (src == tok)
    band = band.reshape(4, NT, P, T).transpose(2, 0, 1, 3).reshape(P, N_BAND)
    return c, np.ascontiguousarray(band)


def chunks(v):
    return np.asarray(v).reshape(-1, P).T


def packed(i):
    a = np.zeros((P, N_PACK), np.float32)
    special = {"cond": np.stack([chunks(i["c_2"][0]), chunks(i["c_ctx_2"])], 2)}
    for name, n in VECS:
        o = PACK[name][0]
        a[:, o:o + n] = special[name].reshape(P, n) if name in special else chunks(i[name])
    gate = {}
    for name, key in (("gate_a", "e_gate_a_w"), ("gate_x", "e_gate_x_w")):
        m = np.zeros((P, 4, P), np.float32)
        for h in range(8):
            m[64 * (h % 2):64 * (h % 2) + 64, h // 2, 64 * (h % 2):64 * (h % 2) + 64] = i[key][0, h]
        gate[name] = m
    pool = np.zeros((P, 2, P), np.float32)
    for g in range(4):
        pool[64 * (g % 2):64 * (g % 2) + 64, g // 2, 64 * (g % 2):64 * (g % 2) + 64] = i["l0_pool_w_2"][g]
    mats = {**gate, "w2a2": np.concatenate([i["e_w2"][0], i["e_a2"][0]], 0), "g2": i["e_g2"][0],
            "router": i["o_router"][0].reshape(KD, P, N_EXP).transpose(1, 0, 2), "pool_w": pool}
    for name, n in MATS:
        o = PACK[name][0]
        a[:, o:o + n] = mats[name].reshape(P, n)
    for name, n in ROWS:
        o = PACK[name][0]
        a[:, o:o + n] = np.asarray(i[name]).reshape(1, n)
    return a


def stream(i):
    w = np.zeros((N_STREAM, P, SLOT), np.float32)

    def columns(n0, m, widths, nk):
        at = 0
        for s, n in enumerate(widths):
            w[n0 + s, :, :nk * n] = m[:, at:at + n].reshape(nk, P, n).transpose(1, 0, 2).reshape(P, -1)
            at += n

    def rows(n0, m):
        for s in range(3):
            part = m[3 * s * P:min(3 * s + 3, KD) * P]
            w[n0 + s, :, :part.size // P] = part.reshape(-1, P, D).transpose(1, 0, 2).reshape(P, -1)

    def ffn(n0, g, u, d):
        nb = g.shape[1] // P
        v = w[n0:n0 + nb].reshape(nb, P, 3, D)
        for q, m in enumerate((g, u)):
            v[:, :, q] = m.reshape(KD, P, nb, P).transpose(2, 1, 0, 3).reshape(nb, P, D)
        v[:, :, 2] = d.reshape(nb, P, D)

    def even(n):
        return [COLS] * (n // COLS) + ([n % COLS] if n % COLS else [])

    for l in range(2):
        columns(FIRST[f"ada{l}"], i[f"l{l}_ada_w_2"], even(6 * D), KD)
    e_in = np.zeros((D, COLS * -(-EVEN_IN // COLS)), np.float32)
    e_in[:, :EVEN_IN] = i["e_w_in"][0]
    columns(FIRST["e_in"], e_in, even(e_in.shape[1]), KD)
    rows(FIRST["e_out"], i["e_w_out"][0])
    ffn(FIRST["e_ffn"], i["e_ffn_gate"][0], i["e_ffn_up"][0], i["e_ffn_down"][0])
    columns(FIRST["qkv"], i["o_w_qkv"][0], even(QKV), KD)
    rows(FIRST["o_out"], i["o_w_o"][0])
    for e in range(N_EXP):
        ffn(MOE_SLOT0 + e * NB_EXP, i["o_moe_gate"][0, e], i["o_moe_up"][0, e], i["o_moe_down"][0, e])
    m = i["l0_w_in_2"]
    q = m[:, 256:1024].reshape(D, 12, 64)[:, list(HEADS0)].reshape(D, 768)
    columns(FIRST["l0_in"], np.concatenate([m[:, :256], q, m[:, 1024:]], 1), even(L0_IN), KD)
    rows(FIRST["l0_out"], i["l0_w_out_2"])
    for name in ("l0_ffn", "l0_ffn_ctx"):
        ffn(FIRST[name], i["l0_ffn_w_gate_2"], i["l0_ffn_w_up_2"], i["l0_ffn_w_down_2"])
    m = i["l1_w_in_2"]
    m = np.concatenate([m[:, :384], m[:, 672:1184], m[:, 384:672], m[:, 1184:]], 1)
    columns(FIRST["l1_in"], m, even(L1_IN), KD)
    columns(FIRST["l1_uq"], i["l1_mla_w_uq_2"], [768], 3)
    columns(FIRST["l1_ukv"], i["l1_mla_w_ukv_2"], [1024], 2)
    rows(FIRST["l1_out"], i["l1_w_out_2"])
    ffn(FIRST["l1_ffn"], i["l1_ffn_w_gate_2"], i["l1_ffn_w_up_2"], i["l1_ffn_w_down_2"])
    return w


def relative_bias(rpb):
    tok = np.arange(T)
    row, col = tok // 64, tok % 64
    start = np.clip(col - 8, 0, 48)
    inside = (col[None] >= start[:, None]) & (col[None] < start[:, None] + 16)
    dr = row[None] - row[:, None] + 7
    dc = np.clip(col[None] - col[:, None] + 15, 0, 30)
    b = np.where(inside[None], rpb[:, dr, dc], np.float32(NEG))
    return np.ascontiguousarray(b.reshape(8, NT, P, T).transpose(2, 1, 0, 3).reshape(P, N_BIAS))


def host_arrays(inputs):
    i = {k: np.asarray(v) for k, v in inputs.items()}
    const, band = constants()
    tm = lambda a: np.ascontiguousarray(a.reshape(NT, P, D).transpose(1, 0, 2).reshape(P, NT * D))
    return {"x": tm(i["x"]), "ctx": tm(i["ctx_2"]),
            "positions": np.ascontiguousarray(i["positions"].reshape(NT, P).T.astype(np.int32)),
            "pack": packed(i), "const": const, "band": band, "bias": relative_bias(i["l1_na_rpb_2"]),
            "stream": stream(i)}


def kernel(**inputs):
    import concourse.bacc as bacc
    from concourse.bass_utils import run_bass_kernel_spmd

    nc = bacc.Bacc("TRN2", target_bir_lowering=False, num_devices=1)
    arrays = host_arrays(inputs)
    args = [nc.dram_tensor(f"{n}_dram", a.shape, mybir.dt.from_np(a.dtype), kind="ExternalInput").ap()
            for n, a in arrays.items()]
    out = nc.dram_tensor("out_dram", (P, NT * D), mybir.dt.float32, kind="ExternalOutput").ap()
    program(nc, *args, out)
    r = run_bass_kernel_spmd(nc, [{f"{n}_dram": a for n, a in arrays.items()}], core_ids=[0])
    got = r.results[0]["out_dram"]
    return np.ascontiguousarray(got.reshape(P, NT, D).transpose(1, 0, 2).reshape(1, T, D))
```

```python
import math

import numpy as np

import concourse.bass as bass
from concourse import mybir
from contextlib import ExitStack

P = 128
D = 1024
KD = D // P
T = 256
NT = T // P
F_FFN = 2816
N_EXP = 8
F_EXP = 3584
RING = 4
SLOT = 3 * D
FBLK = 128
NB_FFN = F_FFN // FBLK
NB_EXP = F_EXP // FBLK
LAMBDA_INIT = 0.8 - 0.6 * math.exp(-0.3)
NEG = -1.0e30
CH = 64
EXP_M_HALF = math.exp(-0.5)
EVEN_IN = 2816
QKV = 3072
L0_IN = 1536
L1_IN = 2208
COLS = 384

HEADS0 = (0, 3, 1, 4, 2, 5, 6, 9, 7, 10, 8, 11)

STREAM = [
    ("e_in", -(-EVEN_IN // COLS)), ("ada0", 6 * D // COLS), ("e_out", 3), ("e_ffn", NB_FFN),
    ("qkv", QKV // COLS), ("ada1", 6 * D // COLS), ("o_out", 3),
    ("l0_in", L0_IN // COLS), ("l0_out", 3), ("l0_ffn", NB_FFN), ("l0_ffn_ctx", NB_FFN),
    ("l1_in", -(-L1_IN // COLS)), ("l1_uq", 1), ("l1_ukv", 1), ("l1_out", 3), ("l1_ffn", NB_FFN),
]
FIRST = {}
N_SLOTS = 0
for _name, _n in STREAM:
    FIRST[_name] = N_SLOTS
    N_SLOTS += _n
N_SLOTS_PADDED = -(-N_SLOTS // RING) * RING
MOE_SLOT0 = N_SLOTS_PADDED
N_STREAM = N_SLOTS_PADDED + N_EXP * NB_EXP
G_MOE = FIRST["l0_in"] // RING
G_EXP = NB_EXP // RING
assert FIRST["l0_in"] % RING == 0 and NB_EXP % RING == 0
CAP = P
MAX_VISITS = N_EXP + 3

VECS = [("e_ln_mix", 8), ("e_ln_ffn", 8), ("o_ln_mix", 8), ("o_ln_ffn", 8),
        ("l0_norm_mix_2", 8), ("l0_norm_ffn_2", 8), ("l1_norm_mix_2", 8), ("l1_norm_ffn_2", 8),
        ("e_conv_w", 16), ("e_conv_b", 4), ("e_gate_a_b", 4), ("e_gate_x_b", 4), ("e_lru_lambda", 4),
        ("e_shift_mu", 14), ("e_w0", 4), ("e_a0", 4), ("e_k_k", 4), ("e_k_a", 4), ("e_r_k", 4),
        ("e_gn_w", 4), ("e_gn_b", 4), ("cond", 16), ("l0_ada_b_2", 48), ("l1_ada_b_2", 48),
        ("l1_mla_q_a_gain_2", 3), ("l1_mla_kv_a_gain_2", 2), ("l0_pool_scale_2", 2)]
MATS = [("gate_a", 512), ("gate_x", 512), ("w2a2", 512), ("g2", 512), ("router", 64), ("pool_w", 256)]
ROWS = [("o_q_norm", 64), ("o_k_norm", 64), ("o_subln", 128), ("o_lambda_q1", 64), ("o_lambda_k1", 64),
        ("o_lambda_q2", 64), ("o_lambda_k2", 64), ("l0_q_gain_2", 64), ("l0_k_gain_2", 64),
        ("l1_mla_q_gain_2", 96), ("l1_mla_k_gain_2", 96), ("l1_na_q_gain_2", 64), ("l1_na_k_gain_2", 64)]
PACK = {}
N_PACK = 0
for _name, _n in VECS + MATS + ROWS:
    PACK[_name] = (N_PACK, _n)
    N_PACK += _n
CONSTS = [("ident", 128), ("ones", 128), ("headones", 128), ("mask4", 512), ("level", 6 * 128),
          ("scanmask", T), ("causal", 128), ("rope64", 2 * NT * 32), ("rope32", 2 * NT * 16),
          ("iota", 128), ("freq", 8)]
CONST = {}
N_CONST = 0
for _name, _n in CONSTS:
    CONST[_name] = (N_CONST, _n)
    N_CONST += _n
N_BAND = 4 * NT * T
N_BIAS = NT * 8 * T


def program(nc, x_in, ctx_in, pos_in, pack_in, const_in, band_in, bias_in, stream_in, out):
    f32 = mybir.dt.float32
    f32r = mybir.dt.float32r
    i32 = mybir.dt.int32
    u32 = mybir.dt.uint32
    ALU = mybir.AluOpType
    ACT = mybir.ActivationFunctionType
    AX = mybir.AxisListType
    MUL, ADD, SUB, MAX, MIN = ALU.mult, ALU.add, ALU.subtract, ALU.max, ALU.min

    ctx = ExitStack()
    with ctx:
        def sb(name, cols, dt=f32):
            return ctx.enter_context(nc.sbuf_tensor(name, [P, cols], dt))

        ring = sb("ring", RING * SLOT)
        x = sb("x", NT * D)
        xc = sb("xc", NT * D)
        pack = sb("pack", N_PACK)
        const = sb("const", N_CONST)
        mods = sb("mods", 2 * 48 * 2)
        geff = sb("geff", 2 * 2 * 2 * 8)
        small = sb("small", 768)
        ARENA = (nc.sbuf_usable_end - 16512) // 4 - (RING * SLOT + 2 * NT * D + N_PACK + N_CONST + 192 + 64 + 768) - 40
        with nc.sbuf_tensor("arena", [P, ARENA], f32) as arena:
            pass
        PARTS0 = 10240
        r_low = sb("r_low", 2048, f32r)
        sb("arena_between", PARTS0 - 2048)
        r_high = sb("r_high", 29696 - PARTS0, f32r)
        psum = ctx.enter_context(nc.psum_tensor("psum", [P, 8, 512], f32))

        sems = {}

        def sem(name):
            if name not in sems:
                sems[name] = ctx.enter_context(nc.semaphore(name))
            return sems[name]

        w_ready = [sem(f"w_ready{r}") for r in range(RING)]
        w_used = [sem(f"w_used{r}") for r in range(RING)]
        e_ready = [sem(f"expert_ready{r}") for r in range(RING)]
        e_used = [sem(f"expert_used{r}") for r in range(RING)]

        def ar(o, n, spec=None, **kw):
            assert o + n <= ARENA, (o, n, ARENA)
            v = arena[:, o:o + n]
            return v.rearrange(spec, **kw) if spec else v

        def parts(o, n, spec, **kw):
            v = r_low[:, o:o + n] if o < PARTS0 else r_high[:, o - PARTS0:o - PARTS0 + n]
            return v.rearrange(spec, **kw)

        def vec(name, i=0, n=1):
            o = PACK[name][0] + i
            return pack[:, o:o + n]

        def mat(name):
            o, n = PACK[name]
            return pack[:, o:o + n]

        def cst(name):
            o, n = CONST[name]
            return const[:, o:o + n]

        ident = cst("ident")
        slot_of = [ring[:, r * SLOT:(r + 1) * SLOT] for r in range(RING)]
        x_tm = x[:, :].rearrange("p (j d) -> p j d", j=NT)
        xc_tm = xc[:, :].rearrange("p (j d) -> p j d", j=NT)
        mod = [mods[:, 96 * l:96 * l + 96].rearrange("p (c n) -> p c n", n=2) for l in range(2)]

        def ge(layer, which, cond, c):
            o = ((layer * 2 + which) * 2 + cond) * 8 + c
            return geff[:, o:o + 1]

        O_XN, O_HT, O_W = 0, 2048, 6144
        xn = ar(O_XN, 2048, "p (j d) -> p j d", j=NT)
        hT = ar(O_HT, 4096, "p (k t) -> p k t", k=KD)

        counts = {}

        def step(eng, ins, name):
            ins.then_inc(sem(name), 1)
            counts[name] = counts.get(name, 0) + 1
            eng.wait_ge(sem(name), counts[name])

        def slot_ready(pe, n):
            pe.wait_ge(w_ready[n % RING], 16 * (n // RING + 1))

        def slot_used(eng, n):
            eng.wait_ge(w_used[n % RING], n // RING + 1)

        block = ctx.enter_context(nc.Block())

        SM = {}
        sm_at = [0]

        def sm(name, n):
            if name not in SM:
                SM[name] = small[:, sm_at[0]:sm_at[0] + n]
                sm_at[0] += n
                assert sm_at[0] <= 768, name
            return SM[name]

        ss = sm("ss", 2)
        scT = sm("scT", 16)

        mean_sq, inv_rms = sm("mean_sq", 32), sm("inv_rms", 32)
        roots = [0]

        def inverse_root_dve(dve, ssq, width):
            n = ssq.shape[1]
            step(dve, dve.tensor_scalar(mean_sq[:, 0:n], ssq, 1.0 / width, 1e-6, MUL, ADD), "rms_in")
            dve.wait_ge(sem("rms_out"), counts["rms_in"])
            step(dve, dve.reciprocal(inv_rms[:, 0:n], inv_rms[:, 0:n]), "dve_step")
            return inv_rms[:, 0:n]

        def root_act(act, n):
            roots[0] += 1
            act.wait_ge(sem("rms_in"), roots[0])
            act.activation(inv_rms[:, 0:n], mean_sq[:, 0:n], ACT.Sqrt).then_inc(sem("rms_out"), 1)

        def norm_dve(dve, k, src, gain, shift, off):
            for j in range(NT):
                step(dve, dve.tensor_tensor_reduce(xn[:, j, :], src[:, j, :], src[:, j, :], 1.0, 0.0, MUL, ADD,
                                                   ss[:, j:j + 1]), "dve_step")
            rstd = inverse_root_dve(dve, ss, D)
            dve.tensor_scalar(xn[:, 0, :], src[:, 0, :], rstd[:, 0:1], None, MUL)
            step(dve, dve.tensor_scalar(xn[:, 1, :], src[:, 1, :], rstd[:, 1:2], None, MUL), "norm_xn")
            for c in range(KD):
                if c % 2 == 0:
                    dve.wait_ge(sem("norm_tr"), 4 * k + c // 2 + 1)
                src_ps = psum[:, c // 2, (c % 2) * T:(c % 2) * T + T]
                ins = dve.tensor_scalar(hT[:, c, off:off + T], src_ps, gain(c), shift(c) if shift else None, MUL,
                                        *([ADD] if shift else []))
            step(dve, ins, "norm_hT")

        def norm_pe(pe, k):
            pe.wait_ge(sem("norm_xn"), k + 1)
            for c in range(KD):
                for j in range(NT):
                    ins = pe.transpose(psum[:, c // 2, (c % 2) * T + j * P:(c % 2) * T + j * P + P],
                                       xn[:, j, c * P:(c + 1) * P], ident)
                if c % 2:
                    ins.then_inc(sem("norm_tr"), 1)

        O_SPLIT = 11264
        w_hi, w_lo = [parts(O_SPLIT + i * 4 * D, 4 * D, "p (b n) -> p b n", b=2) for i in range(2)]
        d_hi, d_lo = [parts(O_SPLIT + (8 + 4 * i) * D, 4 * D, "p (b n) -> p b n", b=4)
                      for i in range(2)]
        x_hi, x_lo = [parts(o, 2048, "p (k t) -> p k t", k=KD) for o in (0, 27648)]

        def blocks(name, n, bank, o, ready, used, hi, lo):
            def pair(at):
                return ar(at, 2 * n, "p (b t) -> p b t", b=2)
            h_hi, h_lo = [parts(PARTS0 + 2 * n * i, 2 * n, "p (b t) -> p b t", b=2) for i in range(2)]
            return {"name": name, "n": n, "bank": bank, "ready": ready, "used": used, "x_hi": hi, "x_lo": lo,
                    "silu": pair(o), "h": pair(o + 2 * n), "h_hi": h_hi, "h_lo": h_lo}

        def place(ph, t0, b0, i, it):
            return (ph + i) % RING, it + (t0 + (ph + i) // RING), it * RING + (b0 + i)

        def turns(nb):
            return (nb - 4) // RING, 2 + (nb - 4) // RING * RING

        def gate_up_pe(pe, f, at, i):
            r, turn, blk = at
            s, n, b = f["name"], f["n"], i % 2
            pe.wait_ge(sem(s + "_w_lo"), blk + 1)
            if i >= 2:
                pe.wait_ge(sem(s + "_h"), blk - 1)
            for part in range(2):
                for k in range(KD):
                    o = part * D + k * P
                    dst = psum[:, f["bank"] + b, part * n:part * n + n]
                    hi, lo = w_hi[:, b, o:o + P], w_lo[:, b, o:o + P]
                    pe.matmul(dst, hi, f["x_hi"][:, k, :], start=(k == 0), stop=False)
                    pe.matmul(dst, hi, f["x_lo"][:, k, :], start=False, stop=False)
                    ins = pe.matmul(dst, lo, f["x_hi"][:, k, :], start=False, stop=(k == KD - 1))
            ins.then_inc(sem(s + "_gu"), 1)

        def down_pe(pe, f, at, i, first, last):
            r, turn, blk = at
            s, b, tiles = f["name"], i % 2, f["n"] // P
            pe.wait_ge(sem(s + "_h"), blk + 1)
            pe.wait_ge(f["used"][r], turn + 1)
            for j in range(tiles):
                for hf in range(2):
                    dst = psum[:, f["bank"] - 2 * tiles + 2 * j + hf, :]
                    hi, lo = [d[:, i % 4, hf * 512:(hf + 1) * 512] for d in (d_hi, d_lo)]
                    h_hi, h_lo = f["h_hi"][:, b, j * P:(j + 1) * P], f["h_lo"][:, b, j * P:(j + 1) * P]
                    pe.matmul(dst, h_hi, hi, start=first, stop=False)
                    pe.matmul(dst, h_hi, lo, start=False, stop=False)
                    ins = pe.matmul(dst, h_lo, hi, start=False, stop=last)
            ins.then_inc(sem(s + "_dn"), 1)

        def blocks_pe(pe, f, ph, t0, b0, nb):
            def gu(i, it=0):
                gate_up_pe(pe, f, place(ph, t0, b0, i, it), i)

            def dn(i, it=0):
                down_pe(pe, f, place(ph, t0, b0, i, it), i, i == 0, i == nb - 1)

            loops, tail = turns(nb)
            gu(0)
            gu(1)
            dn(0)
            with pe.Fori(0, loops) as it:
                for u in range(RING):
                    gu(2 + u, it)
                    dn(1 + u, it)
            for i in range(tail, nb):
                gu(i)
                dn(i - 1)
            dn(nb - 1)

        def split_act(act, f, at, i):
            r, turn, blk = at
            act.wait_ge(f["ready"][r], turn * 16 + 16)
            for part in range(2):
                act.activation(w_hi[:, i % 2, part * D:part * D + D], slot_of[r][:, part * D:part * D + D], ACT.Copy)\
                   .then_inc(sem(f["name"] + "_w_hi"), 1)
            if i >= 4:
                act.wait_ge(sem(f["name"] + "_dn"), blk - 3)
            act.activation(d_hi[:, i % 4, :], slot_of[r][:, 2 * D:3 * D], ACT.Copy).then_inc(sem(f["name"] + "_w_hi"), 1)

        def silu_act(act, f, at, i):
            r, turn, blk = at
            s, b = f["name"], i % 2
            act.wait_ge(sem(s + "_gu"), blk + 1)
            if i >= 2:
                act.wait_ge(sem(s + "_h"), blk - 1)
            act.activation(f["silu"][:, b, :], psum[:, f["bank"] + b, 0:f["n"]], ACT.Silu).then_inc(sem(s + "_silu"), 1)

        def blocks_act(act, f, ph, t0, b0, nb):
            def at(i, it=0):
                return place(ph, t0, b0, i, it)

            def stage(i, it=0):
                silu_act(act, f, at(i, it), i)
                if i + 2 < nb:
                    split_act(act, f, at(i + 2, it), i + 2)

            split_act(act, f, at(0), 0)
            split_act(act, f, at(1), 1)
            loops, tail = turns(nb)
            stage(0)
            stage(1)
            with act.Fori(0, loops) as it:
                for u in range(RING):
                    stage(2 + u, it)
            for i in range(tail, nb):
                stage(i)

        def split_dve(dve, f, at, i):
            r, turn, blk = at
            for part in range(3):
                o = part * D
                hi, lo = [w[:, i % 2, o:o + D] if part < 2 else d[:, i % 4, :] for w, d in ((w_hi, d_hi), (w_lo, d_lo))]
                dve.wait_ge(sem(f["name"] + "_w_hi"), blk * 3 + (part + 1))
                ins = dve.tensor_tensor(lo, slot_of[r][:, o:o + D], hi.bitcast(f32), SUB)
                if part == 1:
                    ins.then_inc(sem(f["name"] + "_w_lo"), 1)
            ins.then_inc(f["used"][r], 1)

        def hidden_dve(dve, f, at, i):
            r, turn, blk = at
            s, n, b = f["name"], f["n"], i % 2
            dve.wait_ge(sem(s + "_silu"), blk + 1)
            up = psum[:, f["bank"] + b, n:2 * n]
            dve.tensor_tensor(f["h"][:, b, :], f["silu"][:, b, :], up, MUL)
            dve.tensor_tensor(f["h_hi"][:, b, :], f["silu"][:, b, :], up, MUL).then_inc(sem(s + "_h_hi"), 1)
            dve.wait_ge(sem(s + "_h_hi"), blk + 1)
            dve.tensor_tensor(f["h_lo"][:, b, :], f["h"][:, b, :], f["h_hi"][:, b, :].bitcast(f32), SUB)\
               .then_inc(sem(s + "_h"), 1)

        def blocks_dve(dve, f, ph, t0, b0, nb):
            def at(i, it=0):
                return place(ph, t0, b0, i, it)

            def stage(i, it=0):
                hidden_dve(dve, f, at(i, it), i)
                if i + 2 < nb:
                    split_dve(dve, f, at(i + 2, it), i + 2)

            split_dve(dve, f, at(0), 0)
            split_dve(dve, f, at(1), 1)
            loops, tail = turns(nb)
            stage(0)
            stage(1)
            with dve.Fori(0, loops) as it:
                for u in range(RING):
                    stage(2 + u, it)
            for i in range(tail, nb):
                stage(i)

        swiglu = blocks("ffn", T, 4, O_W, w_ready, w_used, x_hi, x_lo)

        def ffn_pe(pe, q, name):
            n0 = FIRST[name]
            pe.wait_ge(sem("x_lo"), q + 1)
            blocks_pe(pe, swiglu, n0 % RING, n0 // RING, q * NB_FFN, NB_FFN)

        def ffn_act(act, k, q, name):
            n0 = FIRST[name]
            act.wait_ge(sem("norm_hT"), k + 1)
            act.activation(x_hi, hT[:, :, 0:T], ACT.Copy).then_inc(sem("x_hi"), 1)
            blocks_act(act, swiglu, n0 % RING, n0 // RING, q * NB_FFN, NB_FFN)

        def ffn_dve(dve, q, name):
            n0 = FIRST[name]
            dve.wait_ge(sem("x_hi"), q + 1)
            dve.tensor_tensor(x_lo, hT[:, :, 0:T], x_hi.bitcast(f32), SUB).then_inc(sem("x_lo"), 1)
            blocks_dve(dve, swiglu, n0 % RING, n0 // RING, q * NB_FFN, NB_FFN)
            dve.wait_ge(sem("ffn_dn"), (q + 1) * NB_FFN)

        def add_tokens(dve, dst, scale_row=None, tmp=None):
            for j in range(NT):
                src = psum[:, 2 * j:2 * j + 2, :].rearrange("p b n -> p (b n)")
                if scale_row is not None:
                    step(dve, dve.tensor_tensor(tmp, src, scale_row, MUL), "dve_step")
                    src = tmp
                step(dve, dve.tensor_tensor(dst[:, j, :], dst[:, j, :], src, ADD), "dve_step")

        def out_proj_pe(pe, n0, lhs, tiles):
            for s in range(3):
                slot_ready(pe, n0 + s)
                w = slot_of[(n0 + s) % RING]
                for k in range(3 * s, min(3 * s + 3, KD)):
                    for j in range(tiles):
                        for hf in range(2):
                            o = (k - 3 * s) * D + hf * 512
                            ins = pe.matmul(psum[:, 2 * j + hf, :], lhs[:, k, j * P:(j + 1) * P], w[:, o:o + 512],
                                            start=(k == 0), stop=(k == KD - 1))
                ins.then_inc(w_used[(n0 + s) % RING], 1)

        ADA_SLOTS = 6 * D // COLS
        ADA_0A, ADA_0B = 4, 13
        cond_z = ar(25600, KD * 254, "p (k n) -> p k n", k=KD)
        ada_rows = ar(27648, P)

        def ada_act(act):
            act.wait_ge(sem("pack_in"), 32)
            act.activation(scT, vec("cond", 0, 16), ACT.Silu).then_inc(sem("ada_silu"), 1)

        def ada_z_dve(dve):
            step(dve, dve.memset(cond_z, 0.0), "dve_step")
            step(dve, dve.tensor_copy(cond_z[:, :, 126:128], scT.rearrange("p (k n) -> p k n", k=KD)), "ada_z")

        def ada_pe(pe, l, s0, s1):
            if s0 == 0:
                pe.wait_ge(sem("ada_z"), l + 1)
            n0 = FIRST[f"ada{l}"]
            for s in range(s0, s1):
                slot_ready(pe, n0 + s)
                w = slot_of[(n0 + s) % RING]
                for c in range(3 * s, 3 * s + 3):
                    for k in range(KD):
                        o = k * COLS + (c - 3 * s) * P
                        ins = pe.matmul(psum[:, 6 + l, 0:P], cond_z[:, k, 126 - 2 * c:254 - 2 * c], w[:, o:o + P],
                                        start=(c + k == 0), stop=(c == 3 * ADA_SLOTS - 1 and k == KD - 1))
                ins.then_inc(w_used[(n0 + s) % RING], 1)

        def ada_rows_act(act, l):
            slot_used(act, FIRST[f"ada{l}"] + ADA_SLOTS - 1)
            act.activation(ada_rows, psum[:, 6 + l, 0:P], ACT.Copy).then_inc(sem("ada_rows"), 1)

        def ada_tr_pe(pe, l):
            pe.wait_ge(sem("ada_rows"), l + 1)
            pe.transpose(psum[:, 6 + l, P:2 * P], ada_rows, ident).then_inc(sem("ada_tr"), 1)

        def ada_mods_dve(dve, l):
            dve.wait_ge(sem("ada_tr"), l + 1)
            b = vec(f"l{l}_ada_b_2", 0, 48).unsqueeze(2).to_broadcast([P, 48, 2])
            step(dve, dve.tensor_tensor(mod[l], psum[:, 6 + l, P:P + 96].rearrange("p (c n) -> p c n", n=2), b, ADD),
                 "dve_step")
            for which in range(2):
                g = vec(f"l{l}_norm_{('mix', 'ffn')[which]}_2", 0, 8)
                for cond in range(2):
                    o = ((l * 2 + which) * 2 + cond) * 8
                    sc = mod[l][:, 8 * (3 * which + 1):8 * (3 * which + 1) + 8, cond]
                    step(dve, dve.scalar_tensor_tensor(geff[:, o:o + 8], sc, 1.0, g, ADD, MUL), "dve_step")

        O_PJ, O_PS, O_YT, O_BON, O_GG, O_PR, O_BM, O_KM, O_MISC = 6144, 11864, 15448, 17496, 18520, 19544, 21592, 22616, 23640
        pj = ar(O_PJ, 22 * 260, "p (c t) -> p c t", c=22)
        ps = ar(O_PS, 14 * T, "p (c t) -> p c t", c=14)
        yT = ar(O_YT, 2048, "p (c t) -> p c t", c=8)
        bon = ar(O_BON, 1024, "p (c t) -> p c t", c=4)
        gg = ar(O_GG, 1024, "p (c t) -> p c t", c=4)
        PR = ar(O_PR, 2048, "p (c j w t) -> p c j w t", c=4, j=2, w=2)
        Bm = ar(O_BM, 1024, "p (c t) -> p c t", c=4)
        Km = ar(O_KM, 1024, "p (c t) -> p c t", c=4)
        eC = ar(O_MISC, 16, "p (c n) -> p c n", c=4)
        Ms = ar(O_MISC + 16, 256, "p (c v) -> p c v", c=4)
        oT = ar(O_MISC + 272, 1024, "p (c t) -> p c t", c=4)
        Ysb = ar(O_MISC + 1296, 512)
        t1, t2, t3, t4, t5, t6 = [ar(1024 * i, 1024, "p (c t) -> p c t", c=4) for i in range(6)]
        Q4 = ar(0, 4096, "p (h m t) -> p h m t", h=8, m=4)
        X, XT, AbT, Yb = [ar(4096 + 1024 * i, 1024, "p (h t) -> p h t", h=8) for i in range(4)]
        tm4 = [ar(8192 + 512 * i, 512) for i in range(4)]
        Vt, Bt, Kt, Pt = tm4
        Ub, GVb = ar(10240, 512), ar(10752, 512)
        WTb = ar(11264, 512, "p (c t) -> p c t", c=4)
        n_e = FIRST["e_in"]
        N_EIN = -(-EVEN_IN // COLS)

        def e_proj_pe(pe):
            pe.wait_ge(sem("norm_hT"), 1)
            for s in range(N_EIN):
                slot_ready(pe, n_e + s)
                if s >= 4:
                    pe.wait_ge(sem("e_proj_ev"), s - 3)
                w = slot_of[(n_e + s) % RING]
                for cc in range(min(3, 22 - 3 * s)):
                    for k in range(KD):
                        ins = pe.matmul(psum[:, 2 * (s % 4) + cc // 2, (cc % 2) * T:(cc % 2) * T + T],
                                        w[:, k * COLS + cc * P:k * COLS + (cc + 1) * P], hT[:, k, 0:T],
                                        start=(k == 0), stop=(k == KD - 1))
                ins.then_inc(w_used[(n_e + s) % RING], 1)

        def e_proj_act(act):
            for s in range(N_EIN):
                slot_used(act, n_e + s)
                n = min(3, 22 - 3 * s)
                src = psum[:, 2 * (s % 4):2 * (s % 4) + 2, :].rearrange("p b n -> p (b n)")[:, 0:n * T]
                act.activation(pj[:, 3 * s:3 * s + n, 4:260], src.rearrange("p (c t) -> p c t", c=n), ACT.Copy)\
                   .then_inc(sem("e_proj_ev"), 1)

        spl, omka = sm("spl", 4), sm("omka", 4)
        lz, lz2, lacc = sm("lz", 4), sm("lz2", 4), sm("lacc", 4)
        lexp = sm("lexp", 4)

        def cols_dve(dve):
            def S(ins, name="dve_step"):
                step(dve, ins, name)
            S(dve.tensor_scalar(omka, vec("e_k_a", 0, 4), -1.0, 1.0, MUL, ADD))
            lam = vec("e_lru_lambda", 0, 4)
            S(dve.tensor_scalar(lz, lam, -1.0, None, MUL))
            S(dve.tensor_tensor(lz, lz, lam, MAX), "lru_dve")
            dve.wait_ge(sem("lru_act"), 1)
            S(dve.tensor_scalar(lz, lexp, 2.0, None, ADD))
            S(dve.reciprocal(lz, lz))
            S(dve.tensor_tensor(lz, lz, lexp, MUL))
            S(dve.tensor_tensor(lz2, lz, lz, MUL))
            S(dve.tensor_scalar(lacc, lz2, 2.0 / 17, 2.0 / 15, MUL, ADD))
            for n in (13, 11, 9, 7, 5, 3, 1):
                S(dve.tensor_tensor(lacc, lacc, lz2, MUL))
                S(dve.tensor_scalar(lacc, lacc, 2.0 / n, None, ADD))
            S(dve.tensor_tensor(lacc, lacc, lz, MUL))
            S(dve.tensor_scalar(lz, lam, -1.0, 0.0, MUL, MAX))
            S(dve.tensor_tensor(lacc, lacc, lz, ADD))
            S(dve.tensor_scalar(spl, lacc, -8.0, None, MUL))

        def lru_dve(dve):
            def S(ins, name="dve_step"):
                step(dve, ins, name)
            dve.wait_ge(sem("e_proj_ev"), N_EIN)
            for c in range(4):
                S(dve.tensor_scalar(t1[:, c, :], pj[:, c, 1:257], vec("e_conv_w", c), vec("e_conv_b", c), MUL, ADD))
            for n in range(1, 4):
                for c in range(4):
                    S(dve.scalar_tensor_tensor(t1[:, c, :], pj[:, c, 1 + n:257 + n], vec("e_conv_w", 4 * n + c),
                                               t1[:, c, :], MUL, ADD), "lru_dve" if (n, c) == (3, 3) else "dve_step")
            dve.wait_ge(sem("lru_act"), 2)
            for c in range(4):
                S(dve.tensor_scalar(t2[:, c, :], t2[:, c, :], spl[:, c:c + 1], None, MUL),
                  "lru_dve" if c == 3 else "dve_step")
            dve.wait_ge(sem("lru_act"), 3)
            S(dve.tensor_tensor(t6, t4, t4, MUL))
            S(dve.scalar_tensor_tensor(t6, t6, 1.0, t5, ADD, MUL))
            S(dve.tensor_scalar(t6, t6, -1.0, 0.0, MUL, MAX), "lru_dve")
            dve.wait_ge(sem("lru_act"), 4)
            S(dve.tensor_tensor(t5, t5, t3, MUL))
            S(dve.tensor_tensor(t5, t5, t1, MUL))
            for c in range(4):
                S(dve.tensor_tensor_scan(yT[:, c, :], t4[:, c, :], t5[:, c, :], 0.0, MUL, ADD))
            g = pj[:, 4:8, 4:260]
            S(dve.tensor_tensor(t1, g, g, MUL))
            S(dve.tensor_scalar(t1, t1, 0.044715, 1.0, MUL, ADD))
            S(dve.tensor_tensor(t1, t1, g, MUL), "lru_dve")
            dve.wait_ge(sem("lru_act"), 5)
            S(dve.tensor_tensor(t2, t2, g, MUL))
            S(dve.tensor_tensor(yT[:, 0:4, :], yT[:, 0:4, :], t2, MUL))

        def lru_pe(pe):
            pe.wait_ge(sem("lru_dve"), 2)
            for q, name in enumerate(("gate_a", "gate_x")):
                for c in range(4):
                    ins = pe.matmul(psum[:, 2 * q + c // 2, (c % 2) * T:(c % 2) * T + T],
                                    mat(name)[:, c * P:(c + 1) * P], t1[:, c, :], start=True, stop=True)
            ins.then_inc(sem("lru_gates"), 1)

        def lru_act(act):
            act.wait_ge(sem("lru_gates"), 1)
            for q, (t, b) in enumerate(((t2, "e_gate_a_b"), (t3, "e_gate_x_b"))):
                for c in range(4):
                    ins = act.activation(t[:, c, :], psum[:, 2 * q + c // 2, (c % 2) * T:(c % 2) * T + T], ACT.Sigmoid,
                                         bias=vec(b, c))
            ins.then_inc(sem("lru_act"), 1)
            act.wait_ge(sem("lru_dve"), 3)
            act.activation(t4, t2, ACT.Exp)
            act.activation(t5, t2, ACT.Tanh).then_inc(sem("lru_act"), 1)
            act.wait_ge(sem("lru_dve"), 4)
            act.activation(t5, t6, ACT.Sqrt).then_inc(sem("lru_act"), 1)
            act.wait_ge(sem("lru_dve"), 5)
            act.activation(t2, t1, ACT.Sigmoid, scale=2.0 * math.sqrt(2.0 / math.pi)).then_inc(sem("lru_act"), 1)

        def rwkv_in_dve(dve):
            def S(ins, name="dve_step"):
                step(dve, ins, name)
            S(dve.tensor_tensor(ps, pj[:, 8:22, 3:259], pj[:, 8:22, 4:260], SUB))
            for c in range(14):
                S(dve.scalar_tensor_tensor(ps[:, c, :], ps[:, c, :], vec("e_shift_mu", c), pj[:, 8 + c, 4:260],
                                           MUL, ADD), "rw_shift" if c == 13 else "dve_step")
            dve.wait_ge(sem("rw_act2"), 1)
            S(dve.tensor_scalar(t2, t2, -EXP_M_HALF, None, MUL))
            for c in range(4):
                S(dve.tensor_tensor_scan(t4[:, c, :], cst("scanmask"), t2[:, c, :], 0.0, MUL, ADD))
            S(dve.tensor_tensor(t2, t4, t2, SUB))
            r, k, v = ps[:, 0:4, :], ps[:, 4:8, :], ps[:, 8:12, :]
            for c in range(4):
                S(dve.tensor_scalar(t5[:, c, :], k[:, c, :], vec("e_k_k", c), None, MUL))
            S(dve.tensor_tensor(t6, t5, t5, MUL), "rw_kk2")
            dve.wait_ge(sem("rw_norm"), 1)
            S(dve.tensor_scalar(t6, t6, 1e-12, None, MAX))
            S(dve.reciprocal(t6, t6))
            S(dve.tensor_tensor(t5, t5, t6, MUL))
            for c in range(4):
                S(dve.tensor_scalar(t1[:, c, :], t3[:, c, :], vec("e_k_a", c), omka[:, c:c + 1], MUL, ADD))
            S(dve.tensor_tensor(t1, t1, k, MUL))
            S(dve.tensor_tensor(t6, r, t1, MUL))
            for c in range(4):
                S(dve.tensor_scalar(t6[:, c, :], t6[:, c, :], vec("e_r_k", c), None, MUL),
                  "rw_bonus" if c == 3 else "dve_step")
            dve.wait_ge(sem("rw_bonus_ps"), 1)
            S(dve.tensor_tensor(bon, psum[:, 0:2, :].rearrange("p b (c t) -> p (b c) t", c=2), v, MUL))
            dve.wait_ge(sem("rw_exps"), 1)
            tv = [t.rearrange("p c (j t) -> p c j t", j=NT) for t in (t2, t5, t6, r)]
            for j in range(NT):
                S(dve.tensor_tensor(PR[:, :, j, 0, :], tv[0][:, :, j, :], tv[1][:, :, j, :], MUL))
                S(dve.tensor_tensor(PR[:, :, j, 1, :], tv[2][:, :, j, :], tv[3][:, :, j, :], MUL))
            S(dve.tensor_tensor(t3, t3, t5, MUL))
            S(dve.tensor_tensor(Bm, t3, t4, MUL))
            S(dve.tensor_tensor(Km, t1, t4, MUL))
            S(dve.tensor_copy(eC, t6[:, :, CH - 1:T:CH]))
            ada_mods_dve(dve, 0)
            S(dve.memset(Ms, 0.0), "rw_fm")

        def rwkv_in_act(act):
            act.wait_ge(sem("rw_shift"), 1)
            act.activation(arena[0:64, 0:256], ps[0:64, 12, :], ACT.Tanh)
            act.activation(ar(256, 256), ps[:, 13, :], ACT.Sigmoid).then_inc(sem("rw_act1"), 1)
            act.wait_ge(sem("rw_lora"), 1)
            for q, (t, b) in enumerate(((t2, "e_w0"), (t3, "e_a0"))):
                for c in range(4):
                    act.activation(t[:, c, :], psum[:, 2 * q + c // 2, (c % 2) * T:(c % 2) * T + T], ACT.Sigmoid,
                                   bias=vec(b, c))
            act.activation(gg, psum[:, 4:6, :].rearrange("p b (c t) -> p (b c) t", c=2), ACT.Copy)\
               .then_inc(sem("rw_act2"), 1)
            act.wait_ge(sem("rw_n2"), 1)
            act.activation(t6, psum[:, 2:4, :].rearrange("p b (c t) -> p (b c) t", c=2), ACT.Sqrt)\
               .then_inc(sem("rw_norm"), 1)
            ada_rows_act(act, 0)
            act.wait_ge(sem("rw_bonus_ps"), 1)
            act.activation(t2, t2, ACT.Exp)
            step(act, act.activation(t6, t4, ACT.Exp), "act_step")
            act.activation(t4, t4, ACT.Exp, scale=-1.0).then_inc(sem("rw_exps"), 1)

        def rwkv_in_pe(pe):
            pe.wait_ge(sem("rw_act1"), 1)
            w2a2 = mat("w2a2")
            for c in range(4):
                at = (c % 2) * T
                pe.matmul(psum[:, c // 2, at:at + T], w2a2[0:64, c * P:(c + 1) * P], arena[0:64, 0:256],
                          start=True, stop=True)
                pe.matmul(psum[:, 2 + c // 2, at:at + T], w2a2[64:128, c * P:(c + 1) * P], ps[64:128, 12, :],
                          start=True, stop=True)
                ins = pe.matmul(psum[:, 4 + c // 2, at:at + T], mat("g2")[:, c * P:(c + 1) * P], ar(256, 256),
                                start=True, stop=True)
            ins.then_inc(sem("rw_lora"), 1)
            ada_pe(pe, 0, ADA_0B, ADA_SLOTS)
            for src, bank, wait, done in ((t6, 2, "rw_kk2", "rw_n2"), (t6, 0, "rw_bonus", "rw_bonus_ps")):
                pe.wait_ge(sem(wait), 1)
                for b in range(2):
                    ins = pe.matmul(psum[:, bank + b, :], cst("headones"),
                                    src[:, 2 * b:2 * b + 2, :].rearrange("p c t -> p (c t)"), start=True, stop=True)
                ins.then_inc(sem(done), 1)
            ada_tr_pe(pe, 0)

        def hd(h):
            return 64 * (h % 2), h // 2

        def yo(h):
            return (h % 2) * 256 + (h // 2) * 64

        def rwkv_tile_pe(pe, j):
            if j == 0:
                pe.wait_ge(sem("rw_fm"), 1)
            else:
                pe.wait_ge(sem("seq_m"), 2 * j)
            tk = slice(j * P, (j + 1) * P)
            for a in range(4):
                for c in range(4):
                    src = (ps[:, 8 + c, tk], Bm[:, c, tk], Km[:, c, tk], PR[:, c, j, 0, :])[a]
                    ins = pe.transpose(psum[:, a, c * P:(c + 1) * P], src, ident)
            ins.then_inc(sem("rw_tm"), 1)
            for h in range(8):
                pb, c = hd(h)
                if h >= 4 or j:
                    pe.wait_ge(sem("rw_qev"), 8 * j + h - 3)
                rhs = PR[pb:pb + 64, c, j, :, :].rearrange("p w t -> p (w t)")
                pe.matmul(psum[:, 4 + h % 4, 0:256], Bm[pb:pb + 64, c, tk], rhs, start=True, stop=True)
                pe.matmul(psum[:, 4 + h % 4, 256:512], Km[pb:pb + 64, c, tk], rhs, start=True, stop=True)\
                  .then_inc(sem("rw_q"), 1)
            pe.wait_ge(sem("rw_tmev"), j + 1)
            for l in range(6):
                for g in range(2):
                    n = (6 * j + l) * 2 + g
                    pe.wait_ge(sem("inv_a"), n + 1)
                    for h in range(4 * g, 4 * g + 4):
                        o = (h % 4) * P
                        ins = pe.matmul(psum[:, 4 * g, o:o + P], AbT[:, h, :], X[:, h, :], start=True, stop=True)
                    ins.then_inc(sem("inv_y"), 1)
                for g in range(2):
                    if l == 0:
                        break
                    n = (5 * j + l - 1) * 2 + g
                    pe.wait_ge(sem("inv_yc"), n + 1)
                    for h in range(4 * g, 4 * g + 4):
                        o = (h % 4) * P
                        pe.matmul(psum[:, 4 * g + 1, o:o + P], XT[:, h, :], Yb[:, h, :], start=True, stop=True)
                        ins = pe.matmul(psum[:, 4 * g + 2, o:o + P], Yb[:, h, :], XT[:, h, :], start=True, stop=True)
                    ins.then_inc(sem("inv_xy"), 1)
            pe.wait_ge(sem("inv_x"), j + 1)
            for h in range(8):
                ins = pe.matmul(psum[:, 3, h * 64:h * 64 + 64], Q4[:, h, 2, :], Vt[:, h * 64:h * 64 + 64],
                                start=True, stop=True)
            ins.then_inc(sem("rw_gv"), 1)
            for h in range(8):
                pb, c = hd(h)
                ins = pe.matmul(psum[pb:pb + 64, 0, c * P:(c + 1) * P], Pt[:, h * 64:h * 64 + 64], XT[:, h, :],
                                start=True, stop=True)
            pe.wait_ge(sem("rw_gvev"), j + 1)
            for h in range(8):
                ins = pe.matmul(psum[:, 7, yo(h):yo(h) + 64], XT[:, h, :], GVb[:, h * 64:h * 64 + 64],
                                start=True, stop=True)
            ins.then_inc(sem("rw_uw"), 1)
            pe.wait_ge(sem("rw_uwev"), j + 1)
            for cc in range(2):
                n, tb = 2 * j + cc, CH * cc
                if n:
                    pe.wait_ge(sem("seq_m"), n)
                for h in range(8):
                    pb, c = hd(h)
                    ins = pe.matmul(psum[tb:tb + 64, 1 + 5 * (h % 2), c * 64:c * 64 + 64],
                                    WTb[pb:pb + 64, c, tb:tb + 64], Ms[pb:pb + 64, c, :], start=True, stop=True)
                ins.then_inc(sem("seq_y"), 1)
                for h in range(8):
                    pb, c = hd(h)
                    pe.matmul(psum[pb:pb + 64, 2 + h % 2, c * 64:c * 64 + 64], Ms[pb:pb + 64, c, :],
                              PR[pb:pb + 64, c, j, 1, tb:tb + 64], start=True, stop=True)
                pe.wait_ge(sem("seq_yv"), n + 1)
                for h in range(8):
                    pb, c = hd(h)
                    hs, ys = slice(h * 64, h * 64 + 64), slice(yo(h), yo(h) + 64)
                    o = psum[pb:pb + 64, 4, c * 64:c * 64 + 64]
                    pe.matmul(o, Ysb[tb:tb + 64, ys], Q4[tb:tb + 64, h, 1, tb:tb + 64], start=True, stop=False)
                    pe.matmul(o, Vt[tb:tb + 64, hs], Q4[tb:tb + 64, h, 3, tb:tb + 64], start=False, stop=True)
                    o = psum[pb:pb + 64, 5, c * 64:c * 64 + 64]
                    pe.matmul(o, Bt[tb:tb + 64, hs], Ysb[tb:tb + 64, ys], start=True, stop=False)
                    ins = pe.matmul(o, Kt[tb:tb + 64, hs], Vt[tb:tb + 64, hs], start=False, stop=True)
                ins.then_inc(sem("seq_o"), 1)

        def rwkv_tile_act(act, j):
            act.wait_ge(sem("rw_tm"), j + 1)
            if j:
                act.wait_ge(sem("seq_m"), 2)
            for a in range(4):
                ins = act.activation(tm4[a], psum[:, a, :], ACT.Copy)
            ins.then_inc(sem("rw_tmev"), 1)
            for l in range(1, 6):
                for g in range(2):
                    act.wait_ge(sem("inv_y"), (6 * j + l) * 2 + g + 1)
                    act.activation(Yb[:, 4 * g:4 * g + 4, :], psum[:, 4 * g, :].rearrange("p (h t) -> p h t", h=4),
                                   ACT.Copy).then_inc(sem("inv_yc"), 1)
            act.wait_ge(sem("rw_gv"), j + 1)
            act.activation(GVb, psum[:, 3, :], ACT.Copy).then_inc(sem("rw_gvev"), 1)
            act.wait_ge(sem("rw_uw"), j + 1)
            act.activation(WTb, psum[:, 0, :].rearrange("p (c t) -> p c t", c=4), ACT.Copy)
            act.activation(Ub, psum[:, 7, :], ACT.Copy).then_inc(sem("rw_uwev"), 1)

        def rwkv_tile_dve(dve, j):
            def S(ins, name="dve_step"):
                step(dve, ins, name)
            for h in range(8):
                dve.wait_ge(sem("rw_q"), 8 * j + h + 1)
                S(dve.tensor_tensor(Q4[:, h, :, :].rearrange("p m t -> p (m t)"), psum[:, 4 + h % 4, :], cst("mask4"),
                                    MUL), "rw_qev")
            eye = ident.unsqueeze(1).to_broadcast([P, 8, P])
            S(dve.tensor_copy(X, eye))
            S(dve.tensor_copy(XT, eye))
            for l in range(6):
                lv = cst("level")[:, l * P:(l + 1) * P].unsqueeze(1).to_broadcast([P, 4, P])
                for g in range(2):
                    hs = slice(4 * g, 4 * g + 4)
                    S(dve.tensor_tensor(AbT[:, hs, :], Q4[:, hs, 0, :], lv, MUL), "inv_a")
                for g in range(2):
                    hs = slice(4 * g, 4 * g + 4)
                    if l == 0:
                        dve.wait_ge(sem("inv_y"), (6 * j + l) * 2 + g + 1)
                        S(dve.tensor_tensor(X[:, hs, :], X[:, hs, :],
                                            psum[:, 4 * g, :].rearrange("p (h t) -> p h t", h=4), SUB))
                        S(dve.tensor_tensor(XT[:, hs, :], XT[:, hs, :], AbT[:, hs, :], SUB))
                        continue
                    dve.wait_ge(sem("inv_xy"), (5 * j + l - 1) * 2 + g + 1)
                    for m, t in ((1, X), (2, XT)):
                        S(dve.tensor_tensor(t[:, hs, :], t[:, hs, :],
                                            psum[:, 4 * g + m, :].rearrange("p (h t) -> p h t", h=4), SUB),
                          "inv_x" if (l, g, m) == (5, 1, 2) else "dve_step")
            for cc in range(2):
                n, tb = 2 * j + cc, CH * cc
                rows = slice(tb, tb + CH)
                dve.wait_ge(sem("seq_y"), n + 1)
                for q, bank in enumerate((1, 6)):
                    qs = slice(256 * q, 256 * q + 256)
                    S(dve.scalar_tensor_tensor(Ysb[rows, qs], psum[rows, bank, 0:256], -1.0, Ub[rows, qs], MUL, SUB),
                      "seq_yv" if q else "dve_step")
                dve.wait_ge(sem("seq_o"), n + 1)
                on = oT[:, :, n * CH:(n + 1) * CH]
                S(dve.tensor_copy(on, psum[:, 4, 0:256].rearrange("p (c t) -> p c t", c=4)))
                for q in range(2):
                    hr = slice(64 * q, 64 * q + 64)
                    S(dve.tensor_tensor(on[hr], on[hr], psum[hr, 2 + q, 0:256].rearrange("p (c t) -> p c t", c=4), ADD))
                S(dve.tensor_tensor(Ms, Ms, psum[:, 5, 0:256].rearrange("p (c v) -> p c v", c=4), ADD))
                S(dve.tensor_tensor(Ms, Ms, eC[:, :, n:n + 1].to_broadcast([P, 4, 64]), MUL), "seq_m")

        def rwkv_out_pe(pe):
            pe.wait_ge(sem("seq_m"), 4)
            for b in range(2):
                ins = pe.matmul(psum[:, b, :], cst("headones"), oT[:, 2 * b:2 * b + 2, :].rearrange("p c t -> p (c t)"),
                                start=True, stop=True)
            ins.then_inc(sem("gn_mean"), 1)
            pe.wait_ge(sem("gn_sq"), 1)
            for b in range(2):
                ins = pe.matmul(psum[:, 2 + b, :], cst("headones"),
                                t1[:, 2 * b:2 * b + 2, :].rearrange("p c t -> p (c t)"), start=True, stop=True)
            ins.then_inc(sem("gn_var"), 1)
            pe.wait_ge(sem("mix_fm"), 1)
            out_proj_pe(pe, FIRST["e_out"], yT, NT)

        def rwkv_out_dve(dve):
            def S(ins, name="dve_step"):
                step(dve, ins, name)
            dve.wait_ge(sem("gn_mean"), 1)
            S(dve.scalar_tensor_tensor(oT, psum[:, 0:2, :].rearrange("p b (c t) -> p (b c) t", c=2), -1.0 / 64, oT,
                                       MUL, ADD))
            S(dve.tensor_tensor(t1, oT, oT, MUL), "gn_sq")
            dve.wait_ge(sem("gn_var"), 1)
            S(dve.tensor_scalar(t2, psum[:, 2:4, :].rearrange("p b (c t) -> p (b c) t", c=2), 1.0 / 64, 64e-5, MUL, ADD),
              "gn_ms")
            dve.wait_ge(sem("gn_std"), 1)
            S(dve.reciprocal(t2, t2))
            S(dve.tensor_tensor(oT, oT, t2, MUL))
            for c in range(4):
                S(dve.tensor_scalar(oT[:, c, :], oT[:, c, :], vec("e_gn_w", c), vec("e_gn_b", c), MUL, ADD))
            S(dve.tensor_tensor(oT, oT, bon, ADD))
            S(dve.tensor_tensor(yT[:, 4:8, :], oT, gg, MUL), "mix_fm")
            slot_used(dve, FIRST["e_out"] + 2)
            add_tokens(dve, x_tm)

        def rwkv_out_act(act):
            act.wait_ge(sem("gn_ms"), 1)
            act.activation(t2, t2, ACT.Sqrt).then_inc(sem("gn_std"), 1)

        def tm_proj_pe(pe, tag, n0, widths, lhs, tiles, nk=KD, base=0):
            for s, w in enumerate(widths):
                slot_ready(pe, n0 + s)
                if base + s >= 2:
                    pe.wait_ge(sem(f"{tag}_ev"), base + s - 1)
                for j in range(tiles[s]):
                    for k in range(nk):
                        ins = pe.matmul(psum[:, 4 * ((base + s) % 2) + j, 0:w], lhs[:, k, j * P:(j + 1) * P],
                                        slot_of[(n0 + s) % RING][:, k * w:(k + 1) * w],
                                        start=(k == 0), stop=(k == nk - 1))
                ins.then_inc(w_used[(n0 + s) % RING], 1)

        def tm_proj_act(act, tag, n0, widths, dst, tiles, after):
            at = 0
            for s, w in enumerate(widths):
                slot_used(act, n0 + s)
                b = 4 * (s % 2)
                act.activation(dst[:, 0:tiles[s], at:at + w], psum[:, b:b + tiles[s], 0:w], ACT.Copy)\
                   .then_inc(sem(f"{tag}_ev"), 1)
                at += w
                for n in after.get(s, ()):
                    root_act(act, n)

        hn_ss = sm("hn_ss", 64)

        def head_norm_dve(dve, v, sq, groups, width, gain):
            ssq = hn_ss[:, 0:groups]
            step(dve, dve.tensor_tensor(sq, v, v, MUL), "dve_step")
            step(dve, dve.tensor_reduce(ssq, sq, AX.X, ADD), "dve_step")
            rstd = inverse_root_dve(dve, ssq, width)
            step(dve, dve.tensor_tensor(v, v, rstd.unsqueeze(2).to_broadcast([P, groups, width]), MUL), "dve_step")
            if gain is not None:
                step(dve, dve.tensor_tensor(v, v, gain.unsqueeze(1).to_broadcast([P, groups, width]), MUL), "dve_step")

        def rope_dve(dve, x1, x2, cos, sin, tmp, shape):
            a, b = tmp
            step(dve, dve.tensor_tensor(a, x1, sin, MUL), "dve_step")
            step(dve, dve.tensor_tensor(b, x2, sin, MUL), "dve_step")
            step(dve, dve.tensor_tensor(x1, x1, cos, MUL), "dve_step")
            step(dve, dve.tensor_tensor(x2, x2, cos, MUL), "dve_step")
            step(dve, dve.tensor_tensor(x1, x1, b, SUB), "dve_step")
            step(dve, dve.tensor_tensor(x2, x2, a, ADD), "dve_step")

        qkv = ar(6144, 6144, "p (j n) -> p j n", j=NT)
        dQT = ar(12288, 2048, "p (c t) -> p c t", c=8)
        dKT = ar(14336, 2048, "p (c t) -> p c t", c=8)
        dS = ar(16384, 2048, "p (g k) -> p g k", g=8)
        dsq = ar(18432, 2048)
        dA = ar(20480, 1024, "p (h k) -> p h k", h=4)
        dAT = ar(21504, 1024, "p (h b q) -> p h b q", h=4, b=2)
        dO = ar(22528, 2048, "p (j n) -> p j n", j=NT)
        pos_i = sb("pos_i", NT, i32)
        rope_c, rope_s = sm("rope_c", 16), sm("rope_s", 16)
        rp_a, rp_k, rp_r = sm("rp_a", 16), sm("rp_k", 16), sm("rp_r", 16)
        posf = sm("posf", 2)
        lam2, nlam = sm("lam2", 2), sm("nlam", 1)
        subg = sm("subg", 128)
        d_mx, d_rs = sm("d_mx", 8), sm("d_rs", 8)
        junk = sm("junk", 64)

        def diff_cols_dve(dve):
            def S(ins, name="dve_step"):
                step(dve, ins, name)
            S(dve.tensor_copy(posf, pos_i[:, :]))
            for j in range(NT):
                S(dve.tensor_scalar(rp_a[:, 8 * j:8 * j + 8], cst("freq"), posf[:, j:j + 1], None, MUL))
            magic = 1.5 * 2.0 ** 23
            S(dve.tensor_scalar(rp_k, rp_a, 1.0 / (2.0 * math.pi), magic, MUL, ADD))
            S(dve.tensor_scalar(rp_k, rp_k, -magic, None, ADD))
            c1 = 6.28125
            c2 = float(np.float32(2.0 * math.pi - c1))
            c3 = 2.0 * math.pi - c1 - c2
            S(dve.scalar_tensor_tensor(rp_r, rp_k, -c1, rp_a, MUL, ADD))
            S(dve.scalar_tensor_tensor(rp_r, rp_k, -c2, rp_r, MUL, ADD))
            S(dve.scalar_tensor_tensor(rp_r, rp_k, -c3, rp_r, MUL, ADD))
            S(dve.tensor_scalar(rp_r, rp_r, 3.1415925, -3.1415925, MIN, MAX))
            S(dve.tensor_scalar(rp_a, rp_r, -1.0, None, MUL))
            S(dve.tensor_tensor(rp_a, rp_a, rp_r, MAX))
            S(dve.tensor_scalar(rp_a, rp_a, -1.0, math.pi / 2, MUL, ADD))
            for n, (a, b) in enumerate((("o_lambda_q1", "o_lambda_k1"), ("o_lambda_q2", "o_lambda_k2"))):
                S(dve.tensor_tensor_reduce(junk, mat(a), mat(b), 1.0, 0.0, MUL, ADD, lam2[:, n:n + 1]),
                  "df_cols" if n else "dve_step")
            S(dve.tensor_scalar(subg, mat("o_subln"), 1.0 - LAMBDA_INIT, None, MUL))
            dve.wait_ge(sem("df_sin"), 1)
            S(dve.tensor_tensor(nlam, lam2[:, 1:2], lam2[:, 0:1], SUB))
            S(dve.tensor_scalar(nlam, nlam, -LAMBDA_INIT, None, ADD))

        def diff_cols_act(act):
            act.wait_ge(sem("df_cols"), 1)
            act.activation(rope_s, rp_r, ACT.Sin)
            act.activation(rope_c, rp_a, ACT.Sin)
            act.activation(lam2, lam2, ACT.Exp).then_inc(sem("df_sin"), 1)

        def diff_dve(dve):
            def S(ins, name="dve_step"):
                step(dve, ins, name)
            diff_cols_dve(dve)
            ada_z_dve(dve)
            for part, name in enumerate(("o_q_norm", "o_k_norm")):
                dve.wait_ge(sem("qkv_ev"), -(-(part + 1) * D // COLS))
                for j in range(NT):
                    v = qkv[:, j, part * D:(part + 1) * D].rearrange("p (g d) -> p g d", g=16)
                    head_norm_dve(dve, v, dsq[:, 0:D].rearrange("p (g d) -> p g d", g=16), 16, 64, mat(name))
                    cos, sin = [t[:, 8 * j:8 * j + 8].unsqueeze(1).to_broadcast([P, 16, 8]) for t in (rope_c, rope_s)]
                    tmp = [dsq[:, 128 * i:128 * i + 128].rearrange("p (g d) -> p g d", g=16) for i in range(2)]
                    rope_dve(dve, v[:, :, 0:8], v[:, :, 8:16], cos, sin, tmp, None)
            dve.sem_inc(sem("df_rope"), 1)
            dve.wait_ge(sem("heads_tr"), 2)
            S(dve.tensor_copy(dKT, psum[:, 4:8, :].rearrange("p b (c t) -> p (b c) t", c=2)), "k_fm")
            for n in range(4):
                j, half = n // 2, n % 2
                w = P * (j + 1)
                src = psum[:, 0:4, :].rearrange("p b (u k) -> p (b u) k", u=2)
                dve.wait_ge(sem("df_s"), n + 1)
                mask = cst("causal").unsqueeze(1).to_broadcast([P, 8, P])
                S(dve.scalar_tensor_tensor(dS[:, :, w - P:w], src[:, :, w - P:w], 0.125, mask, MUL, ADD))
                if j:
                    S(dve.tensor_scalar(dS[:, :, 0:P], src[:, :, 0:P], 0.125, None, MUL))
                S(dve.tensor_reduce(d_mx, dS[:, :, 0:w], AX.X, MAX))
                S(dve.tensor_scalar(d_mx, d_mx, -1.0, None, MUL), "df_max")
                dve.wait_ge(sem("df_exp"), n + 1)
                S(dve.reciprocal(d_rs, d_rs))
                S(dve.tensor_scalar(d_rs[:, 4:8], d_rs[:, 4:8], nlam[:, 0:1], None, MUL))
                S(dve.tensor_tensor(dS[:, :, 0:w], dS[:, :, 0:w], d_rs.unsqueeze(2).to_broadcast([P, 8, w]), MUL))
                S(dve.tensor_tensor(dA[:, :, 0:w], dS[:, 0:4, 0:w], dS[:, 4:8, 0:w], ADD), "df_attn")
                dve.wait_ge(sem("df_pv"), n + 1)
                S(dve.tensor_copy(dO[:, j, 512 * half:512 * half + 512], psum[:, 6, :]), "df_o")
            v = ar(22528, 2048, "p (g d) -> p g d", g=16)
            head_norm_dve(dve, v, dsq.rearrange("p (g d) -> p g d", g=16), 16, 128, subg)
            dve.sem_inc(sem("df_on"), 1)
            ada_mods_dve(dve, 1)
            dve.wait_ge(sem("mix_tr"), 1)
            S(dve.tensor_copy(hT[:, :, 0:T], psum[:, 0:4, :].rearrange("p b (c t) -> p (b c) t", c=2)), "mix_fm")
            slot_used(dve, FIRST["o_out"] + 2)
            add_tokens(dve, x_tm)

        def diff_act(act):
            diff_cols_act(act)
            tm_proj_act(act, "qkv", FIRST["qkv"], [COLS] * (QKV // COLS), qkv, [NT] * (QKV // COLS),
                        {2: [16] * NT, 5: [16] * NT})
            act.wait_ge(sem("heads_tr"), 1)
            act.activation(dQT, psum[:, 0:4, :].rearrange("p b (c t) -> p (b c) t", c=2), ACT.Copy)\
               .then_inc(sem("q_fm"), 1)
            for n in range(4):
                w = P * (n // 2 + 1)
                act.wait_ge(sem("df_max"), n + 1)
                for g in range(8):
                    ins = act.activation(dS[:, g, 0:w], dS[:, g, 0:w], ACT.Exp, bias=d_mx[:, g:g + 1],
                                         accum_out=d_rs[:, g:g + 1])
                ins.then_inc(sem("df_exp"), 1)
                act.wait_ge(sem("df_t"), n + 1)
                src = psum[:, 4:6, :].rearrange("p b (h k q) -> p (b h) k q", h=2, k=2)
                nb = n // 2 + 1
                act.activation(dAT[:, :, 0:nb, :], src[:, :, 0:nb, :], ACT.Copy).then_inc(sem("df_tev"), 1)
            ada_rows_act(act, 1)
            root_act(act, 16)

        def diff_pe(pe):
            pe.wait_ge(sem("norm_hT"), 3)
            tm_proj_pe(pe, "qkv", FIRST["qkv"], [COLS] * (QKV // COLS), hT, [NT] * (QKV // COLS))
            pe.wait_ge(sem("df_rope"), 1)
            pe.wait_ge(sem("qkv_ev"), QKV // COLS)
            for part in range(2):
                for c in range(8):
                    for j in range(NT):
                        at = (c % 2) * T + j * P
                        ins = pe.transpose(psum[:, 4 * part + c // 2, at:at + P],
                                           qkv[:, j, part * D + c * P:part * D + (c + 1) * P], ident)
                ins.then_inc(sem("heads_tr"), 1)
            pe.wait_ge(sem("q_fm"), 1)
            pe.wait_ge(sem("k_fm"), 1)
            for n in range(4):
                j, half = n // 2, n % 2
                if n:
                    pe.wait_ge(sem("df_o"), n)
                for part in range(2):
                    for hl in range(4):
                        h, pb = 4 * half + hl, 64 * part
                        at = (hl % 2) * T
                        ins = pe.matmul(psum[:, 2 * part + hl // 2, at:at + P * (j + 1)],
                                        dQT[pb:pb + 64, h, j * P:(j + 1) * P], dKT[pb:pb + 64, h, 0:P * (j + 1)],
                                        start=True, stop=True)
                ins.then_inc(sem("df_s"), 1)
                ada_pe(pe, 1, ADA_SLOTS * n // 4, ADA_SLOTS * (n + 1) // 4)
                pe.wait_ge(sem("df_attn"), n + 1)
                for hl in range(4):
                    for b in range(j + 1):
                        at = (hl % 2) * T + b * P
                        ins = pe.transpose(psum[:, 4 + hl // 2, at:at + P], dA[:, hl, b * P:(b + 1) * P], ident)
                ins.then_inc(sem("df_t"), 1)
                pe.wait_ge(sem("df_tev"), n + 1)
                for hl in range(4):
                    h = 4 * half + hl
                    for b in range(j + 1):
                        ins = pe.matmul(psum[:, 6, hl * P:(hl + 1) * P], dAT[:, hl, b, :],
                                        qkv[:, b, 2 * D + h * P:2 * D + (h + 1) * P], start=(b == 0), stop=(b == j))
                ins.then_inc(sem("df_pv"), 1)
            ada_tr_pe(pe, 1)
            pe.wait_ge(sem("df_on"), 1)
            for c in range(8):
                for j in range(NT):
                    at = (c % 2) * T + j * P
                    ins = pe.transpose(psum[:, c // 2, at:at + P], dO[:, j, c * P:(c + 1) * P], ident)
            ins.then_inc(sem("mix_tr"), 1)
            pe.wait_ge(sem("mix_fm"), 2)
            out_proj_pe(pe, FIRST["o_out"], hT, NT)

        logit = sm("logit", 16)
        top = sm("top", 16)
        topf = sm("topf", 4)
        gts = sm("gts", 4)
        oneh = sm("oneh", 8)
        over, rank = sm("over", 8), sm("rank", 8)
        topi = sb("topi", 16, u32)
        plan_i = ar(9888, 16).bitcast(i32)
        plan_f = sm("plan_f", 16)
        xe = ar(6144, KD * CAP, "p (k s) -> p k s", k=KD)
        pick = ar(7168, NT * CAP, "p (j s) -> p j s", j=NT)
        give = ar(7424, NT * CAP, "p (j s) -> p j s", j=NT)
        giveT = ar(7680, NT * CAP, "p (j t) -> p j t", j=NT)
        oute = ar(7936, D)
        before = ar(8960, P)
        NV = MAX_VISITS + 1
        sel, pos, wgt = [ar(9088 + 16 * i, 16, "p (e j) -> p e j", j=NT) for i in range(3)]
        vsel, vpos, vwgt = [ar(9152 + 2 * NV * i, 2 * NV) for i in range(3)]
        xe_hi, xe_lo = [parts(27648 + D * i, D, "p (k s) -> p k s", k=KD) for i in range(2)]
        experts = {"name": "moe", "ready": e_ready, "used": e_used}
        e_silu, e_h = [ar(10240 + 2 * CAP * i, 2 * CAP, "p (b t) -> p b t", b=2) for i in range(2)]
        eh_hi, eh_lo = [parts(10752 + 2 * CAP * i, 2 * CAP, "p (b t) -> p b t", b=2) for i in range(2)]
        tot = ar(9856, 8)
        pick_tmp = ar(9872, 16)

        def moe_count(eng):
            eng.wait_ge(sem("moe_plan"), 1)
            return eng.value_load(plan_i[0:1, 0:1], min_val=N_EXP, max_val=MAX_VISITS)

        def moe_gather_pe(pe, v):
            pe.wait_ge(sem("moe_pick"), v + 1)
            for half in range(2):
                for c in range(4):
                    k = 4 * half + c
                    for j in range(NT):
                        ins = pe.matmul(psum[:, 6 + half, c * CAP:(c + 1) * CAP], xn[:, j, k * P:(k + 1) * P],
                                        pick[:, j, :], start=(j == 0), stop=(j == NT - 1))
                ins.then_inc(sem("moe_gather"), 1)

        def moe_gate_up_pe(pe, at, i):
            r, turn, blk = at
            b = i % 2
            pe.wait_ge(sem("moe_w_lo"), blk + 1)
            if i >= 2:
                pe.wait_ge(sem("moe_h"), blk - 1)
            dst = psum[:, 6 + b, 0:2 * FBLK].rearrange("p (g n) -> p g n", g=2)
            for k in range(KD):
                hi, lo = [w[:, b, 0:2 * D].rearrange("p (g c n) -> p g c n", g=2, c=KD)[:, :, k, :] for w in (w_hi, w_lo)]
                pe.matmul(dst, xe_hi[:, k, :], hi, start=(k == 0), stop=False)
                pe.matmul(dst, xe_hi[:, k, :], lo, start=False, stop=False)
                ins = pe.matmul(dst, xe_lo[:, k, :], hi, start=False, stop=(k == KD - 1))
            if i < NT:
                ins = pe.transpose(psum[:, 6 + b, 3 * P:4 * P], give[:, i, :], ident)
            ins.then_inc(sem("moe_gu"), 1)

        def moe_transpose_pe(pe, at, i):
            r, turn, blk = at
            pe.wait_ge(sem("moe_h32"), blk + 1)
            pe.transpose(psum[:, 6 + i % 2, 2 * P:3 * P], e_h[:, i % 2, :], ident).then_inc(sem("moe_tr"), 1)

        def moe_down_pe(pe, at, i):
            r, turn, blk = at
            b = i % 2
            pe.wait_ge(sem("moe_h"), blk + 1)
            pe.wait_ge(e_used[r], turn + 1)
            for hf in range(2):
                dst = psum[:, 4 + hf, :]
                hi, lo = [d[:, i % 4, hf * 512:(hf + 1) * 512] for d in (d_hi, d_lo)]
                pe.matmul(dst, eh_hi[:, b, :], hi, start=(i == 0), stop=False)
                pe.matmul(dst, eh_hi[:, b, :], lo, start=False, stop=False)
                ins = pe.matmul(dst, eh_lo[:, b, :], hi, start=False, stop=(i == NB_EXP - 1))
            ins.then_inc(sem("moe_dn"), 1)

        def moe_pe(pe):
            pe.wait_ge(sem("norm_hT"), 4)
            for j in range(NT):
                for k in range(KD):
                    ins = pe.matmul(psum[:, 6, 8 * j:8 * j + 8], hT[:, k, j * P:(j + 1) * P],
                                    mat("router")[:, 8 * k:8 * k + 8], start=(k == 0), stop=(k == KD - 1))
            ins.then_inc(sem("moe_routed"), 1)
            pe.wait_ge(sem("moe_sel"), 1)
            for j in range(NT):
                for hf in range(2):
                    pe.matmul(psum[:, 2 * j + hf, :], giveT[:, 0, :], x_tm[:, j, hf * 512:(hf + 1) * 512],
                              start=True, stop=False)
            pe.matmul(psum[:, 7, 0:8], before, sel[:, :, 0], start=True, stop=True)
            pe.matmul(psum[:, 7, 8:16], cst("ones"), sel[:, :, 0], start=True, stop=False)
            pe.matmul(psum[:, 7, 8:16], before, sel[:, :, 1], start=False, stop=True)
            for j in range(NT):
                ins = pe.matmul(psum[:, 7, 16:24], cst("ones"), sel[:, :, j], start=(j == 0), stop=(j == NT - 1))
            ins.then_inc(sem("moe_routed"), 1)
            n_visits = moe_count(pe)
            moe_gather_pe(pe, 0)
            with pe.Fori(0, n_visits) as v:
                def gu(i, it=0):
                    moe_gate_up_pe(pe, place(0, v * G_EXP, v * NB_EXP, i, it), i)

                def tr(i, it=0):
                    moe_transpose_pe(pe, place(0, v * G_EXP, v * NB_EXP, i, it), i)

                def dn(i, it=0):
                    moe_down_pe(pe, place(0, v * G_EXP, v * NB_EXP, i, it), i)

                pe.wait_ge(sem("moe_xe"), v + 1)
                gu(0)
                gu(1)
                tr(0)
                gu(2)
                tr(1)
                dn(0)
                with pe.Fori(0, G_EXP - 1) as it:
                    for u in range(RING):
                        gu(3 + u, it)
                        tr(2 + u, it)
                        dn(1 + u, it)
                gu(NB_EXP - 1)
                for i in range(NB_EXP - 3, NB_EXP):
                    if i + 1 < NB_EXP:
                        tr(i + 1)
                    dn(i)
                moe_gather_pe(pe, v + 1)
                pe.wait_ge(sem("moe_out_act"), v + 1)
                pe.wait_ge(sem("moe_out_dve"), v + 1)
                for j in range(NT):
                    for hf in range(2):
                        pe.matmul(psum[:, 2 * j + hf, :], giveT[:, j, :], oute[:, hf * 512:(hf + 1) * 512],
                                  start=False, stop=False)
            for j in range(NT):
                for hf in range(2):
                    ins = pe.matmul(psum[:, 2 * j + hf, :], ident, x_tm[:, j, hf * 512:(hf + 1) * 512],
                                    start=False, stop=True)
            ins.then_inc(sem("moe_sum"), 1)

        def moe_xe_act(act, v):
            act.wait_ge(sem("moe_gather"), 2 * v + 2)
            for dst in (xe, xe_hi):
                for c in range(4, 8):
                    ins = act.activation(dst[:, c, :], psum[:, 7, (c - 4) * CAP:(c - 3) * CAP], ACT.Copy,
                                         scale=vec("o_ln_ffn", c))
            ins.then_inc(sem("moe_xe_hi"), 1)

        def moe_silu_act(act, at, i):
            r, turn, blk = at
            act.wait_ge(sem("moe_gu"), blk + 1)
            act.activation(e_silu[:, i % 2, :], psum[:, 6 + i % 2, 0:FBLK], ACT.Silu).then_inc(sem("moe_silu"), 1)

        def moe_hi_act(act, at, i):
            r, turn, blk = at
            act.wait_ge(sem("moe_tr"), blk + 1)
            act.activation(eh_hi[:, i % 2, :], psum[:, 6 + i % 2, 2 * P:3 * P], ACT.Copy).then_inc(sem("moe_h_hi"), 1)

        def moe_act(act):
            act.wait_ge(sem("moe_top"), 1)
            act.activation(gts[:, 0:2], gts[:, 2:4], ACT.Exp).then_inc(sem("moe_exp"), 1)
            n_visits = moe_count(act)
            with act.Fori(0, n_visits) as v:
                def at(i, it=0):
                    return place(0, v * G_EXP, v * NB_EXP, i, it)

                def stage(i, it=0):
                    if i < NB_EXP:
                        moe_silu_act(act, at(i, it), i)
                    if i:
                        moe_hi_act(act, at(i - 1, it), i - 1)
                    if i + 2 < NB_EXP:
                        split_act(act, experts, at(i + 2, it), i + 2)

                split_act(act, experts, at(0), 0)
                moe_xe_act(act, v)
                split_act(act, experts, at(1), 1)
                loops, tail = turns(NB_EXP)
                stage(0)
                stage(1)
                with act.Fori(0, loops) as it:
                    for u in range(RING):
                        stage(2 + u, it)
                for i in range(tail, NB_EXP + 1):
                    stage(i)
                act.wait_ge(sem("moe_dn"), v * NB_EXP + NB_EXP)
                act.activation(oute[:, 0:512], psum[:, 4, :], ACT.Copy).then_inc(sem("moe_out_act"), 1)

        def moe_pick_dve(dve, v):
            for j in range(NT):
                at = bass.ds(v * NT + j, 1) if not isinstance(v, int) else slice(v * NT + j, v * NT + j + 1)
                dve.tensor_scalar(give[:, j, :], cst("iota"), vpos[:, at], vwgt[:, at], ALU.is_equal, MUL)
                ins = dve.tensor_scalar(pick[:, j, :], cst("iota"), vpos[:, at], vsel[:, at], ALU.is_equal, MUL)
            ins.then_inc(sem("moe_pick"), 1)

        def moe_xe_dve(dve, v):
            dve.wait_ge(sem("moe_gather"), 2 * v + 1)
            gain = vec("o_ln_ffn", 0, 4).unsqueeze(2).to_broadcast([P, 4, CAP])
            for dst in (xe, xe_hi):
                ins = dve.tensor_tensor(dst[:, 0:4, :], psum[:, 6, :].rearrange("p (c s) -> p c s", c=4), gain, MUL)
            ins.then_inc(sem("moe_xe_own"), 1)
            dve.wait_ge(sem("moe_xe_own"), v + 1)
            dve.wait_ge(sem("moe_xe_hi"), v + 1)
            dve.tensor_tensor(xe_lo, xe, xe_hi.bitcast(f32), SUB).then_inc(sem("moe_xe"), 1)

        def moe_hidden_dve(dve, at, i):
            r, turn, blk = at
            b = i % 2
            dve.wait_ge(sem("moe_silu"), blk + 1)
            if i < NT:
                dve.tensor_copy(giveT[:, i, :], psum[:, 6 + b, 3 * P:4 * P])
            dve.tensor_tensor(e_h[:, b, :], e_silu[:, b, :], psum[:, 6 + b, FBLK:2 * FBLK], MUL).then_inc(sem("moe_h32"), 1)

        def moe_lo_dve(dve, at, i):
            r, turn, blk = at
            b = i % 2
            dve.wait_ge(sem("moe_h_hi"), blk + 1)
            dve.tensor_tensor(eh_lo[:, b, :], psum[:, 6 + b, 2 * P:3 * P], eh_hi[:, b, :].bitcast(f32), SUB)\
               .then_inc(sem("moe_h"), 1)

        def moe_plan_dve(dve):
            def S(ins, name="dve_step"):
                step(dve, ins, name)
            iota8 = cst("iota")[:, 0:N_EXP]
            S(dve.tensor_scalar(before, cst("causal"), 0.0, None, ALU.is_lt))
            S(dve.memset(giveT[:, 0, :], 0.0))
            dve.wait_ge(sem("moe_routed"), 1)
            S(dve.tensor_copy(logit, psum[:, 6, 0:16]))
            for j in range(NT):
                S(dve.max(top[:, 8 * j:8 * j + 8], logit[:, 8 * j:8 * j + 8]))
                S(dve.max_index(topi[:, 8 * j:8 * j + 8], top[:, 8 * j:8 * j + 8], logit[:, 8 * j:8 * j + 8]))
                S(dve.tensor_copy(topf[:, 2 * j:2 * j + 2], topi[:, 8 * j:8 * j + 2]))
                S(dve.tensor_tensor(gts[:, 2 + j:3 + j], top[:, 8 * j + 1:8 * j + 2], top[:, 8 * j:8 * j + 1], SUB),
                  "moe_top" if j else "dve_step")
            for j in range(NT):
                S(dve.tensor_scalar(oneh, iota8, topf[:, 2 * j:2 * j + 1], None, ALU.is_equal))
                S(dve.scalar_tensor_tensor(sel[:, :, j], iota8, topf[:, 2 * j + 1:2 * j + 2], oneh, ALU.is_equal, MAX),
                  "moe_sel" if j else "dve_step")
            dve.wait_ge(sem("moe_exp"), 1)
            S(dve.tensor_scalar(gts[:, 2:4], gts[:, 0:2], 1.0, None, ADD))
            S(dve.reciprocal(gts[:, 2:4], gts[:, 2:4]))
            S(dve.tensor_tensor(gts[:, 0:2], gts[:, 0:2], gts[:, 2:4], MUL))
            for j in range(NT):
                S(dve.tensor_scalar(oneh, iota8, topf[:, 2 * j + 1:2 * j + 2], gts[:, j:j + 1], ALU.is_equal, MUL))
                S(dve.tensor_scalar(wgt[:, :, j], iota8, topf[:, 2 * j:2 * j + 1], gts[:, 2 + j:3 + j],
                                    ALU.is_equal, MUL))
                S(dve.tensor_tensor(wgt[:, :, j], wgt[:, :, j], oneh, ADD))
            dve.wait_ge(sem("moe_routed"), 2)
            for j in range(NT):
                S(dve.tensor_copy(pos[:, :, j], psum[:, 7, 8 * j:8 * j + 8]))
            S(dve.tensor_scalar(over, psum[:, 7, 16:24], float(CAP), None, ALU.is_gt))
            S(dve.memset(rank[:, 0:1], 0.0))
            for e in range(1, N_EXP):
                S(dve.tensor_tensor(rank[:, e:e + 1], rank[:, e - 1:e], over[:, e - 1:e], ADD))
            S(dve.tensor_tensor(plan_f[:, 0:1], rank[:, 7:8], over[:, 7:8], ADD))
            S(dve.tensor_scalar(plan_f[:, 0:1], plan_f[:, 0:1], float(N_EXP), None, ADD))
            for dst, src in ((vsel, sel), (vpos, pos), (vwgt, wgt)):
                S(dve.memset(dst[:, 2 * N_EXP:2 * NV], 0.0))
                S(dve.tensor_copy(dst[:, 0:2 * N_EXP], src.rearrange("p e j -> p (e j)")))
            S(dve.tensor_copy(plan_f[:, 1:9], iota8))
            for n in range(MAX_VISITS - N_EXP):
                S(dve.scalar_tensor_tensor(oneh, rank, float(n), over, ALU.is_equal, MUL))
                S(dve.tensor_tensor_reduce(pick_tmp[:, 0:8], oneh, iota8, 1.0, 0.0, MUL, ADD,
                                           plan_f[:, 9 + n:10 + n]))
                for dst, src in ((vsel, sel), (vpos, pos), (vwgt, wgt)):
                    for j in range(NT):
                        o = 2 * (N_EXP + n) + j
                        S(dve.tensor_tensor_reduce(pick_tmp[:, 0:8], oneh, src[:, :, j], 1.0, 0.0, MUL, ADD,
                                                   dst[:, o:o + 1]))
            S(dve.tensor_scalar(vpos[:, 2 * N_EXP:2 * MAX_VISITS], vpos[:, 2 * N_EXP:2 * MAX_VISITS], -float(CAP), None,
                                ADD))
            S(dve.tensor_copy(plan_i[:, 0:12], plan_f[:, 0:12]), "moe_plan")

        def moe_dve(dve):
            moe_plan_dve(dve)
            n_visits = moe_count(dve)
            moe_pick_dve(dve, 0)
            with dve.Fori(0, n_visits) as v:
                def at(i, it=0):
                    return place(0, v * G_EXP, v * NB_EXP, i, it)

                def stage(i, it=0):
                    if i < NB_EXP:
                        moe_hidden_dve(dve, at(i, it), i)
                    if i:
                        moe_lo_dve(dve, at(i - 1, it), i - 1)
                    if i + 2 < NB_EXP:
                        split_dve(dve, experts, at(i + 2, it), i + 2)

                split_dve(dve, experts, at(0), 0)
                moe_xe_dve(dve, v)
                split_dve(dve, experts, at(1), 1)
                loops, tail = turns(NB_EXP)
                stage(0)
                stage(1)
                moe_pick_dve(dve, v + 1)
                with dve.Fori(0, loops) as it:
                    for u in range(RING):
                        stage(2 + u, it)
                for i in range(tail, NB_EXP + 1):
                    stage(i)
                dve.wait_ge(sem("moe_dn"), v * NB_EXP + NB_EXP)
                dve.tensor_copy(oute[:, 512:1024], psum[:, 5, :]).then_inc(sem("moe_out_dve"), 1)
            dve.wait_ge(sem("moe_sum"), 1)
            for j in range(NT):
                step(dve, dve.tensor_copy(x_tm[:, j, :], psum[:, 2 * j:2 * j + 2, :].rearrange("p b n -> p (b n)")),
                     "dve_step")

        def spread_dve(dve, q, layer, idx, cond, dst, diag):
            d3 = diag.rearrange("p (c n) -> p c n", c=8)
            for c in range(8):
                ins = dve.tensor_scalar(d3[:, c, :], ident, mod[layer][:, 8 * idx + c, cond:cond + 1], None, MUL)
            step(dve, ins, "spread_diag")
            dve.wait_ge(sem("spread_ps"), q + 1)
            step(dve, dve.tensor_copy(dst, psum[:, 6:8, :].rearrange("p b n -> p (b n)")), "spread_ev")

        def spread_pe(pe, q, diag):
            pe.wait_ge(sem("spread_diag"), q + 1)
            for b in range(2):
                ins = pe.matmul(psum[:, 6 + b, :], cst("ones"), diag[:, 512 * b:512 * b + 512], start=True, stop=True)
            ins.then_inc(sem("spread_ps"), 1)

        at_mx, at_rs, at_rc = sm("at_mx", 4), sm("at_rs", 8), sm("at_rc", 4)
        at_n = {"pe": 0, "act": 0, "dve": 0}

        def attn_pe(pe, rounds, probs, pT):
            r0 = at_n["pe"]
            at_n["pe"] += len(rounds)

            def scores(n):
                rd = rounds[n]
                for i in range(4):
                    ins = pe.matmul(psum[:, i, 0:rd["keys"]], rd["q"][i], rd["k"][i], start=True, stop=True)
                ins.then_inc(sem("at_s"), 1)

            scores(0)
            for n, rd in enumerate(rounds):
                nb = rd["keys"] // P
                if n + 1 < len(rounds):
                    pe.wait_ge(sem("at_exp"), r0 + n + 1)
                    scores(n + 1)
                if r0 + n:
                    pe.wait_ge(sem("at_o"), r0 + n)
                for i in range(4):
                    pe.wait_ge(sem("at_norm"), 4 * (r0 + n) + i + 1)
                    for b in range(nb):
                        ins = pe.transpose(psum[:, 4 + i, b * P:(b + 1) * P], probs[:, i, b * P:(b + 1) * P], ident)
                ins.then_inc(sem("at_t"), 1)
                pe.wait_ge(sem("at_teva"), r0 + n + 1)
                pe.wait_ge(sem("at_tevb"), r0 + n + 1)
                for i in range(4):
                    rows = rd["rows"][i]
                    for b in range(nb):
                        ins = pe.matmul(psum[rows:rows + 64, 4, i * P:(i + 1) * P], rd["v"][i][b], pT[:, i, b, :],
                                        start=(b == 0), stop=(b == nb - 1))
                ins.then_inc(sem("at_pv"), 1)

        def attn_act(act, rounds, probs, pT, scale):
            r0 = at_n["act"]
            at_n["act"] += len(rounds)

            def exps(n):
                rd = rounds[n]
                act.wait_ge(sem("at_max"), r0 + n + 1)
                for i in range(4):
                    src = probs[:, i, 0:rd["keys"]] if rd["bias"] is not None else psum[:, i, 0:rd["keys"]]
                    o = 4 * ((r0 + n) % 2) + i
                    ins = act.activation(probs[:, i, 0:rd["keys"]], src, ACT.Exp, bias=at_mx[:, i:i + 1],
                                         scale=1.0 if rd["bias"] is not None else scale, accum_out=at_rs[:, o:o + 1])
                ins.then_inc(sem("at_exp"), 1)

            exps(0)
            for n, rd in enumerate(rounds):
                nb = rd["keys"] // P
                act.wait_ge(sem("at_t"), r0 + n + 1)
                act.activation(pT[:, 0:2, 0:nb, :], psum[:, 4:6, 0:rd["keys"]].rearrange("p i (b q) -> p i b q", q=P),
                               ACT.Copy).then_inc(sem("at_teva"), 1)
                if n + 1 < len(rounds):
                    exps(n + 1)
                act.wait_ge(sem("at_pv"), r0 + n + 1)
                for i in range(4):
                    rows = rd["rows"][i]
                    ins = act.activation(rd["o"][i], psum[rows:rows + 64, 4, i * P:(i + 1) * P], ACT.Copy)
                ins.then_inc(sem("at_o"), 1)

        def attn_dve(dve, rounds, probs, pT, scale):
            r0 = at_n["dve"]
            at_n["dve"] += len(rounds)

            def S(ins, name="dve_step"):
                step(dve, ins, name)

            def maxima(n):
                rd = rounds[n]
                dve.wait_ge(sem("at_s"), r0 + n + 1)
                src = psum[:, 0:4, 0:rd["keys"]]
                if rd["bias"] is not None:
                    dve.tensor_scalar(probs[:, :, T:2 * T], src[:, :, T:2 * T], scale, None, MUL)
                    S(dve.scalar_tensor_tensor(probs[:, :, 0:T], src[:, :, 0:T], scale, rd["bias"], MUL, ADD))
                    src = probs[:, :, 0:rd["keys"]]
                S(dve.tensor_reduce(at_mx, src, AX.X, MAX))
                S(dve.tensor_scalar(at_mx, at_mx, -1.0 if rd["bias"] is not None else -scale, None, MUL), "at_max")

            def normalise(n):
                dve.wait_ge(sem("at_exp"), r0 + n + 1)
                o = 4 * ((r0 + n) % 2)
                S(dve.reciprocal(at_rc, at_rs[:, o:o + 4]))
                for i in range(4):
                    w = probs[:, i, 0:rounds[n]["keys"]]
                    dve.tensor_scalar(w, w, at_rc[:, i:i + 1], None, MUL).then_inc(sem("at_norm"), 1)

            maxima(0)
            normalise(0)
            for n, rd in enumerate(rounds):
                nb = rd["keys"] // P
                ahead = n + 1 < len(rounds) and rounds[n + 1]["bias"] is None
                if ahead:
                    maxima(n + 1)
                dve.wait_ge(sem("at_t"), r0 + n + 1)
                dve.tensor_copy(pT[:, 2:4, 0:nb, :], psum[:, 6:8, 0:rd["keys"]].rearrange("p i (b q) -> p i b q", q=P))\
                   .then_inc(sem("at_tevb"), 1)
                if n + 1 < len(rounds):
                    if not ahead:
                        maxima(n + 1)
                    normalise(n + 1)

        def padded_keys_pool(pool, keys):
            pool.memset(keys[64:128, 0::2, :], 0.0)
            pool.memset(keys[0:64, 1::2, :], 0.0).then_inc(sem("pad_zero"), 1)

        g_in = ar(6144, 6144, "p (j n) -> p j n", j=4)
        gQT = ar(12288, 3072, "p (c t) -> p c t", c=6)
        gKT = ar(2048, 2048, "p (g t) -> p g t", g=4)
        mixT = ar(16384, 4096, "p (c t) -> p c t", c=8)
        g_probs = ar(20480, 2048, "p (i k) -> p i k", i=4)
        g_pT = ar(22528, 2048, "p (i b q) -> p i b q", i=4, b=4)
        band = ar(27648, 2048, "p (g i t) -> p g i t", g=4, i=2)
        dT = ar(5120, 1024, "p (m c t) -> p m c t", m=2, c=2)
        g_scr = ar(0, 2048)
        gB = [ar(2048, 1024), ar(3072, 1024)]
        gdiag = ar(4096, 1024)
        gtmp = ar(0, 1024)

        def l0_rounds():
            out = []
            for j in range(4):
                keys = 4 * P if j < 2 else 2 * P
                k0 = 4 * P - keys
                for q in range(3):
                    ns = range(4 * q, 4 * q + 4)
                    hs = [HEADS0[n] for n in ns]
                    out.append({"keys": keys, "bias": None,
                                "q": [gQT[:, n // 2, j * P:(j + 1) * P] for n in ns],
                                "k": [gKT[:, h // 3, k0:4 * P] for h in hs],
                                "v": [[g_in[:, b, 1280 + 64 * (h // 3):1344 + 64 * (h // 3)]
                                       for b in range(k0 // P, 4)] for h in hs],
                                "rows": [64 * (h % 2) for h in hs],
                                "o": [mixT[64 * (h % 2):64 * (h % 2) + 64, 2 + h // 2, j * P:(j + 1) * P] for h in hs]})
            return out

        def l0_pe(pe):
            n0 = FIRST["l0_in"]
            pe.wait_ge(sem("norm_hT"), 6)
            for j in range(4):
                if j >= 2:
                    pe.wait_ge(sem("l0_ev"), j - 1)
                for s in range(4):
                    if j == 0:
                        slot_ready(pe, n0 + s)
                    r = (n0 + s) % RING
                    for k in range(KD):
                        ins = pe.matmul(psum[:, 4 * (j % 2) + s, 0:COLS], hT[:, k, j * P:(j + 1) * P],
                                        slot_of[r][:, k * COLS:(k + 1) * COLS], start=(k == 0), stop=(k == KD - 1))
                    if j == 3:
                        ins.then_inc(w_used[r], 1)
                if j < 3:
                    ins.then_inc(sem("l0_pj"), 1)
            pe.wait_ge(sem("l0_ev"), 4)
            pe.wait_ge(sem("band_in"), 16)
            for m in range(2):
                for g in range(4):
                    pb = 64 * (g % 2)
                    for i in range(NT):
                        ins = pe.matmul(psum[pb:pb + 64, m, (g // 2) * T:(g // 2) * T + T],
                                        g_in[:, 2 * m + i, 64 * g:64 * g + 64], band[:, g, i, :],
                                        start=(i == 0), stop=(i == NT - 1))
            ins.then_inc(sem("pool_d"), 1)
            pe.wait_ge(sem("pool_dev"), 1)
            for m in range(2):
                for c in range(2):
                    ins = pe.matmul(psum[:, 2 + m, c * T:c * T + T], mat("pool_w")[:, c * P:(c + 1) * P], dT[:, m, c, :],
                                    start=True, stop=True)
            ins.then_inc(sem("pool_y"), 1)
            pe.wait_ge(sem("pool_yev"), 1)
            for j in range(4):
                pe.wait_ge(sem("l0_heads"), j + 1)
                for c in range(8):
                    ins = pe.transpose(psum[:, c, j * P:(j + 1) * P], g_in[:, j, T + c * P:T + (c + 1) * P], ident)
            ins.then_inc(sem("heads_tr"), 1)
            pe.wait_ge(sem("q_fm"), 2)
            pe.wait_ge(sem("k_fm"), 2)
            attn_pe(pe, l0_rounds(), g_probs, g_pT)
            pe.wait_ge(sem("at_o"), at_n["pe"])
            spread_pe(pe, 0, gdiag)
            pe.wait_ge(sem("spread_ev"), 1)
            spread_pe(pe, 1, gdiag)
            pe.wait_ge(sem("spread_ev"), 2)
            out_proj_pe(pe, FIRST["l0_out"], mixT, 4)

        def l0_act(act):
            act.wait_ge(sem("norm_hT"), 5)
            act.dma_start(ar(27648, 2048), band_in).then_inc(sem("band_in"), 16)
            for j in range(4):
                if j < 3:
                    act.wait_ge(sem("l0_pj"), j + 1)
                else:
                    slot_used(act, FIRST["l0_in"] + 3)
                b = 4 * (j % 2)
                act.activation(g_in[:, j, :].rearrange("p (s n) -> p s n", s=4), psum[:, b:b + 4, 0:COLS], ACT.Copy)\
                   .then_inc(sem("l0_ev"), 1)
                root_act(act, 16)
            act.wait_ge(sem("pool_d"), 1)
            act.activation(dT.rearrange("p m c t -> p m (c t)"), psum[:, 0:2, :], ACT.Copy).then_inc(sem("pool_dev"), 1)
            act.wait_ge(sem("heads_tr"), 3)
            act.activation(gQT, psum[:, 0:6, :], ACT.Copy).then_inc(sem("q_fm"), 1)
            attn_act(act, l0_rounds(), g_probs, g_pT, 0.125)

        def l0_dve(dve):
            def S(ins, name="dve_step"):
                step(dve, ins, name)
            for j in range(4):
                dve.wait_ge(sem("l0_ev"), j + 1)
                v = g_in[:, j, T:T + 1024].rearrange("p (g d) -> p g d", g=16)
                head_norm_dve(dve, v, g_scr[:, 0:1024].rearrange("p (g d) -> p g d", g=16), 16, 64, None)
                for a, b, name in ((0, 12, "l0_q_gain_2"), (12, 16, "l0_k_gain_2")):
                    S(dve.tensor_tensor(v[:, a:b, :], v[:, a:b, :],
                                        mat(name).unsqueeze(1).to_broadcast([P, b - a, 64]), MUL))
                if j < 2:
                    axial_dve(dve, v, 16, 64, "rope64", j, 16, g_scr[:, 1024:2048])
                dve.sem_inc(sem("l0_heads"), 1)
            dve.wait_ge(sem("pool_y"), 1)
            for m in range(2):
                for c in range(2):
                    S(dve.tensor_scalar(mixT[:, c, m * T:m * T + T], psum[:, 2 + m, c * T:c * T + T],
                                        vec("l0_pool_scale_2", c), None, MUL), "pool_yev" if m * c else "dve_step")
            dve.wait_ge(sem("heads_tr"), 3)
            dve.wait_ge(sem("pad_zero"), 1)
            dve.tensor_copy(gKT[0:64, 0::2, :], psum[0:64, 6:8, :])
            S(dve.tensor_copy(gKT[64:128, 1::2, :], psum[64:128, 6:8, :]), "k_fm")
            attn_dve(dve, l0_rounds(), g_probs, g_pT, 0.125)
            for cond in range(2):
                spread_dve(dve, cond, 0, 2, cond, gB[cond], gdiag)
            for m, dst in enumerate((x_tm, xc_tm)):
                slot_used(dve, FIRST["l0_out"] + 2)
                for j in range(NT):
                    S(dve.tensor_tensor(gtmp, psum[:, 4 * m + 2 * j:4 * m + 2 * j + 2, :].rearrange("p b n -> p (b n)"),
                                        gB[m], MUL))
                    S(dve.tensor_tensor(dst[:, j, :], dst[:, j, :], gtmp, ADD))

        def axial_dve(dve, v, groups, width, name, j, half, scratch):
            tab = cst(name)[:, j * 4 * half:(j + 1) * 4 * half].rearrange("p (f a d) -> p f a d", f=2, a=2)
            w = v[:, :, width - 4 * half:width].rearrange("p g (a s d) -> p g a s d", a=2, s=2)
            n = groups * half
            for a in range(2):
                cos, sin = [tab[:, f, a, :].unsqueeze(1).to_broadcast([P, groups, half]) for f in range(2)]
                tmp = [scratch[:, i * n:(i + 1) * n].rearrange("p (g d) -> p g d", g=groups) for i in range(2)]
                rope_dve(dve, w[:, :, a, 0, :], w[:, :, a, 1, :], cos, sin, tmp, None)

        fB, fdiag, ftmp = ar(8192, 1024), ar(9216, 1024), ar(10240, 1024)

        def gated_ffn_pe(pe, g, q, name):
            spread_pe(pe, g, fdiag)
            ffn_pe(pe, q, name)

        def gated_ffn_dve(dve, g, k, q, layer, cond, dst, name):
            norm_dve(dve, k, dst, lambda c: ge(layer, 1, cond, c), lambda c: mod[layer][:, 24 + c, cond:cond + 1], 0)
            spread_dve(dve, g, layer, 5, cond, fB, fdiag)
            ffn_dve(dve, q, name)
            add_tokens(dve, dst, fB, ftmp)

        W_L1 = [COLS] * (L1_IN // COLS) + [L1_IN % COLS]
        TILES_L1 = [2, 2, 4, 4, 4, 4]
        C_CQ, C_NQ, C_CKV, C_KR, C_NK, C_NV = 0, 384, 896, 1152, 1184, 1696
        m_in = ar(6144, 4 * L1_IN, "p (j n) -> p j n", j=4)
        cqT = ar(14976, 768, "p (c t) -> p c t", c=3)
        ckvT = ar(15744, 1024, "p (c t) -> p c t", c=2)
        mkv = ar(16768, 4096, "p (j n) -> p j n", j=4)
        mk = ar(20864, 3072, "p (j n) -> p j n", j=4)
        mkT = ar(23936, 4096, "p (h t) -> p h t", h=8)
        mqT = ar(0, 2048, "p (h t) -> p h t", h=8)
        mq = ar(2048, 1536, "p (j n) -> p j n", j=NT)
        m_scr = ar(4096, 2048)
        m_mixT = ar(2048, 2048, "p (c t) -> p c t", c=8)
        m_probs = ar(20864, 2048, "p (i k) -> p i k", i=4)
        m_pT = ar(4096, 2048, "p (i b q) -> p i b q", i=4, b=4)
        bias = ar(16768, 4096, "p (j h k) -> p j h k", j=NT, h=8)
        nqT = ar(23936, 1024, "p (c t) -> p c t", c=4)
        nkT = ar(24960, 4096, "p (h t) -> p h t", h=8)

        def m_out(h, j):
            return m_mixT[64 * (h % 2):64 * (h % 2) + 64, h // 2, j * P:(j + 1) * P]

        def mla_rounds():
            return [{"keys": 4 * P, "bias": None,
                     "q": [mqT[0:96, h, j * P:(j + 1) * P] for h in range(4 * q, 4 * q + 4)],
                     "k": [mkT[0:96, h, :] for h in range(4 * q, 4 * q + 4)],
                     "v": [[mkv[:, b, 128 * h + 64:128 * h + 128] for b in range(4)] for h in range(4 * q, 4 * q + 4)],
                     "rows": [64 * (h % 2) for h in range(4)],
                     "o": [m_out(h, j) for h in range(4 * q, 4 * q + 4)]}
                    for j in range(NT) for q in range(2)]

        def na_rounds():
            return [{"keys": 4 * P, "bias": bias[:, j, 4 * q:4 * q + 4, :],
                     "q": [nqT[:, h // 2, j * P:(j + 1) * P] for h in range(4 * q, 4 * q + 4)],
                     "k": [nkT[:, h, :] for h in range(4 * q, 4 * q + 4)],
                     "v": [[m_in[:, b, C_NV + 64 * h:C_NV + 64 * h + 64] for b in range(4)]
                           for h in range(4 * q, 4 * q + 4)],
                     "rows": [64 * (h % 2) for h in range(4)],
                     "o": [m_out(8 + h, j) for h in range(4 * q, 4 * q + 4)]}
                    for j in range(NT) for q in range(2)]

        def l1_pe(pe):
            pe.wait_ge(sem("norm_hT"), 10)
            tm_proj_pe(pe, "l1", FIRST["l1_in"], W_L1, hT, TILES_L1)
            pe.wait_ge(sem("l1_ev"), len(W_L1))
            pe.wait_ge(sem("l1_low"), 1)
            for c in range(3):
                for j in range(NT):
                    at = (c % 2) * T + j * P
                    pe.transpose(psum[:, c // 2, at:at + P], m_in[:, j, C_CQ + c * P:C_CQ + (c + 1) * P], ident)
            for c in range(2):
                for j in range(4):
                    ins = pe.transpose(psum[:, 2 + c, j * P:(j + 1) * P],
                                       m_in[:, j, C_CKV + c * P:C_CKV + (c + 1) * P], ident)
            ins.then_inc(sem("l1_ltr"), 1)
            pe.wait_ge(sem("l1_lowT"), 1)
            n = FIRST["l1_uq"]
            slot_ready(pe, n)
            for j in range(NT):
                for hf in range(2):
                    for k in range(3):
                        o = k * 768 + hf * COLS
                        ins = pe.matmul(psum[:, 4 + 2 * j + hf, 0:COLS], cqT[:, k, j * P:(j + 1) * P],
                                        slot_of[n % RING][:, o:o + COLS], start=(k == 0), stop=(k == 2))
            ins.then_inc(w_used[n % RING], 1)
            n = FIRST["l1_ukv"]
            slot_ready(pe, n)
            pe.wait_ge(sem("l1_qev"), 1)
            for j in range(4):
                for hf in range(2):
                    for k in range(2):
                        o = k * D + hf * 512
                        ins = pe.matmul(psum[:, 2 * j + hf, :], ckvT[:, k, j * P:(j + 1) * P],
                                        slot_of[n % RING][:, o:o + 512], start=(k == 0), stop=(k == 1))
            ins.then_inc(w_used[n % RING], 1)
            pe.wait_ge(sem("l1_kvev"), 1)
            pe.wait_ge(sem("l1_mq"), 1)
            for h in range(8):
                for j in range(NT):
                    at = (h % 2) * T + j * P
                    ins = pe.transpose(psum[0:96, h // 2, at:at + P], mq[:, j, 96 * h:96 * h + 96], ident)
            ins.then_inc(sem("l1_mqtr"), 1)
            pe.wait_ge(sem("l1_mqT"), 1)
            pe.wait_ge(sem("l1_mk"), 1)
            for h in range(8):
                for j in range(4):
                    ins = pe.transpose(psum[0:96, h, j * P:(j + 1) * P], mk[:, j, 96 * h:96 * h + 96], ident)
            ins.then_inc(sem("l1_mktr"), 1)
            pe.wait_ge(sem("l1_mkT"), 1)
            attn_pe(pe, mla_rounds(), m_probs, m_pT)
            pe.wait_ge(sem("at_o"), at_n["pe"])
            for c in range(4):
                for j in range(NT):
                    at = (c % 2) * T + j * P
                    pe.transpose(psum[:, c // 2, at:at + P], m_in[:, j, C_NQ + c * P:C_NQ + (c + 1) * P], ident)
                for j in range(4):
                    ins = pe.transpose(psum[:, 2 + c, j * P:(j + 1) * P], m_in[:, j, C_NK + c * P:C_NK + (c + 1) * P],
                                       ident)
            ins.then_inc(sem("l1_ntr"), 1)
            pe.wait_ge(sem("l1_nqT"), 1)
            pe.wait_ge(sem("l1_nkT"), 1)
            attn_pe(pe, na_rounds(), m_probs, m_pT)
            pe.wait_ge(sem("at_o"), at_n["pe"])
            spread_pe(pe, 4, fdiag)
            pe.wait_ge(sem("spread_ev"), 5)
            out_proj_pe(pe, FIRST["l1_out"], m_mixT, NT)

        def l1_act(act):
            tm_proj_act(act, "l1", FIRST["l1_in"], W_L1, m_in, TILES_L1,
                        {0: [1] * NT, 2: [8] * NT + [1] * 4, 4: [8] * 4})
            slot_used(act, FIRST["l1_uq"])
            act.activation(mq.rearrange("p j (h n) -> p (j h) n", h=2), psum[:, 4:8, 0:COLS], ACT.Copy)\
               .then_inc(sem("l1_qev"), 1)
            for _ in range(NT):
                root_act(act, 8)
            slot_used(act, FIRST["l1_ukv"])
            act.activation(mkv.rearrange("p j (h n) -> p (j h) n", h=2), psum[:, :, :], ACT.Copy)\
               .then_inc(sem("l1_kvev"), 1)
            act.wait_ge(sem("l1_mqtr"), 1)
            act.activation(mqT[0:96], psum[0:96, 0:4, :].rearrange("p b (h t) -> p (b h) t", h=2), ACT.Copy)\
               .then_inc(sem("l1_mqT"), 1)
            for _ in range(4):
                root_act(act, 8)
            act.wait_ge(sem("l1_mktr"), 1)
            act.activation(mkT[0:96], psum[0:96, :, :], ACT.Copy).then_inc(sem("l1_mkT"), 1)
            attn_act(act, mla_rounds(), m_probs, m_pT, 96.0 ** -0.5)
            act.dma_start(ar(16768, 4096), bias_in).then_inc(sem("bias_in"), 16)
            act.wait_ge(sem("l1_ntr"), 1)
            act.wait_ge(sem("pad_zero"), 2)
            act.activation(nkT[0:64, 0::2, :], psum[0:64, 2:6, :], ACT.Copy)
            act.activation(nkT[64:128, 1::2, :], psum[64:128, 2:6, :], ACT.Copy).then_inc(sem("l1_nkT"), 1)
            attn_act(act, na_rounds(), m_probs, m_pT, 0.125)

        def l1_dve(dve):
            def S(ins, name="dve_step"):
                step(dve, ins, name)
            scr = ar(16768, 512)
            def low(at, n, tiles):
                for j in range(tiles):
                    head_norm_dve(dve, m_in[:, j, at:at + n].unsqueeze(1), scr[:, 0:n].unsqueeze(1), 1, n, None)

            def heads(at, name, tiles):
                for j in range(tiles):
                    head_norm_dve(dve, m_in[:, j, at:at + 512].rearrange("p (g d) -> p g d", g=8),
                                  scr.rearrange("p (g d) -> p g d", g=8), 8, 64, mat(name))

            def arrived(end):
                dve.wait_ge(sem("l1_ev"), -(-end // COLS))

            arrived(C_CQ + 384)
            low(C_CQ, 384, NT)
            arrived(C_NQ + 512)
            heads(C_NQ, "l1_na_q_gain_2", NT)
            arrived(C_CKV + 256)
            low(C_CKV, 256, 4)
            dve.sem_inc(sem("l1_low"), 1)
            arrived(C_NK + 512)
            heads(C_NK, "l1_na_k_gain_2", 4)
            dve.wait_ge(sem("l1_ltr"), 1)
            for c in range(3):
                S(dve.tensor_scalar(cqT[:, c, :], psum[:, c // 2, (c % 2) * T:(c % 2) * T + T],
                                    vec("l1_mla_q_a_gain_2", c), None, MUL))
            for c in range(2):
                S(dve.tensor_scalar(ckvT[:, c, :], psum[:, 2 + c, :], vec("l1_mla_kv_a_gain_2", c), None, MUL),
                  "l1_lowT" if c else "dve_step")
            dve.wait_ge(sem("l1_qev"), 1)
            scr = m_scr[:, 0:768].rearrange("p (g d) -> p g d", g=8)
            for j in range(NT):
                v = mq[:, j, :].rearrange("p (g d) -> p g d", g=8)
                head_norm_dve(dve, v, scr, 8, 96, mat("l1_mla_q_gain_2"))
                axial_dve(dve, v, 8, 96, "rope32", j, 8, m_scr[:, 1024:2048])
            dve.sem_inc(sem("l1_mq"), 1)
            dve.wait_ge(sem("l1_kvev"), 1)
            for j in range(4):
                v = mk[:, j, :].rearrange("p (g d) -> p g d", g=8)
                S(dve.tensor_copy(v[:, :, 0:64], mkv[:, j, :].rearrange("p (g d) -> p g d", g=8)[:, :, 0:64]))
                S(dve.tensor_copy(v[:, :, 64:96], m_in[:, j, C_KR:C_KR + 32].unsqueeze(1).to_broadcast([P, 8, 32])))
                head_norm_dve(dve, v, scr, 8, 96, mat("l1_mla_k_gain_2"))
                if j < NT:
                    axial_dve(dve, v, 8, 96, "rope32", j, 8, m_scr[:, 1024:2048])
            dve.sem_inc(sem("l1_mk"), 1)
            dve.wait_ge(sem("l1_mkT"), 1)
            attn_dve(dve, mla_rounds(), m_probs, m_pT, 96.0 ** -0.5)
            dve.wait_ge(sem("l1_ntr"), 1)
            S(dve.tensor_copy(nqT, psum[:, 0:2, :].rearrange("p b (c t) -> p (b c) t", c=2)), "l1_nqT")
            dve.wait_ge(sem("bias_in"), 16)
            attn_dve(dve, na_rounds(), m_probs, m_pT, 0.125)
            spread_dve(dve, 4, 1, 2, 0, fB, fdiag)
            slot_used(dve, FIRST["l1_out"] + 2)
            add_tokens(dve, x_tm, fB, ftmp)

        @block.sync
        def _(sp):
            sp.dma_start(x[:, :], x_in).then_inc(sem("x_in"), 16)
            for dst, src in ((pack, pack_in), (const, const_in)):
                sp.dma_start(dst[:, :], src).then_inc(sem("pack_in"), 16)
            for r in range(RING):
                sp.dma_start(slot_of[r], stream_in[r]).then_inc(w_ready[r], 16)
            for dst, src in ((xc, ctx_in), (pos_i, pos_in)):
                sp.dma_start(dst[:, :], src).then_inc(sem("ctx_in"), 16)
            g_end = N_SLOTS_PADDED // RING
            with sp.Fori(1, min(G_MOE, g_end)) as g:
                for r in range(RING):
                    sp.wait_ge(w_used[r], g)
                    sp.dma_start(slot_of[r], stream_in[g * RING + r]).then_inc(w_ready[r], 16)
            for r in range(RING):
                sp.wait_ge(w_used[r], G_MOE)
                sp.dma_start(slot_of[r], stream_in[MOE_SLOT0 + r]).then_inc(e_ready[r], 16)
            with sp.Fori(1, (N_EXP - 1) * G_EXP) as g:
                for r in range(RING):
                    sp.wait_ge(e_used[r], g)
                    sp.dma_start(slot_of[r], stream_in[g * RING + (MOE_SLOT0 + r)]).then_inc(e_ready[r], 16)
            n_visits = moe_count(sp)
            with sp.Fori(N_EXP - 1, n_visits) as v:
                expert = sp.value_load(plan_i[0:1, bass.ds(v + 1, 1)], min_val=0, max_val=N_EXP - 1)
                with sp.Fori(0, G_EXP) as g:
                    for r in range(RING):
                        sp.wait_ge(e_used[r], v * G_EXP + g)
                        sp.dma_start(slot_of[r], stream_in[expert * NB_EXP + g * RING + (MOE_SLOT0 + r)])\
                          .then_inc(e_ready[r], 16)
            for r in range(RING):
                sp.wait_ge(e_used[r], n_visits * G_EXP)
                sp.dma_start(slot_of[r], stream_in[G_MOE * RING + r]).then_inc(w_ready[r], 16)
            with sp.Fori(G_MOE + 1, g_end) as g:
                for r in range(RING):
                    sp.wait_ge(w_used[r], g)
                    sp.dma_start(slot_of[r], stream_in[g * RING + r]).then_inc(w_ready[r], 16)
            sp.wait_ge(sem("x_final"), 1)
            sp.dma_start(out, x[:, :]).then_inc(sem("stored"), 16)
            sp.wait_ge(sem("stored"), 16)

        @block.tensor
        def _(pe):
            pe.wait_ge(sem("pack_in"), 32)
            norm_pe(pe, 0)
            e_proj_pe(pe)
            pe.wait_ge(sem("e_proj_ev"), N_EIN)
            ada_pe(pe, 0, 0, ADA_0A)
            lru_pe(pe)
            ada_pe(pe, 0, ADA_0A, ADA_0B)
            rwkv_in_pe(pe)
            for j in range(NT):
                rwkv_tile_pe(pe, j)
            rwkv_out_pe(pe)
            norm_pe(pe, 1)
            ffn_pe(pe, 0, "e_ffn")
            norm_pe(pe, 2)
            diff_pe(pe)
            norm_pe(pe, 3)
            moe_pe(pe)
            norm_pe(pe, 4)
            norm_pe(pe, 5)
            l0_pe(pe)
            norm_pe(pe, 6)
            gated_ffn_pe(pe, 2, 1, "l0_ffn")
            norm_pe(pe, 7)
            gated_ffn_pe(pe, 3, 2, "l0_ffn_ctx")
            norm_pe(pe, 8)
            norm_pe(pe, 9)
            l1_pe(pe)
            norm_pe(pe, 10)
            gated_ffn_pe(pe, 5, 3, "l1_ffn")

        @block.scalar
        def _(act):
            ada_act(act)
            root_act(act, NT)
            act.wait_ge(sem("lru_dve"), 1)
            act.activation(lexp, lz, ACT.Exp, scale=-1.0).then_inc(sem("lru_act"), 1)
            e_proj_act(act)
            lru_act(act)
            rwkv_in_act(act)
            for j in range(NT):
                rwkv_tile_act(act, j)
            rwkv_out_act(act)
            root_act(act, NT)
            ffn_act(act, 1, 0, "e_ffn")
            root_act(act, NT)
            diff_act(act)
            root_act(act, NT)
            moe_act(act)
            root_act(act, NT)
            root_act(act, NT)
            l0_act(act)
            for k, q, name in ((6, 1, "l0_ffn"), (7, 2, "l0_ffn_ctx")):
                root_act(act, NT)
                ffn_act(act, k, q, name)
            root_act(act, NT)
            root_act(act, NT)
            l1_act(act)
            root_act(act, NT)
            ffn_act(act, 10, 3, "l1_ffn")

        @block.vector
        def _(dve):
            dve.wait_ge(sem("x_in"), 16)
            dve.wait_ge(sem("pack_in"), 32)
            norm_dve(dve, 0, x_tm, lambda c: vec("e_ln_mix", c), None, 0)
            dve.wait_ge(sem("ada_silu"), 1)
            ada_z_dve(dve)
            cols_dve(dve)
            step(dve, dve.memset(pj[:, :, 0:4], 0.0), "dve_step")
            lru_dve(dve)
            rwkv_in_dve(dve)
            for j in range(NT):
                rwkv_tile_dve(dve, j)
            rwkv_out_dve(dve)
            norm_dve(dve, 1, x_tm, lambda c: vec("e_ln_ffn", c), None, 0)
            ffn_dve(dve, 0, "e_ffn")
            add_tokens(dve, x_tm)
            norm_dve(dve, 2, x_tm, lambda c: vec("o_ln_mix", c), None, 0)
            dve.wait_ge(sem("ctx_in"), 32)
            diff_dve(dve)
            norm_dve(dve, 3, x_tm, lambda c: vec("o_ln_ffn", c), None, 0)
            moe_dve(dve)
            for k, src, cond in ((4, x_tm, 0), (5, xc_tm, 1)):
                norm_dve(dve, k, src, lambda c, cond=cond: ge(0, 0, cond, c),
                         lambda c, cond=cond: mod[0][:, c, cond:cond + 1], T * cond)
            l0_dve(dve)
            gated_ffn_dve(dve, 2, 6, 1, 0, 0, x_tm, "l0_ffn")
            gated_ffn_dve(dve, 3, 7, 2, 0, 1, xc_tm, "l0_ffn_ctx")
            for k, src, cond in ((8, x_tm, 0), (9, xc_tm, 1)):
                norm_dve(dve, k, src, lambda c, cond=cond: ge(1, 0, cond, c),
                         lambda c, cond=cond: mod[1][:, c, cond:cond + 1], T * cond)
            l1_dve(dve)
            gated_ffn_dve(dve, 5, 10, 3, 1, 0, x_tm, "l1_ffn")
            dve.sem_inc(sem("x_final"), 1)

        @block.gpsimd
        def _(pool):
            pool.wait_ge(sem("l0_ev"), 4)
            padded_keys_pool(pool, gKT)
            pool.wait_ge(sem("at_o"), len(l0_rounds()) + len(mla_rounds()))
            padded_keys_pool(pool, nkT)


def constants():
    c = np.zeros((P, N_CONST), np.float32)

    def put(name, a):
        o, n = CONST[name]
        c[:, o:o + n] = np.asarray(a, np.float32).reshape(P, n)

    s, t = np.arange(P)[:, None], np.arange(P)[None, :]
    same = s // CH == t // CH
    put("ident", s == t)
    put("ones", np.ones((P, P)))
    put("headones", s // 64 == t // 64)
    put("mask4", np.concatenate([(s < t) & same, (s <= t) & same] * 2, 1))
    put("level", np.concatenate([((t >> l) & 1 == 1) & (s >> l == (t >> l) - 1) for l in range(6)], 1))
    put("scanmask", np.broadcast_to((np.arange(T) % CH != 0)[None], (P, T)))
    put("causal", np.where(t <= s, 0.0, NEG))
    tok = np.arange(T)
    for name, d in (("rope64", 32), ("rope32", 16)):
        inv = (np.float32(10000.0) ** (-np.arange(d // 2, dtype=np.float32) * 2.0 / d)).astype(np.float32)
        ang = np.stack([tok // 64, tok % 64], 1).astype(np.float32)[:, :, None] * inv
        tab = np.stack([np.cos(ang), np.sin(ang)], 1).reshape(NT, P, -1).transpose(1, 0, 2)
        put(name, tab)
    put("iota", np.broadcast_to(np.arange(P)[None], (P, P)))
    put("freq", np.broadcast_to((np.float32(500000.0) ** (-np.arange(0, 16, 2, dtype=np.float32) / 16))[None], (P, 8)))
    band = np.zeros((4, T, T), np.float32)
    for g, w in enumerate((2, 4, 8, 16)):
        lo, hi = np.clip(tok - w // 2, 0, T), np.clip(tok - w // 2 + w, 0, T)
        src = np.arange(T)[:, None]
        band[g] = ((src >= lo) & (src < hi)) / (hi - lo).astype(np.float32) - (src == tok)
    band = band.reshape(4, NT, P, T).transpose(2, 0, 1, 3).reshape(P, N_BAND)
    return c, np.ascontiguousarray(band)


def chunks(v):
    return np.asarray(v).reshape(-1, P).T


def packed(i):
    a = np.zeros((P, N_PACK), np.float32)
    special = {"cond": np.stack([chunks(i["c_2"][0]), chunks(i["c_ctx_2"])], 2)}
    for name, n in VECS:
        o = PACK[name][0]
        a[:, o:o + n] = special[name].reshape(P, n) if name in special else chunks(i[name])
    gate = {}
    for name, key in (("gate_a", "e_gate_a_w"), ("gate_x", "e_gate_x_w")):
        m = np.zeros((P, 4, P), np.float32)
        for h in range(8):
            m[64 * (h % 2):64 * (h % 2) + 64, h // 2, 64 * (h % 2):64 * (h % 2) + 64] = i[key][0, h]
        gate[name] = m
    pool = np.zeros((P, 2, P), np.float32)
    for g in range(4):
        pool[64 * (g % 2):64 * (g % 2) + 64, g // 2, 64 * (g % 2):64 * (g % 2) + 64] = i["l0_pool_w_2"][g]
    mats = {**gate, "w2a2": np.concatenate([i["e_w2"][0], i["e_a2"][0]], 0), "g2": i["e_g2"][0],
            "router": i["o_router"][0].reshape(KD, P, N_EXP).transpose(1, 0, 2), "pool_w": pool}
    for name, n in MATS:
        o = PACK[name][0]
        a[:, o:o + n] = mats[name].reshape(P, n)
    for name, n in ROWS:
        o = PACK[name][0]
        a[:, o:o + n] = np.asarray(i[name]).reshape(1, n)
    return a


def stream(i):
    w = np.zeros((N_STREAM, P, SLOT), np.float32)

    def columns(n0, m, widths, nk):
        at = 0
        for s, n in enumerate(widths):
            w[n0 + s, :, :nk * n] = m[:, at:at + n].reshape(nk, P, n).transpose(1, 0, 2).reshape(P, -1)
            at += n

    def rows(n0, m):
        for s in range(3):
            part = m[3 * s * P:min(3 * s + 3, KD) * P]
            w[n0 + s, :, :part.size // P] = part.reshape(-1, P, D).transpose(1, 0, 2).reshape(P, -1)

    def ffn(n0, g, u, d):
        nb = g.shape[1] // P
        v = w[n0:n0 + nb].reshape(nb, P, 3, D)
        for q, m in enumerate((g, u)):
            v[:, :, q] = m.reshape(KD, P, nb, P).transpose(2, 1, 0, 3).reshape(nb, P, D)
        v[:, :, 2] = d.reshape(nb, P, D)

    def even(n):
        return [COLS] * (n // COLS) + ([n % COLS] if n % COLS else [])

    for l in range(2):
        columns(FIRST[f"ada{l}"], i[f"l{l}_ada_w_2"], even(6 * D), KD)
    e_in = np.zeros((D, COLS * -(-EVEN_IN // COLS)), np.float32)
    e_in[:, :EVEN_IN] = i["e_w_in"][0]
    columns(FIRST["e_in"], e_in, even(e_in.shape[1]), KD)
    rows(FIRST["e_out"], i["e_w_out"][0])
    ffn(FIRST["e_ffn"], i["e_ffn_gate"][0], i["e_ffn_up"][0], i["e_ffn_down"][0])
    columns(FIRST["qkv"], i["o_w_qkv"][0], even(QKV), KD)
    rows(FIRST["o_out"], i["o_w_o"][0])
    for e in range(N_EXP):
        ffn(MOE_SLOT0 + e * NB_EXP, i["o_moe_gate"][0, e], i["o_moe_up"][0, e], i["o_moe_down"][0, e])
    m = i["l0_w_in_2"]
    q = m[:, 256:1024].reshape(D, 12, 64)[:, list(HEADS0)].reshape(D, 768)
    columns(FIRST["l0_in"], np.concatenate([m[:, :256], q, m[:, 1024:]], 1), even(L0_IN), KD)
    rows(FIRST["l0_out"], i["l0_w_out_2"])
    for name in ("l0_ffn", "l0_ffn_ctx"):
        ffn(FIRST[name], i["l0_ffn_w_gate_2"], i["l0_ffn_w_up_2"], i["l0_ffn_w_down_2"])
    m = i["l1_w_in_2"]
    m = np.concatenate([m[:, :384], m[:, 672:1184], m[:, 384:672], m[:, 1184:]], 1)
    columns(FIRST["l1_in"], m, even(L1_IN), KD)
    columns(FIRST["l1_uq"], i["l1_mla_w_uq_2"], [768], 3)
    columns(FIRST["l1_ukv"], i["l1_mla_w_ukv_2"], [1024], 2)
    rows(FIRST["l1_out"], i["l1_w_out_2"])
    ffn(FIRST["l1_ffn"], i["l1_ffn_w_gate_2"], i["l1_ffn_w_up_2"], i["l1_ffn_w_down_2"])
    return w


def relative_bias(rpb):
    tok = np.arange(T)
    row, col = tok // 64, tok % 64
    start = np.clip(col - 8, 0, 48)
    inside = (col[None] >= start[:, None]) & (col[None] < start[:, None] + 16)
    dr = row[None] - row[:, None] + 7
    dc = np.clip(col[None] - col[:, None] + 15, 0, 30)
    b = np.where(inside[None], rpb[:, dr, dc], np.float32(NEG))
    return np.ascontiguousarray(b.reshape(8, NT, P, T).transpose(2, 1, 0, 3).reshape(P, N_BIAS))


def host_arrays(inputs):
    i = {k: np.asarray(v) for k, v in inputs.items()}
    const, band = constants()
    tm = lambda a: np.ascontiguousarray(a.reshape(NT, P, D).transpose(1, 0, 2).reshape(P, NT * D))
    return {"x": tm(i["x"]), "ctx": tm(i["ctx_2"]),
            "positions": np.ascontiguousarray(i["positions"].reshape(NT, P).T.astype(np.int32)),
            "pack": packed(i), "const": const, "band": band, "bias": relative_bias(i["l1_na_rpb_2"]),
            "stream": stream(i)}


def kernel(**inputs):
    import concourse.bacc as bacc
    from concourse.bass_utils import run_bass_kernel_spmd

    nc = bacc.Bacc("TRN2", target_bir_lowering=False, num_devices=1)
    arrays = host_arrays(inputs)
    args = [nc.dram_tensor(f"{n}_dram", a.shape, mybir.dt.from_np(a.dtype), kind="ExternalInput").ap()
            for n, a in arrays.items()]
    out = nc.dram_tensor("out_dram", (P, NT * D), mybir.dt.float32, kind="ExternalOutput").ap()
    program(nc, *args, out)
    r = run_bass_kernel_spmd(nc, [{f"{n}_dram": a for n, a in arrays.items()}], core_ids=[0])
    got = r.results[0]["out_dram"]
    return np.ascontiguousarray(got.reshape(P, NT, D).transpose(1, 0, 2).reshape(1, T, D))
```
